# Optimizing a Trainium2 kernel written in Bass

```python
import math
import jax, jax.numpy as jnp
from jax import lax
import numpy as np
import jax
import jax.numpy as jnp

D_MODEL = 1024
BATCH = 1
SEQ = 512
DEPTH = 2

CHUNK = 64
N_META = 16
N_A_LAYERS = DEPTH // 2
N_B_LAYERS = DEPTH - N_A_LAYERS
D_RNN = 3 * D_MODEL // 2
N_LRU_BLOCKS = 16
LRU_BLOCK = D_RNN // N_LRU_BLOCKS
LRU_C = 8.0
CONV_A_WIDTH = 4
N_FOX_HEADS = 16
FOX_HEAD_DIM = D_MODEL // N_FOX_HEADS
Q_BLOCK = 128
D_FF = ((8 * D_MODEL // 3 + 255) // 256) * 256
CONV_F_WIDTH = 3
DN_ALPHA = (2 * DEPTH) ** 0.25
DN_BETA = (8 * DEPTH) ** -0.25
LN_EPS = 1e-5


def layer_norm(x, g, b):
    xf = x.astype(jnp.float32)
    mu = jnp.mean(xf, axis=-1, keepdims=True)
    var = jnp.mean(jnp.square(xf - mu), axis=-1, keepdims=True)
    y = (xf - mu) * lax.rsqrt(var + LN_EPS)
    return (y * g.astype(jnp.float32) + b.astype(jnp.float32)).astype(x.dtype)

def causal_dwconv(x, w, b):
    width = w.shape[0]
    length = x.shape[1]
    xp = jnp.pad(x, ((0, 0), (width - 1, 0), (0, 0)))
    y = b
    for k in range(width):
        y = y + xp[:, k:k + length] * w[k]
    return y

def rg_lru(x, w_r, b_r, w_i, b_i, lam):
    bsz, length, width = x.shape
    xb = x.reshape(bsz, length, N_LRU_BLOCKS, LRU_BLOCK)
    r = jax.nn.sigmoid(jnp.einsum('blnc,ncd->blnd', xb, w_r).reshape(bsz, length, width) + b_r)
    i = jax.nn.sigmoid(jnp.einsum('blnc,ncd->blnd', xb, w_i).reshape(bsz, length, width) + b_i)
    log_a = -LRU_C * r.astype(jnp.float32) * jax.nn.softplus(-lam.astype(jnp.float32))
    a = jnp.exp(log_a)
    u = jnp.sqrt(-jnp.expm1(2.0 * log_a)) * (i * x).astype(jnp.float32)

    def combine(left, right):
        a1, b1 = left
        a2, b2 = right
        return a1 * a2, a2 * b1 + b2

    _, h = lax.associative_scan(combine, (a, u), axis=1)
    return h.astype(x.dtype)

def recurrent_mixer(x, w_in, conv_w, conv_b, w_r, b_r, w_i, b_i, lam, w_out):
    gr = x @ w_in
    gate, rec = gr[..., :D_RNN], gr[..., D_RNN:]
    rec = causal_dwconv(rec, conv_w, conv_b)
    h = rg_lru(rec, w_r, b_r, w_i, b_i, lam)
    return (jax.nn.gelu(gate) * h) @ w_out

def conv_ffn(x, w_in, conv_w, conv_b, w_out):
    h = causal_dwconv(x @ w_in, conv_w, conv_b)
    gate, val = h[..., :D_FF], h[..., D_FF:]
    return (jax.nn.gelu(gate) * val) @ w_out

def to_heads_padded(t, lp):
    bsz, length, _ = t.shape
    t = t.reshape(bsz, length, N_FOX_HEADS, FOX_HEAD_DIM).transpose(0, 2, 1, 3)
    return jnp.pad(t, ((0, 0), (0, 0), (0, lp - length), (0, 0)))

def shared_kv(x, kv_w, f_b):
    length = x.shape[1]
    lp = -(-length // Q_BLOCK) * Q_BLOCK
    z = x @ kv_w
    k = to_heads_padded(z[..., :D_MODEL], lp)
    v = to_heads_padded(z[..., D_MODEL:2 * D_MODEL], lp)
    log_f = jax.nn.log_sigmoid(z[..., 2 * D_MODEL:].astype(jnp.float32) + f_b.astype(jnp.float32))
    c = jnp.cumsum(log_f, axis=1).transpose(0, 2, 1)
    c = jnp.pad(c, ((0, 0), (0, 0), (0, lp - length)), mode='edge')
    return k, v, c

def forgetting_attention(q, k, v, c):
    lp = q.shape[2]
    scale = q.shape[-1] ** -0.5
    outs = []
    for q0 in range(0, lp, Q_BLOCK):
        end = q0 + Q_BLOCK
        s = jnp.einsum('bhqd,bhkd->bhqk', q[:, :, q0:end], k[:, :, :end]).astype(jnp.float32) * scale
        s = s + c[:, :, q0:end, None] - c[:, :, None, :end]
        mask = jnp.arange(end)[None, :] <= jnp.arange(q0, end)[:, None]
        s = jnp.where(mask, s, -jnp.inf)
        p = jax.nn.softmax(s, axis=-1).astype(v.dtype)
        outs.append(jnp.einsum('bhqk,bhkd->bhqd', p, v[:, :, :end]))
    return jnp.concatenate(outs, axis=2)

def fox_mixer(x, w_in, w_out, k, v, c):
    bsz, length, _ = x.shape
    qg = x @ w_in
    q = to_heads_padded(qg[..., :D_MODEL], k.shape[2])
    o = forgetting_attention(q, k, v, c)[:, :, :length]
    o = o.transpose(0, 2, 1, 3).reshape(bsz, length, D_MODEL)
    return (o * jax.nn.sigmoid(qg[..., D_MODEL:])) @ w_out

def first_inputs(seed: int = 0) -> dict:
    key = jax.random.key(seed)
    ks = jax.random.split(key, 24)
    f32 = jnp.float32
    d = D_MODEL

    def nrm(k, shape, scale):
        return jax.random.normal(k, shape, f32) * scale

    u = jax.random.uniform(ks[9], (N_A_LAYERS, D_RNN), f32, 0.9, 0.999)
    a0 = u ** (1.0 / LRU_C)
    lam = jnp.log(a0) - jnp.log1p(-a0)

    kv_w = jnp.concatenate([
        nrm(ks[11], (d, d), d ** -0.5),
        nrm(ks[12], (d, d), d ** -0.5 * DN_BETA),
        nrm(ks[13], (d, N_FOX_HEADS), d ** -0.5),
    ], axis=1)

    return {
        "x": nrm(ks[0], (BATCH, SEQ, d), 1.0),
        "meta": nrm(ks[1], (N_META, d), 1.0),
        "a_w_in": nrm(ks[2], (N_A_LAYERS, d, 2 * D_RNN), d ** -0.5),
        "a_conv_w": nrm(ks[3], (N_A_LAYERS, CONV_A_WIDTH, D_RNN), CONV_A_WIDTH ** -0.5),
        "a_conv_b": nrm(ks[4], (N_A_LAYERS, D_RNN), 0.02),
        "a_w_r": nrm(ks[5], (N_A_LAYERS, N_LRU_BLOCKS, LRU_BLOCK, LRU_BLOCK), LRU_BLOCK ** -0.5),
        "a_b_r": nrm(ks[6], (N_A_LAYERS, D_RNN), 0.02),
        "a_w_i": nrm(ks[7], (N_A_LAYERS, N_LRU_BLOCKS, LRU_BLOCK, LRU_BLOCK), LRU_BLOCK ** -0.5),
        "a_b_i": nrm(ks[8], (N_A_LAYERS, D_RNN), 0.02),
        "a_lambda": lam,
        "a_w_out": nrm(ks[10], (N_A_LAYERS, D_RNN, d), D_RNN ** -0.5 * DN_BETA),
        "kv_w": kv_w,
        "kv_f_b": jax.random.uniform(ks[14], (N_FOX_HEADS,), f32, 1.0, 4.0),
        "b_w_in": nrm(ks[15], (N_B_LAYERS, d, 2 * d), d ** -0.5),
        "b_w_out": nrm(ks[16], (N_B_LAYERS, d, d), d ** -0.5 * DN_BETA),
        "f_w_in": nrm(ks[17], (DEPTH, d, 2 * D_FF), d ** -0.5),
        "f_conv_w": nrm(ks[18], (DEPTH, CONV_F_WIDTH, 2 * D_FF), CONV_F_WIDTH ** -0.5),
        "f_conv_b": nrm(ks[19], (DEPTH, 2 * D_FF), 0.02),
        "f_w_out": nrm(ks[20], (DEPTH, D_FF, d), D_FF ** -0.5 * DN_BETA),
        "ln1_g": 1.0 + nrm(ks[21], (DEPTH, d), 0.02),
        "ln1_b": nrm(ks[22], (DEPTH, d), 0.02),
        "ln2_g": 1.0 + nrm(ks[23], (DEPTH, d), 0.02),
        "ln2_b": nrm(jax.random.fold_in(key, 99), (DEPTH, d), 0.02),
    }

def first_block(x, meta, a_w_in, a_conv_w, a_conv_b, a_w_r, a_b_r, a_w_i, a_b_i, a_lambda, a_w_out,
              kv_w, kv_f_b, b_w_in, b_w_out, f_w_in, f_conv_w, f_conv_b, f_w_out,
              ln1_g, ln1_b, ln2_g, ln2_b):
    bsz = x.shape[0]
    h = jnp.concatenate([jnp.broadcast_to(meta.astype(x.dtype), (bsz, N_META, D_MODEL)), x], axis=1)
    k = v = c = None
    for layer in range(DEPTH):
        if layer < N_A_LAYERS:
            mix = recurrent_mixer(h, a_w_in[layer], a_conv_w[layer], a_conv_b[layer],
                                  a_w_r[layer], a_b_r[layer], a_w_i[layer], a_b_i[layer],
                                  a_lambda[layer], a_w_out[layer])
        else:
            if layer == N_A_LAYERS:
                k, v, c = shared_kv(h, kv_w, kv_f_b)
            j = layer - N_A_LAYERS
            mix = fox_mixer(h, b_w_in[j], b_w_out[j], k, v, c)
        h = layer_norm(DN_ALPHA * h + mix, ln1_g[layer], ln1_b[layer])
        ffn = conv_ffn(h, f_w_in[layer], f_conv_w[layer], f_conv_b[layer], f_w_out[layer])
        h = layer_norm(DN_ALPHA * h + ffn, ln2_g[layer], ln2_b[layer])
    return h[:, N_META:]


SSD_D_INNER = D_MODEL
SSD_HEADDIM = 64
SSD_HEADS = SSD_D_INNER // SSD_HEADDIM
SSD_GROUPS = 2
SSD_STATE = 128
SSD_CONV = 5
SSD_CHUNK = 128
MLSTM_D = D_MODEL
MLSTM_HEADS = 8
MLSTM_HEADDIM = MLSTM_D // MLSTM_HEADS
MLSTM_CHUNK = 128
GLA_HEADS = 4
GLA_DK = D_MODEL // 2
GLA_DV = D_MODEL
GLA_HEAD_DK = GLA_DK // GLA_HEADS
GLA_HEAD_DV = GLA_DV // GLA_HEADS
GLA_RANK = 16
GLA_TAU = 16.0
GLA_CHUNK = 64
FFN_DIM = 11 * D_MODEL // 4
FFN_CONV = 3
NORM_EPS = 1e-6

SSD_XBC = SSD_D_INNER + 2 * SSD_GROUPS * SSD_STATE
L0_SPLITS = (SSD_D_INNER, SSD_XBC, 2 * SSD_HEADS, MLSTM_D, MLSTM_D, MLSTM_D, MLSTM_D, 4 * MLSTM_HEADS)
L0_IN = sum(L0_SPLITS)
L0_MIX = SSD_D_INNER + MLSTM_D
L1_SPLITS = (GLA_DK, GLA_DK, GLA_DV, GLA_DV, 2 * GLA_RANK)
L1_IN = sum(L1_SPLITS)
N_EVEN_LAYERS = (DEPTH + 1) // 2
N_ODD_LAYERS = DEPTH // 2


def _split(u, sizes):
    return jnp.split(u, np.cumsum(sizes)[:-1].tolist(), axis=-1)

def _rev(t):
    return jnp.flip(t, axis=1)

def _lower_tri(n):
    return jnp.tril(jnp.ones((n, n), dtype=bool))

def _rmsnorm(x, g):
    xf = x.astype(jnp.float32)
    y = xf * lax.rsqrt(jnp.mean(xf * xf, axis=-1, keepdims=True) + NORM_EPS)
    return (y * g.astype(jnp.float32)).astype(x.dtype)

def _head_rmsnorm(x, g, n_heads):
    shp = x.shape
    xh = x.reshape(shp[:-1] + (n_heads, shp[-1] // n_heads))
    return _rmsnorm(xh, g.reshape(n_heads, -1)).reshape(shp)

def _dwconv(x, w, b):
    k = w.shape[0]
    y = lax.conv_general_dilated(x, w[:, None, :], window_strides=(1,), padding=[(k // 2, k // 2)],
                                 dimension_numbers=('NWC', 'WIO', 'NWC'), feature_group_count=x.shape[-1])
    return y + b

def _bidirectional(scan_fn, seq_fwd, seq_bwd, par_fwd=(), par_bwd=()):
    y_f = scan_fn(*seq_fwd, *par_fwd)
    y_b = scan_fn(*[_rev(t) for t in seq_bwd], *par_bwd)
    return y_f + _rev(y_b)

def _ssd_scan(x, dt, bm, cm, a):
    bsz, s, nh, p = x.shape
    g, n = bm.shape[2], bm.shape[3]
    e = nh // g
    l = SSD_CHUNK
    c = s // l
    dt = dt.astype(jnp.float32)
    xdt = (x * dt[..., None]).reshape(bsz, c, l, g, e, p)
    cs = jnp.cumsum((dt * a.astype(jnp.float32)).reshape(bsz, c, l, g, e), axis=2)
    bm = bm.reshape(bsz, c, l, g, n)
    cm = cm.reshape(bsz, c, l, g, n)
    cs_t = jnp.transpose(cs, (0, 3, 4, 1, 2))
    decay = jnp.exp(jnp.where(_lower_tri(l), cs_t[..., :, None] - cs_t[..., None, :], -jnp.inf))
    cb = jnp.einsum('bclgn,bcsgn->bgcls', cm, bm)
    y = jnp.einsum('bgecls,bcsgep->bclgep', cb[:, :, None] * decay, xdt)
    x_end = xdt * jnp.exp(cs[:, :, -1:] - cs)[..., None]
    states = jnp.einsum('bclgn,bclgep->cbgepn', bm, x_end)
    chunk_decay = jnp.exp(jnp.transpose(cs[:, :, -1], (1, 0, 2, 3)))

    def step(hs, inp):
        st, dec = inp
        return dec[..., None, None] * hs + st, hs

    _, h_prev = lax.scan(step, jnp.zeros(states.shape[1:], states.dtype), (states, chunk_decay))
    y = y + jnp.einsum('bclgn,cbgepn->bclgep', cm, h_prev) * jnp.exp(cs)[..., None]
    return y.reshape(bsz, s, nh, p)

def _mlstm_scan(q, k, v, ig, lf):
    bsz, s, nh, dk = q.shape
    dv = v.shape[-1]
    l = MLSTM_CHUNK
    c = s // l
    q = q.reshape(bsz, c, l, nh, dk)
    k = k.reshape(bsz, c, l, nh, dk)
    v = v.reshape(bsz, c, l, nh, dv)
    ig = ig.astype(jnp.float32).reshape(bsz, c, l, nh)
    fc = jnp.cumsum(lf.astype(jnp.float32).reshape(bsz, c, l, nh), axis=2)
    f_end = fc[:, :, -1]
    a = f_end[:, :, None] - fc + ig
    m_loc = jnp.max(a, axis=2)
    kw = k * jnp.exp(a - m_loc[:, :, None])[..., None]
    c_loc = jnp.einsum('bclhk,bclhv->cbhkv', kw, v)
    n_loc = jnp.transpose(jnp.sum(kw, axis=2), (1, 0, 2, 3))

    def step(carry, inp):
        c_st, n_st, m_st = carry
        c_l, n_l, m_l, f_l = inp
        m_new = jnp.maximum(f_l + m_st, m_l)
        s_old = jnp.exp(f_l + m_st - m_new)
        s_loc = jnp.exp(m_l - m_new)
        c_new = s_old[..., None, None] * c_st + s_loc[..., None, None] * c_l
        n_new = s_old[..., None] * n_st + s_loc[..., None] * n_l
        return (c_new, n_new, m_new), (c_st, n_st, m_st)

    init = (jnp.zeros(c_loc.shape[1:], c_loc.dtype), jnp.zeros(n_loc.shape[1:], n_loc.dtype),
            jnp.zeros((bsz, nh), jnp.float32))
    _, (c_st, n_st, m_st) = lax.scan(step, init, (c_loc, n_loc, jnp.transpose(m_loc, (1, 0, 2)),
                                                  jnp.transpose(f_end, (1, 0, 2))))
    fc_t = jnp.transpose(fc, (0, 3, 1, 2))
    ig_t = jnp.transpose(ig, (0, 3, 1, 2))
    dmat = jnp.where(_lower_tri(l), fc_t[..., :, None] - fc_t[..., None, :] + ig_t[..., None, :], -jnp.inf)
    m_inter = fc_t + jnp.transpose(m_st, (1, 2, 0))[..., None]
    m_t = jnp.maximum(m_inter, jnp.max(dmat, axis=-1))
    wmat = jnp.einsum('bclhk,bcshk->bhcls', q, k) * jnp.exp(dmat - m_t[..., None])
    s_inter = jnp.transpose(jnp.exp(m_inter - m_t), (0, 2, 3, 1))
    num = (jnp.einsum('bhcls,bcshv->bclhv', wmat, v)
           + s_inter[..., None] * jnp.einsum('bclhk,cbhkv->bclhv', q, c_st))
    den = (jnp.transpose(jnp.sum(wmat, axis=-1), (0, 2, 3, 1))
           + s_inter * jnp.einsum('bclhk,cbhk->bclh', q, n_st))
    floor = jnp.exp(-jnp.transpose(m_t, (0, 2, 3, 1)))
    h = num / jnp.maximum(jnp.abs(den), floor)[..., None]
    return h.reshape(bsz, s, nh, dv)

def _gla_scan(q, k, v, la):
    bsz, s, nh, dk = q.shape
    dv = v.shape[-1]
    l = GLA_CHUNK
    c = s // l
    q = q.reshape(bsz, c, l, nh, dk)
    k = k.reshape(bsz, c, l, nh, dk)
    v = v.reshape(bsz, c, l, nh, dv)
    bc = jnp.cumsum(la.astype(jnp.float32).reshape(bsz, c, l, nh, dk), axis=2)
    b_end = bc[:, :, -1:]
    q_in = q * jnp.exp(bc)
    att = jnp.einsum('bclhk,bcshk->bhcls', q_in, k * jnp.exp(-bc))
    att = jnp.where(_lower_tri(l), att, 0.0)
    o = jnp.einsum('bhcls,bcshv->bclhv', att, v)
    u = jnp.einsum('bclhk,bclhv->cbhkv', k * jnp.exp(b_end - bc), v)
    dec = jnp.exp(jnp.transpose(b_end[:, :, 0], (1, 0, 2, 3)))

    def step(st, inp):
        u_c, d_c = inp
        return d_c[..., None] * st + u_c, st

    _, s_prev = lax.scan(step, jnp.zeros(u.shape[1:], u.dtype), (u, dec))
    o = o + jnp.einsum('bclhk,cbhkv->bclhv', q_in, s_prev)
    return o.reshape(bsz, s, nh, dv)

def _ssd_mlstm_mixer(h, w_in, conv_w, conv_b, dt_bias, a_log, d_skip, ssd_norm, ig_bias, fg_bias, mlstm_norm, w_out):
    bsz, s, _ = h.shape
    z, xbc, dt_raw, q, k, v, o_pre, gates = _split(h @ w_in, L0_SPLITS)
    xbc = jax.nn.silu(_dwconv(xbc, conv_w, conv_b))
    xs, bm, cm = _split(xbc, (SSD_D_INNER, SSD_GROUPS * SSD_STATE, SSD_GROUPS * SSD_STATE))
    xs = xs.reshape(bsz, s, SSD_HEADS, SSD_HEADDIM)
    bm = bm.reshape(bsz, s, SSD_GROUPS, SSD_STATE)
    cm = cm.reshape(bsz, s, SSD_GROUPS, SSD_STATE)
    dt = jax.nn.softplus(dt_raw.reshape(bsz, s, 2, SSD_HEADS).astype(jnp.float32) + dt_bias)
    a = -jnp.exp(a_log.astype(jnp.float32))
    y = _bidirectional(_ssd_scan, (xs, dt[:, :, 0], bm, cm), (xs, dt[:, :, 1], bm, cm), (a[0],), (a[1],))
    y = y + d_skip[:, None] * xs
    y = _head_rmsnorm(y.reshape(bsz, s, SSD_D_INNER) * jax.nn.silu(z), ssd_norm, SSD_GROUPS)
    q = q.reshape(bsz, s, MLSTM_HEADS, MLSTM_HEADDIM)
    k = k.reshape(bsz, s, MLSTM_HEADS, MLSTM_HEADDIM) * MLSTM_HEADDIM ** -0.5
    v = v.reshape(bsz, s, MLSTM_HEADS, MLSTM_HEADDIM)
    gates = gates.reshape(bsz, s, 2, 2, MLSTM_HEADS).astype(jnp.float32)
    ig = gates[:, :, 0] + ig_bias
    lf = jax.nn.log_sigmoid(gates[:, :, 1] + fg_bias)
    hm = _bidirectional(_mlstm_scan, (q, k, v, ig[:, :, 0], lf[:, :, 0]), (q, k, v, ig[:, :, 1], lf[:, :, 1]))
    hm = jax.nn.sigmoid(o_pre) * hm.reshape(bsz, s, MLSTM_D)
    hm = _head_rmsnorm(hm, mlstm_norm, MLSTM_HEADS)
    return jnp.concatenate([y, hm], axis=-1) @ w_out

def _gla_mixer(h, w_in, gate_w2, gate_b, gla_norm, w_out):
    bsz, s, _ = h.shape
    q, k, v, r, g_lr = _split(h @ w_in, L1_SPLITS)
    q = q.reshape(bsz, s, GLA_HEADS, GLA_HEAD_DK) * GLA_HEAD_DK ** -0.5
    k = k.reshape(bsz, s, GLA_HEADS, GLA_HEAD_DK)
    v = v.reshape(bsz, s, GLA_HEADS, GLA_HEAD_DV)
    g_lr = g_lr.reshape(bsz, s, 2, GLA_RANK)
    logits = jnp.einsum('bsdr,drk->bsdk', g_lr, gate_w2) + gate_b
    la = (jax.nn.log_sigmoid(logits.astype(jnp.float32)) / GLA_TAU).reshape(bsz, s, 2, GLA_HEADS, GLA_HEAD_DK)
    o = _bidirectional(_gla_scan, (q, k, v, la[:, :, 0]), (q, k, v, la[:, :, 1]))
    o = _head_rmsnorm(o.reshape(bsz, s, GLA_DV), gla_norm, GLA_HEADS) * jax.nn.silu(r)
    return o @ w_out

def _conv_ffn(h, w_up, conv_w, conv_b, w_down):
    u = _dwconv(h @ w_up, conv_w, conv_b)
    gate, val = jnp.split(u, 2, axis=-1)
    return (jax.nn.gelu(gate, approximate=True) * val) @ w_down

def second_inputs(seed: int = 0) -> dict:
    key = jax.random.key(seed)
    keys = jax.random.split(key, 24)

    def nrm(i, shape, scale):
        return scale * jax.random.normal(keys[i], shape, jnp.float32)

    ne, no = N_EVEN_LAYERS, N_ODD_LAYERS
    dt0 = jnp.exp(jax.random.uniform(keys[5], (ne, 2, SSD_HEADS), jnp.float32, math.log(1e-3), math.log(1e-1)))
    return {
        'x': nrm(0, (BATCH, SEQ, D_MODEL), 1.0),
        'norm_g': 1.0 + nrm(1, (DEPTH, 4, D_MODEL), 0.05),
        'ab_w_in': nrm(2, (ne, D_MODEL, L0_IN), D_MODEL ** -0.5),
        'ab_conv_w': nrm(3, (ne, SSD_CONV, SSD_XBC), SSD_CONV ** -0.5),
        'ab_conv_b': nrm(4, (ne, SSD_XBC), 0.02),
        'ab_dt_bias': dt0 + jnp.log(-jnp.expm1(-dt0)),
        'ab_a_log': jnp.log(jax.random.uniform(keys[6], (ne, 2, SSD_HEADS), jnp.float32, 1.0, 16.0)),
        'ab_d_skip': 1.0 + nrm(7, (ne, SSD_HEADS), 0.1),
        'ab_ssd_norm': 1.0 + nrm(8, (ne, SSD_D_INNER), 0.05),
        'ab_ig_bias': nrm(9, (ne, 2, MLSTM_HEADS), 0.1),
        'ab_fg_bias': jnp.linspace(3.0, 6.0, MLSTM_HEADS, dtype=jnp.float32) + nrm(10, (ne, 2, MLSTM_HEADS), 0.1),
        'ab_mlstm_norm': 1.0 + nrm(11, (ne, MLSTM_D), 0.05),
        'ab_w_out': nrm(12, (ne, L0_MIX, D_MODEL), L0_MIX ** -0.5),
        'c_w_in': nrm(13, (no, D_MODEL, L1_IN), D_MODEL ** -0.5),
        'c_gate_w2': nrm(14, (no, 2, GLA_RANK, GLA_DK), GLA_RANK ** -0.5),
        'c_gate_b': nrm(15, (no, 2, GLA_DK), 0.1),
        'c_norm': 1.0 + nrm(16, (no, GLA_DV), 0.05),
        'c_w_out': nrm(17, (no, GLA_DV, D_MODEL), GLA_DV ** -0.5),
        'ffn_w_up': nrm(18, (DEPTH, D_MODEL, 2 * FFN_DIM), D_MODEL ** -0.5),
        'ffn_conv_w': nrm(19, (DEPTH, FFN_CONV, 2 * FFN_DIM), FFN_CONV ** -0.5),
        'ffn_conv_b': nrm(20, (DEPTH, 2 * FFN_DIM), 0.02),
        'ffn_w_down': nrm(21, (DEPTH, FFN_DIM, D_MODEL), FFN_DIM ** -0.5),
    }

def second_block(x, norm_g, ab_w_in, ab_conv_w, ab_conv_b, ab_dt_bias, ab_a_log, ab_d_skip, ab_ssd_norm,
              ab_ig_bias, ab_fg_bias, ab_mlstm_norm, ab_w_out, c_w_in, c_gate_w2, c_gate_b, c_norm, c_w_out,
              ffn_w_up, ffn_conv_w, ffn_conv_b, ffn_w_down):
    for i in range(DEPTH):
        j = i // 2
        h = _rmsnorm(x, norm_g[i, 0])
        if i % 2 == 0:
            h = _ssd_mlstm_mixer(h, ab_w_in[j], ab_conv_w[j], ab_conv_b[j], ab_dt_bias[j], ab_a_log[j],
                                 ab_d_skip[j], ab_ssd_norm[j], ab_ig_bias[j], ab_fg_bias[j], ab_mlstm_norm[j],
                                 ab_w_out[j])
        else:
            h = _gla_mixer(h, c_w_in[j], c_gate_w2[j], c_gate_b[j], c_norm[j], c_w_out[j])
        x = x + _rmsnorm(h, norm_g[i, 1])
        f = _conv_ffn(_rmsnorm(x, norm_g[i, 2]), ffn_w_up[i], ffn_conv_w[i], ffn_conv_b[i], ffn_w_down[i])
        x = x + _rmsnorm(f, norm_g[i, 3])
    return x


def setup_inputs(seed=0):
    out = dict(first_inputs(seed))
    for name, value in second_inputs(seed + 1).items():
        if name != "x":
            out[name + "_2"] = value
    return out


def reference(
    x, meta, a_w_in, a_conv_w, a_conv_b, a_w_r, a_b_r, a_w_i, a_b_i, a_lambda, a_w_out, kv_w,
    kv_f_b, b_w_in, b_w_out, f_w_in, f_conv_w, f_conv_b, f_w_out, ln1_g, ln1_b, ln2_g, ln2_b,
    norm_g_2, ab_w_in_2, ab_conv_w_2, ab_conv_b_2, ab_dt_bias_2, ab_a_log_2, ab_d_skip_2,
    ab_ssd_norm_2, ab_ig_bias_2, ab_fg_bias_2, ab_mlstm_norm_2, ab_w_out_2, c_w_in_2,
    c_gate_w2_2, c_gate_b_2, c_norm_2, c_w_out_2, ffn_w_up_2, ffn_conv_w_2, ffn_conv_b_2,
    ffn_w_down_2,
):
    x = first_block(
        x, meta, a_w_in, a_conv_w, a_conv_b, a_w_r, a_b_r, a_w_i, a_b_i, a_lambda, a_w_out,
        kv_w, kv_f_b, b_w_in, b_w_out, f_w_in, f_conv_w, f_conv_b, f_w_out, ln1_g, ln1_b, ln2_g,
        ln2_b,
    )
    return second_block(
        x, norm_g_2, ab_w_in_2, ab_conv_w_2, ab_conv_b_2, ab_dt_bias_2, ab_a_log_2, ab_d_skip_2,
        ab_ssd_norm_2, ab_ig_bias_2, ab_fg_bias_2, ab_mlstm_norm_2, ab_w_out_2, c_w_in_2,
        c_gate_w2_2, c_gate_b_2, c_norm_2, c_w_out_2, ffn_w_up_2, ffn_conv_w_2, ffn_conv_b_2,
        ffn_w_down_2,
    )


_drawn_inputs = setup_inputs


def setup_inputs(seed=0):
    import zlib

    import numpy as np

    out = dict(_drawn_inputs(seed))
    spreads = {}
    factors = {'a_b_r': 25.186, 'a_b_i': 8.0, 'ab_ig_bias_2': 8.0}
    for name, (base, spread) in spreads.items():
        noise = np.random.default_rng([zlib.crc32(name.encode()), seed]).standard_normal(out[name].shape)
        drawn = base * np.exp(spread * noise) if base else spread * noise
        out[name] = jnp.asarray(drawn.astype(out[name].dtype))
    for name, factor in factors.items():
        out[name] = (out[name] * factor).astype(out[name].dtype)
    return out
```

```python
from contextlib import ExitStack

import concourse.bass as bass
from concourse import mybir
import numpy as np

F32 = mybir.dt.float32
ALU = mybir.AluOpType
ACT = mybir.ActivationFunctionType
AXX = mybir.AxisListType.X
ds = bass.ds

P = 128
D = 1024
KD = D // P
META = 16
SEQ = 512
T1 = META + SEQ
T2 = SEQ
HALF = T1 // 2
RNN = 3 * D // 2
LRU = 96
DFF = 2816
NF = DFF // P
SLOTS = 4
BUFS = 4
ALPHA = float((2 * 2) ** 0.25)
BIG = 1.0e30
LRU_PIECES = [(0, 0), (0, 1), (1, 0), (1, 1), (1, 2), (2, 1), (2, 2)]

UNITS = {}
_u = 0
for _name, _count in [("lru", 32), ("lru_out", 16), ("ffn0", 68), ("fox_f", 1), ("fox", 32), ("fox_out", 8), ("ffn1", 68),
                      ("ssd_pre", 6), ("ssd", 16), ("mlstm", 32), ("mix_out", 16), ("ffn2", 68),
                      ("gla_pre", 1), ("gla", 24), ("gla_out", 8), ("ffn3", 68)]:
    UNITS[_name] = _u
    _u += _count
N_UNITS = _u

COLS = {}
_c = 0
for _name, _count in [("a_conv", 12 * 5), ("a_br", 12), ("a_bi", 12), ("a_lam", 12), ("fox_fb", 1),
                      ("ln1_g", 16), ("ln1_b", 16), ("ln2_g", 16), ("ln2_b", 16), ("norm_g", 64),
                      ("ffn0", 8 * NF), ("ffn1", 8 * NF), ("ffn2", 8 * NF), ("ffn3", 8 * NF),
                      ("ab_conv", 12 * 6), ("dt_bias", 1), ("a_log", 1), ("ig_bias", 1), ("fg_bias", 1),
                      ("d_skip", 8), ("ssd_norm", 8), ("mlstm_norm", 8), ("gate_b", 8), ("gla_norm", 8)]:
    COLS[_name] = _c
    _c += _count
N_COLS = _c


class Chain:

    def __init__(self, eng, sem):
        self.eng, self.sem, self.n, self.at = eng, sem, 0, 0

    def __call__(self, ins):
        ins.then_inc(self.sem, 1)
        self.n += 1
        self.eng.wait_ge(self.sem, self.at + self.n)

    def loop(self, i, per):
        self.start, self.per = self.n, per
        self.at = i * per

    def end(self, trips):
        assert self.n - self.start == self.per, ("per", self.n - self.start)
        self.n += (trips - 1) * self.per
        self.at = 0


def build(nc, x_t, units, cols, gate_w2, out, stop_after=None):
    ctx = ExitStack()
    with ctx:
        def sb(name, shape):
            return ctx.enter_context(nc.sbuf_tensor(name, shape, F32))

        def sem(name):
            return ctx.enter_context(nc.semaphore(name))

        X = sb("residual", [P, KD, T1])
        Z = sb("stream", [P, KD, T1])
        A = sb("acts", [P, NF, T1])
        W = sb("w_ring", [P, SLOTS, KD, P])
        PAR = sb("params", [P, N_COLS])
        ID = sb("identity", [P, P])
        ONES = sb("ones", [P, P])
        MEANW = sb("mean_weights", [P, 3, P])
        CAUSAL_ADD = sb("causal_add", [P, P])
        LOWER = sb("keep_l_ge_s", [P, P])
        UPPER = sb("keep_l_le_s", [P, P])
        NORM_MU = sb("norm_mu", [P, T1])
        NORM_R = sb("norm_r", [P, T1])
        SMALL = sb("small", [P, 192])
        SCR = sb("scratch", [P, 20200])
        PS = ctx.enter_context(nc.psum_tensor("psum", [P, 8, 512], F32))
        PSF = PS[:, :, :].rearrange("p b c -> p (b c)")

        def scratch(at, *shape):
            n = int(np.prod(shape))
            v = SCR[:, at:at + n]
            if len(shape) == 2:
                v = v.rearrange("p (a b) -> p a b", a=shape[0])
            if len(shape) == 3:
                v = v.rearrange("p (a b c) -> p a b c", a=shape[0], b=shape[1])
            return v

        def ps_tile(bank, T, rows=P):
            return PS[0:rows, bank:bank + 2, 0:HALF] if T == T1 else PS[0:rows, bank, 0:T]

        def sv(ap, T):
            return ap.rearrange("p (h t) -> p h t", h=2) if T == T1 else ap

        def parts(T):
            return [(0, 0, HALF), (1, HALF, HALF)] if T == T1 else [(0, 0, T)]

        def col(name, k=0, rows=P):
            if isinstance(k, int):
                return PAR[0:rows, COLS[name] + k:COLS[name] + k + 1]
            return PAR[0:rows, ds(k + COLS[name], 1)]

        w_full = [sem(f"w_full{b}") for b in range(SLOTS)]
        w_started = sem("w_started")
        tile_full = sem("tile_full")
        tile_free = sem("tile_free")
        loaded = sem("loaded")
        w2_loaded = sem("w2_loaded")
        consts_ready = sem("consts_ready")
        out_done = sem("out_done")
        s_dve = sem("dve_chain")
        s_act = sem("act_chain")
        s_pool = sem("pool_chain")
        setup_lam = sem("setup_lam")
        setup_lam_act = sem("setup_lam_act")
        lam_ready = sem("lam_ready")

        sems = {}

        def S(name):
            if name not in sems:
                sems[name] = sem(name)
            return sems[name]

        NORMS = ["lru", "ffn0", "fox", "ffn1", "mixin", "mix", "ffn2in", "ffn2", "glain", "gla", "ffn3in", "ffn3"]
        FFNS = ["ffn0", "ffn1", "ffn2", "ffn3"]
        PER = {"z": KD, "mean": 1, "mu": 1, "ctr": KD, "sc": KD, "sq": KD, "var": 1, "std": 1, "x": KD,
               "pad": 1, "tap": 2 * NF, "conv": 2 * NF, "gelu": NF, "act": NF}

        def shared(what, name):
            return S(("ffn_" if what in ("pad", "tap", "conv", "gelu", "act") else "norm_") + what)

        def when(name, what, n):
            order = FFNS if what in ("pad", "tap", "conv", "gelu", "act") else NORMS
            return shared(what, name), n + PER[what] * order.index(name)

        def at_k(name, what):
            return shared(what, name), lambda k: when(name, what, k + 1)[1]

        block = ctx.enter_context(nc.Block())

        TILES = {}
        n = 0
        for name, count in [("lru", 48), ("lru_out", 8), ("ffn0", 52), ("fox_f", 1), ("fox", 32), ("fox_out", 8), ("ffn1", 52),
                            ("ssd_pre", 7), ("ssd", 16), ("mlstm", 32), ("mix_out", 8), ("ffn2", 52),
                            ("gla_pre", 1), ("gla", 24), ("gla_out", 8), ("ffn3", 52)]:
            TILES[name] = n
            n += count
        TILES["end"] = n

        phases = ["lru", "ffn0", "fox", "ffn1", "mix", "ffn2", "gla", "ffn3"]
        if stop_after is not None:
            phases = phases[:phases.index(stop_after) + 1]

        CH = [(0, META)] + [(META + P * q, P) for q in range(SEQ // P)]
        STEPS = [(ch, hh) for ch in range(len(CH)) for hh in range(2)]
        NS = len(STEPS)
        fx_q, fx_k, fx_sg = scratch(9452, 2, T1), scratch(528, T1), scratch(1056, T1)
        fx_v = scratch(1584, 5, P)
        fx_p, fx_ptb, fx_o = scratch(2224, 2, T1), scratch(3280, 2, 5, P), scratch(4560, P)
        fx_nm, fx_sum, fx_rs = scratch(4688, 2), scratch(4690, 2), scratch(4692, 2)
        fx_c, fx_nc = scratch(4700, T1), scratch(5228, T1)
        fx_l, fx_r = scratch(5756, 2, T1), scratch(6812, 2, T1)
        fx_x, fx_ab, fx_e = scratch(7868, T1), scratch(8396, T1), scratch(8924, T1)

        def apart(pe):
            pe.sem_inc(S("pe_steps"), 1)

        def fox_pe(pe, unit, buffer_free, gemm, gemm_tokens, h):
            pe.wait_ge(tile_free, BUFS + TILES["fox_f"])
            s = unit(UNITS["fox_f"], 0, 0, 0)
            gemm(2 * (TILES["fox_f"] % 4), [(s, 0, KD)], h, T1, 0, 16).then_inc(tile_full, 1)
            bank = lambda j: 2 * ((TILES["fox"] + j) % 4)
            with pe.Fori(0, KD) as i:
                pe.wait_ge(S("fx_out"), i * 5)
                for j in range(4):
                    buffer_free("fox", i, 4, j, 4)
                    s = unit(UNITS["fox"], i, 4, j)
                    if j == 2:
                        chunks = [(1, 0, 0, META)] + [(0, P * q, META + P * q, P) for q in range(4)]
                        gemm_tokens(bank(j), s, h, chunks).then_inc(tile_full, 1)
                    else:
                        gemm(bank(j), [(s, 0, KD)], h, T1).then_inc(tile_full, 1)
                pe.wait_ge(tile_free, i * 4 + (BUFS + TILES["fox"] + 4))
                pe.wait_ge(S("fx_sel"), i * 2 + 2)

                def scores(n):
                    ch, hh = STEPS[n]
                    qs, qn = CH[ch]
                    ke = qs + qn
                    base = 512 * (4 + 2 * (n % 2))
                    if n >= 2:
                        pe.wait_ge(S("fx_exp"), i * NS + (n - 1))
                    apart(pe)
                    for a, b in [(0, min(ke, 512))] + ([(512, ke)] if ke > 512 else []):
                        nc.tensor.matmul(PSF[0:qn, base + a:base + b], fx_q[:, hh, qs:ke], fx_k[:, a:b], start=True, stop=False)
                        da = max(a, qs)
                        if da < b:
                            nc.tensor.matmul(PSF[0:qn, base + da:base + b], ID[0:qn, 0:qn], CAUSAL_ADD[0:qn, da - qs:b - qs],
                                             start=False, stop=False)
                        mm = nc.tensor.matmul(PSF[0:qn, base + a:base + b], fx_l[:, hh, qs:ke], fx_r[:, hh, a:b],
                                              start=False, stop=True)
                    mm.then_inc(S("fx_s"), 1)

                def turn(ch):
                    qn = CH[ch][1]
                    pe.wait_ge(S("fx_on"), i * NS + (2 * ch + 2))
                    if ch > 0:
                        pe.wait_ge(S("fx_out"), i * 5 + ch)
                    apart(pe)
                    nc.tensor.transpose(PS[:, 3, 0:qn], fx_o[0:qn, :], ID[0:qn, 0:qn]).then_inc(S("fx_ot"), 1)

                scores(0)
                for n, (ch, hh) in enumerate(STEPS):
                    qs, qn = CH[ch]
                    if n + 1 < NS:
                        scores(n + 1)
                    pe.wait_ge(S("fx_exp"), i * NS + (n + 1))
                    apart(pe)
                    for kb in range(ch + 1):
                        ks, kn = CH[kb]
                        dst = PS[0:kn, 1, 0:qn] if kb == 0 else PS[0:kn, 0, P * (kb - 1):P * (kb - 1) + qn]
                        mm = nc.tensor.transpose(dst, fx_p[0:qn, n % 2, ks:ks + kn], ID[0:qn, 0:qn])
                    mm.then_inc(S("fx_tr"), 1)
                    if hh == 0 and ch > 0:
                        turn(ch - 1)
                    pe.wait_ge(S("fx_pt"), i * NS + (n + 1))
                    if n > 0:
                        pe.wait_ge(S("fx_on"), i * NS + n)
                    apart(pe)
                    for kb in range(ch + 1):
                        kn = CH[kb][1]
                        mm = nc.tensor.matmul(PS[0:qn, 2, 0:P], fx_ptb[0:kn, n % 2, kb, 0:qn], fx_v[0:kn, kb, :],
                                              start=(kb == 0), stop=(kb == ch))
                    mm.then_inc(S("fx_pv"), 1)
                turn(len(CH) - 1)
            pe.wait_ge(S("fx_out"), 5 * KD)

        def fox_act(act, c, full):
            full("fox_f", 0, 0, 0)
            nc.scalar.activation(sv(fx_x[0:16, :], T1), ps_tile(2 * (TILES["fox_f"] % 4), T1, 16), ACT.Identity,
                                 bias=col("fox_fb", 0, 16)).then_inc(tile_free, 1)
            act.wait_ge(S("fx_abs"), 1)
            c(nc.scalar.activation(fx_e[0:16, :], fx_ab[0:16, :], ACT.Exp, scale=-1.0))
            nc.scalar.activation(fx_ab[0:16, :], fx_e[0:16, :], ACT.Ln, bias=SMALL[0:16, 182:183]).then_inc(S("fx_ln"), 1)
            bank = lambda j: 2 * ((TILES["fox"] + j) % 4)
            act.wait_ge(S("fx_zero"), 1)
            with act.Fori(0, KD) as i:
                act.wait_ge(S("fx_out"), i * 5)
                full("fox", i, 4, 0)
                for hh in range(2):
                    half = slice(64 * hh, 64 * hh + 64)
                    q = nc.scalar.activation(sv(fx_q[half, hh, :], T1), PS[half, bank(0):bank(0) + 2, 0:HALF], ACT.Copy, scale=0.125)
                q.then_inc(tile_free, 1)
                full("fox", i, 4, 1)
                nc.scalar.activation(sv(fx_k, T1), ps_tile(bank(1), T1), ACT.Copy).then_inc(tile_free, 1)
                full("fox", i, 4, 2)
                nc.scalar.activation(fx_v[0:META, 0, :], PS[0:META, bank(2) + 1, 0:P], ACT.Copy)
                nc.scalar.activation(fx_v[:, 1:5, :], PS[:, bank(2), :].rearrange("p (a b) -> p a b", a=4), ACT.Copy).then_inc(tile_free, 1)
                full("fox", i, 4, 3)
                nc.scalar.activation(sv(fx_sg, T1), ps_tile(bank(3), T1), ACT.Sigmoid).then_inc(tile_free, 1)

                def scaled(n):
                    ch, hh = STEPS[n]
                    qn = CH[ch][1]
                    act.wait_ge(S("fx_pv"), i * NS + (n + 1))
                    if hh == 0 and ch > 0:
                        act.wait_ge(S("fx_ot"), i * 5 + ch)
                    nc.scalar.activation(fx_o[0:qn, 64 * hh:64 * hh + 64], PS[0:qn, 2, 64 * hh:64 * hh + 64], ACT.Copy,
                                         scale=fx_rs[0:qn, n % 2:n % 2 + 1]).then_inc(S("fx_on"), 1)

                for n, (ch, hh) in enumerate(STEPS):
                    qs, qn = CH[ch]
                    ke = qs + qn
                    base = 512 * (4 + 2 * (n % 2))
                    act.wait_ge(S("fx_mx"), i * NS + (n + 1))
                    if n >= 2:
                        act.wait_ge(S("fx_tr"), i * NS + (n - 1))
                    nc.scalar.activation(fx_p[0:qn, n % 2, 0:ke], PSF[0:qn, base:base + ke], ACT.Exp, bias=fx_nm[0:qn, n % 2:n % 2 + 1],
                                         accum_out=fx_sum[0:qn, n % 2:n % 2 + 1]).then_inc(S("fx_exp"), 1)
                    if n >= 1:
                        scaled(n - 1)
                scaled(NS - 1)

        def fox_dve(dve, c):
            v = nc.vector
            c(v.memset(NORM_MU[:, :], 1.0))
            c(v.memset(fx_l[0:32, :, :], 0.0))
            c(v.memset(fx_l[64:128, :, :], 0.0))
            c(v.memset(fx_r[:, :, :], 1.0))
            c(v.memset(fx_l[32:64, :, :], 0.0))
            c(v.memset(fx_l[32:48, :, :], 1.0))
            c(v.memset(fx_q[64:128, 0, :], 0.0))
            v.memset(fx_q[0:64, 1, :], 0.0).then_inc(S("fx_zero"), 1)
            dve.wait_ge(tile_free, BUFS + TILES["fox_f"] + 1)
            x, ab = fx_x[0:16, :], fx_ab[0:16, :]
            v.scalar_tensor_tensor(out=ab, in0=x, scalar=-1.0, in1=x, op0=ALU.mult, op1=ALU.max).then_inc(S("fx_abs"), 1)
            dve.wait_ge(S("fx_ln"), 1)
            c(v.scalar_tensor_tensor(out=x, in0=x, scalar=0.0, in1=ab, op0=ALU.min, op1=ALU.subtract))
            c(v.tensor_tensor_scan(fx_c[0:16, :], NORM_MU[0:16, :], x, 0.0, ALU.mult, ALU.add))
            c(v.tensor_scalar(fx_nc[0:16, :], fx_c[0:16, :], -1.0, None, ALU.mult))
            with dve.Fori(0, KD) as i:
                c.loop(i, 2 + NS)
                for hh in range(2):
                    sel = ID[0:16, ds(i * 2 + hh, 1)]
                    c(v.tensor_scalar(fx_l[0:16, hh, :], fx_c[0:16, :], sel, None, ALU.mult))
                    v.tensor_scalar(fx_r[32:48, hh, :], fx_nc[0:16, :], sel, None, ALU.mult).then_inc(S("fx_sel"), 1)

                def output(ch):
                    qs, qn = CH[ch]
                    dve.wait_ge(S("fx_ot"), i * 5 + (ch + 1))
                    v.tensor_tensor(A[:, i, qs:qs + qn], PS[:, 3, 0:qn], fx_sg[:, qs:qs + qn], ALU.mult).then_inc(S("fx_out"), 1)

                for n in range(NS + 1):
                    if n < NS:
                        qs, qn = CH[STEPS[n][0]]
                        base = 512 * (4 + 2 * (n % 2))
                        dve.wait_ge(S("fx_s"), i * NS + (n + 1))
                        v.tensor_reduce(fx_nm[0:qn, n % 2:n % 2 + 1], PSF[0:qn, base:base + qs + qn], AXX, ALU.max,
                                        negate=True).then_inc(S("fx_mx"), 1)
                    if n >= 1:
                        m = n - 1
                        ch, hh = STEPS[m]
                        qn = CH[ch][1]
                        dve.wait_ge(S("fx_tr"), i * NS + (m + 1))
                        c(v.reciprocal(fx_rs[0:qn, m % 2:m % 2 + 1], fx_sum[0:qn, m % 2:m % 2 + 1]))
                        first = v.tensor_copy(fx_ptb[0:META, m % 2, 0, 0:qn], PS[0:META, 1, 0:qn])
                        if ch > 0:
                            first = v.tensor_copy(fx_ptb[:, m % 2, 1:ch + 1, :], PS[:, 0, 0:P * ch].rearrange("p (a b) -> p a b", a=ch))
                        first.then_inc(S("fx_pt"), 1)
                        if hh == 0 and ch > 0:
                            output(ch - 1)
                output(len(CH) - 1)
            c.end(KD)

        NC4 = T2 // P
        sd_xp, sd_y, sd_xs, sd_sz = scratch(0, 2, 516), scratch(1040, 2, T2), scratch(2064, T2), scratch(2576, T2)
        sd_xt, sd_cb = scratch(3088, NC4, P), scratch(3600, 2, NC4, T2)
        sd_r, sd_rm = scratch(7696, NC4, T2), scratch(9744, NC4, T2)
        sd_e, sd_w = scratch(11792, 2, NC4, T2), scratch(15888, NC4, T2)
        sd_bc = scratch(11792, 4, T2)
        sd_ec = sd_e.rearrange("p a b c -> p (a b c)").rearrange("p (a c) -> p a c", a=8)
        sd_rms = scratch(17936, 2, T2)
        sd_sel, sd_a, sd_tot = scratch(18960, 16), scratch(18976, 1), scratch(18977, 4)
        row_x, row_a, row_e, row_t, row_z = (A[0:48, 16 + q, 0:T2] for q in range(5))
        row_dt = A[0:48, 21, 0:T2]
        MIXC = sb("mixer_columns", [P, 4, 4, 48])
        nr_cols, dt_cols, g_cols, fl_cols = (MIXC[:, q, :, :] for q in range(4))
        ML_NEG_M = sb("mlstm_rows", [48, T2])

        def rng(d, j):
            return (P * j, T2) if d == 0 else (0, P * (j + 1))

        def mix_pre_bank(j):
            return (TILES["ssd_pre"] + j) % 2

        def ssd_pe(pe, unit, buffer_free, gemm, h):
            pe.wait_ge(tile_free, BUFS + TILES["ssd_pre"])
            for j, (u, m0, m1) in enumerate([(0, 0, 48), (1, 0, 40), (1, 64, 104), (2, 0, P), (3, 0, P), (4, 0, P), (5, 0, P)]):
                buffer_free("ssd_pre", 0, 0, j, 2)
                s = unit(UNITS["ssd_pre"], 0, 0, u) if j != 2 else s
                gemm(mix_pre_bank(j), [(s, 0, KD)], h, T2, m0, m1, last=(j != 1)).then_inc(tile_full, 1)
            pe.wait_ge(S("mx_bc"), 4)
            for g in range(2):
                for j in range(NC4):
                    q = 4 * g + j
                    if q >= 2:
                        pe.wait_ge(S("mx_cb"), q - 1)
                    nc.tensor.matmul(PS[:, 4 + q % 2, :], sd_bc[:, g, P * j:P * j + P], sd_bc[:, 2 + g, :], start=True, stop=True).then_inc(S("mx_cbp"), 1)
            for q, (name, bank, rows) in enumerate([("mx_dt", 3, 48), ("mx_r", 2, 48), ("mx_g", 6, 40), ("mx_fl", 7, 40)]):
                pe.wait_ge(S(name), 1)
                src = {"mx_dt": lambda j: row_dt[0:48, P * j:P * j + P], "mx_r": lambda j: sd_r[0:48, j, P * j:P * j + P],
                       "mx_g": lambda j: row_a[0:40, P * j:P * j + P], "mx_fl": lambda j: row_e[0:40, P * j:P * j + P]}[name]
                for j in range(NC4):
                    mm = nc.tensor.transpose(PS[:, bank, 64 * j:64 * j + rows], src(j), ID[0:rows, 0:rows])
                mm.then_inc(S("mx_turned"), 1)
            pe.wait_ge(S("mx_cols"), 4)
            for g in range(2):
                with pe.Fori(0, 2) as i:
                    for b in range(2):
                        pairs = 4 * g + b
                        for j in range(2):
                            t = 8 * g + 2 * b + j
                            buffer_free("ssd", i, 4, t, 2)
                            s = unit(UNITS["ssd"], i, 4, t)
                            gemm((TILES["ssd"] + t) % 2, [(s, 0, KD)], h, T2).then_inc(tile_full, 1)
                        pe.wait_ge(S("sd_xs"), i * 2 + (pairs + 1))
                        for j in range(NC4):
                            mm = nc.tensor.transpose(PS[:, 5, P * j:P * j + P], sd_xs[:, P * j:P * j + P], ID[:, :])
                        mm.then_inc(S("sd_xt"), 1)
                        for hh in range(2):
                            heads = 2 * pairs + hh
                            pe.wait_ge(S("sd_rm"), i * 4 + (heads + 1))
                            for q in range(8):
                                j, d = divmod(q, 2)
                                a, z = rng(d, j)
                                pe.wait_ge(S("sd_arg"), i * 32 + max(8 * heads + q - 1, 0))
                                apart(pe)
                                nc.tensor.matmul(PS[:, 2 + q % 2, 0:z - a], ONES[32 * d:32 * d + 16, :], sd_rm[32 * d:32 * d + 16, j, a:z],
                                                 start=True, stop=True).then_inc(S("sd_bcast"), 1)
                            pe.wait_ge(S("sd_w"), i * 16 + 4 * (heads + 1))
                            pe.wait_ge(S("sd_xtc"), i * 2 + (pairs + 1))
                            if hh == 0:
                                pe.wait_ge(S("sd_out"), i * 2 + pairs)
                            for j in range(NC4):
                                mm = nc.tensor.matmul(PS[64 * hh:64 * hh + 64, 4, :], sd_xt[:, j, 64 * hh:64 * hh + 64], sd_w[:, j, :],
                                                      start=(j == 0), stop=(j == NC4 - 1))
                            mm.then_inc(S("sd_y"), 1)
            for g in range(2):
                for k in range(4):
                    pe.wait_ge(S("sd_sq"), 4 * g + k + 1)
                    mm = nc.tensor.matmul(PS[:, 6 + g, :], MEANW[:, 1, :], sd_ec[:, 4 * g + k, :], start=(k == 0), stop=(k == 3))
                mm.then_inc(S("sd_ms"), 1)

        def ssd_act(act, c, full):
            a = nc.scalar
            full("ssd_pre", 0, 0, 0)
            a.activation(row_x, PS[0:48, mix_pre_bank(0), :], ACT.Identity, bias=col("dt_bias", 0, 48)).then_inc(tile_free, 1)
            c(a.activation(sd_a[0:48, :], col("a_log", 0, 48), ACT.Exp))
            act.wait_ge(S("mx_dtabs"), 1)
            a.activation(row_e, row_a, ACT.Exp, scale=-1.0).then_inc(S("mx_dtexp"), 1)
            act.wait_ge(S("mx_dt"), 1)
            full("ssd_pre", 0, 0, 1)
            a.activation(row_t[0:40, :], PS[0:40, mix_pre_bank(1), :], ACT.Identity, bias=col("ig_bias", 0, 40)).then_inc(tile_free, 1)
            full("ssd_pre", 0, 0, 2)
            a.activation(row_x[0:40, :], PS[0:40, mix_pre_bank(2), :], ACT.Identity, bias=col("fg_bias", 0, 40)).then_inc(tile_free, 1)
            act.wait_ge(S("mx_lfabs"), 1)
            c(a.activation(row_e[0:40, :], row_a[0:40, :], ACT.Exp, scale=-1.0))
            a.activation(row_a[0:40, :], row_e[0:40, :], ACT.Ln, bias=SMALL[0:40, 182:183]).then_inc(S("mx_lfln"), 1)
            act.wait_ge(S("mx_fm"), 1)
            a.activation(row_e[0:40, :], row_z[0:40, :], ACT.Exp, scale=-1.0).then_inc(S("mx_fl"), 1)
            act.wait_ge(S("mx_pad"), 1)
            for q in range(4):
                full("ssd_pre", 0, 0, 3 + q)
                if q >= 2:
                    act.wait_ge(S("mx_conv"), q - 1)
                conv_first(act, c, q % 2, mix_pre_bank(3 + q), COLS["ab_conv"] + 6 * (8 + q), "mx_tap", BUFS + TILES["ssd_pre"] + 4 + q)
                if q >= 1:
                    act.wait_ge(S("mx_conv"), q)
                    a.activation(sd_bc[:, q - 1, :], sd_y[:, (q - 1) % 2, :], ACT.Silu).then_inc(S("mx_bc"), 1)
            act.wait_ge(S("mx_conv"), 4)
            a.activation(sd_bc[:, 3, :], sd_y[:, 1, :], ACT.Silu).then_inc(S("mx_bc"), 1)
            for q in range(8):
                act.wait_ge(S("mx_cbp"), q + 1)
                a.activation(sd_cb[:, q // 4, q % 4, :], PS[:, 4 + q % 2, :], ACT.Copy).then_inc(S("mx_cb"), 1)
            for q, (dst, bank, rows, scale) in enumerate([(dt_cols, 3, 48, 1.0), (nr_cols, 2, 48, -1.0), (g_cols, 6, 40, 1.0), (fl_cols, 7, 40, 1.0)]):
                act.wait_ge(S("mx_turned"), q + 1)
                a.activation(dst[:, :, 0:rows], PS[:, bank, 0:256].rearrange("p (j c) -> p j c", j=4)[:, :, 0:rows], ACT.Copy,
                             scale=scale).then_inc(S("mx_cols"), 1)
            for g in range(2):
                with act.Fori(0, 2) as i:
                    for b in range(2):
                        pairs = 4 * g + b
                        t = 8 * g + 2 * b
                        full("ssd", i, 4, t)
                        act.wait_ge(S("sd_out"), i * 2 + pairs)
                        conv_first(act, c, 0, (TILES["ssd"] + t) % 2, i * 12 + (COLS["ab_conv"] + 6 * pairs), "sd_tap", i * 4 + (BUFS + TILES["ssd"] + t + 1))
                        full("ssd", i, 4, t + 1)
                        a.activation(sd_sz, PS[:, (TILES["ssd"] + t + 1) % 2, :], ACT.Silu).then_inc(tile_free, 1)
                        act.wait_ge(S("sd_conv"), i * 2 + (pairs + 1))
                        a.activation(sd_xs, sd_y[:, 0, :], ACT.Silu).then_inc(S("sd_xs"), 1)
                        act.wait_ge(S("sd_xt"), i * 2 + (pairs + 1))
                        a.activation(sd_xt, PS[:, 5, :].rearrange("p (j c) -> p j c", j=4), ACT.Copy).then_inc(S("sd_xtc"), 1)
                        for hh in range(2):
                            heads = 2 * pairs + hh
                            for q in range(8):
                                j, d = divmod(q, 2)
                                lo, hi = rng(d, j)
                                act.wait_ge(S("sd_arg"), i * 32 + (8 * heads + q + 1))
                                a.activation(sd_e[:, d, j, lo:hi], sd_e[:, d, j, lo:hi], ACT.Exp).then_inc(S("sd_exp"), 1)
            act.wait_ge(S("sd_out"), 8)
            for k in range(8):
                a.activation(sd_ec[:, k, :], A[:, k, 0:T2], ACT.Square).then_inc(S("sd_sq"), 1)
            for g in range(2):
                act.wait_ge(S("sd_ms"), g + 1)
                a.activation(sd_rms[:, g, :], PS[:, 6 + g, :], ACT.Sqrt, bias=SMALL[:, 181:182]).then_inc(S("sd_std"), 1)

        def conv_first(act, c, b, bank, w0, signal, freed):
            nc.scalar.activation(sd_xp[:, b, 2:2 + T2], PS[:, bank, :], ACT.Copy).then_inc(tile_free, 1)
            act.wait_ge(tile_free, freed)
            w = lambda k: PAR[:, w0 + k:w0 + k + 1] if isinstance(w0, int) else PAR[:, ds(w0 + k, 1)]
            nc.scalar.activation(sd_y[:, b, :], sd_xp[:, b, 0:T2], ACT.Identity, bias=w(5), scale=w(0)).then_inc(S(signal), 1)

        def conv_rest(dve, c, b, w0, signal):
            w = lambda k: PAR[:, w0 + k:w0 + k + 1] if isinstance(w0, int) else PAR[:, ds(w0 + k, 1)]
            for k in range(1, 5):
                ins = nc.vector.scalar_tensor_tensor(out=sd_y[:, b, :], in0=sd_xp[:, b, k:k + T2], scalar=w(k), in1=sd_y[:, b, :],
                                                     op0=ALU.mult, op1=ALU.add)
                if k < 4:
                    c(ins)
            ins.then_inc(S(signal), 1)

        def ssd_dve(dve, c, log1p_of_exp):
            v = nc.vector
            c(v.memset(NORM_MU[:, :], 1.0))
            c(v.memset(sd_r[0:48, :, :], 0.0))
            c(v.memset(sd_xp[:, :, 0:2], 0.0))
            v.memset(sd_xp[:, :, 2 + T2:4 + T2], 0.0).then_inc(S("mx_pad"), 1)
            dve.wait_ge(consts_ready, 1)
            c(v.tensor_tensor(sd_sel[0:48, :], ID[0:48, 0:16], ID[0:48, 32:48], ALU.add))
            dve.wait_ge(tile_free, BUFS + TILES["ssd_pre"] + 1)
            v.scalar_tensor_tensor(out=row_a, in0=row_x, scalar=-1.0, in1=row_x, op0=ALU.mult, op1=ALU.max).then_inc(S("mx_dtabs"), 1)
            dve.wait_ge(S("mx_dtexp"), 1)
            log1p_of_exp(row_a, row_e, row_z, row_t, row_dt)
            v.scalar_tensor_tensor(out=row_dt, in0=row_x, scalar=0.0, in1=row_dt, op0=ALU.max, op1=ALU.add).then_inc(S("mx_dt"), 1)
            dve.wait_ge(S("mx_dt"), 1)
            row_la = sd_w[0:48, 0, :]
            c(v.tensor_scalar(row_la, row_dt, sd_a[0:48, :], -1.0, ALU.mult, ALU.mult))
            one = lambda r0, n: NORM_MU[r0:r0 + 16, 0:n]
            for j in range(NC4):
                lo, hi = P * j, P * j + P
                for r0, rev in ((0, 1), (32, -1)):
                    r = slice(r0, r0 + 16)
                    own, la = sd_r[r, j, lo:hi][:, ::rev], row_la[r, lo:hi][:, ::rev]
                    c(v.tensor_tensor_scan(own, one(r0, P), la, 0.0, ALU.mult, ALU.add))
                    last = hi - 1 if rev == 1 else lo
                    c(v.tensor_copy(sd_tot[r, j:j + 1], sd_r[r, j, last:last + 1]))
                    c(v.tensor_scalar(sd_r[r, j, lo:hi], sd_r[r, j, lo:hi], sd_tot[r, j:j + 1], None, ALU.subtract))
                    a, z = (hi, T2) if rev == 1 else (0, lo)
                    if z > a:
                        c(v.tensor_tensor_scan(sd_r[r, j, a:z][:, ::rev], one(r0, z - a), row_la[r, a:z][:, ::rev], 0.0, ALU.mult, ALU.add))
            v.memset(sd_tot[0:48, 0:1], 0.0).then_inc(S("mx_r"), 1)
            dve.wait_ge(tile_free, BUFS + TILES["ssd_pre"] + 3)
            x, ab, f, ig, m = row_x[0:40, :], row_a[0:40, :], row_e, row_t[0:40, :], row_z[0:40, :]
            v.scalar_tensor_tensor(out=ab, in0=x, scalar=-1.0, in1=x, op0=ALU.mult, op1=ALU.max).then_inc(S("mx_lfabs"), 1)
            dve.wait_ge(S("mx_lfln"), 1)
            c(v.scalar_tensor_tensor(out=x, in0=x, scalar=0.0, in1=ab, op0=ALU.min, op1=ALU.subtract))
            c(v.memset(row_e[0:40, :], 0.0))
            c(v.memset(row_z[0:40, :], 0.0))
            for r0, rev in ((0, 1), (32, -1)):
                r = slice(r0, r0 + 8)
                c(v.tensor_tensor_scan(row_e[r, ::rev], NORM_MU[r, 0:T2], row_x[r, ::rev], 0.0, ALU.mult, ALU.add))
            v.tensor_tensor(ab, ig, row_e[0:40, :], ALU.subtract).then_inc(S("mx_g"), 1)
            dve.wait_ge(S("mx_g"), 1)
            for r0, rev in ((0, 1), (32, -1)):
                r = slice(r0, r0 + 8)
                c(v.tensor_tensor_scan(row_z[r, ::rev], row_a[r, ::rev], row_a[r, ::rev], 0.0, ALU.max, ALU.max))
            c(v.tensor_scalar(ML_NEG_M[0:40, :], m, -1.0, None, ALU.mult))
            v.tensor_tensor(m, m, row_e[0:40, :], ALU.add).then_inc(S("mx_fm"), 1)
            for q in range(4):
                dve.wait_ge(S("mx_tap"), q + 1)
                conv_rest(dve, c, q % 2, COLS["ab_conv"] + 6 * (8 + q), "mx_conv")
            dve.wait_ge(S("mx_cols"), 4)
            for g in range(2):
                with dve.Fori(0, 2) as i:
                    c.loop(i, 2 * (3 + 2 * (3 + 3 + 2 * 4) + 1))
                    for b in range(2):
                        pairs = 4 * g + b
                        dve.wait_ge(S("sd_tap"), i * 2 + (pairs + 1))
                        conv_rest(dve, c, 0, i * 12 + (COLS["ab_conv"] + 6 * pairs), "sd_conv")
                        for hh in range(2):
                            heads = 2 * pairs + hh
                            for q in range(8):
                                j, d = divmod(q, 2)
                                lo, hi = rng(d, j)
                                dve.wait_ge(S("sd_bcast"), i * 32 + (8 * heads + q + 1))
                                v.tensor_scalar(sd_e[:, d, j, lo:hi], PS[:, 2 + q % 2, 0:hi - lo], nr_cols[:, j, ds(i * 4 + (heads + 32 * d), 1)], 0.0,
                                                ALU.add, ALU.min).then_inc(S("sd_arg"), 1)
                            dve.wait_ge(S("sd_y"), i * 4 + heads)
                            for j in range(NC4):
                                lo, hi = P * j, P * j + P
                                dve.wait_ge(S("sd_mask"), i * 32 + (8 * heads + 2 * j + 2))
                                dt = [dt_cols[:, j, ds(i * 4 + (heads + 32 * d), 1)] for d in range(2)]
                                cb = sd_cb[:, g, j, :]
                                if j < NC4 - 1:
                                    c(v.scalar_tensor_tensor(out=sd_w[:, j, hi:T2], in0=sd_e[:, 0, j, hi:T2], scalar=dt[0], in1=cb[:, hi:T2],
                                                             op0=ALU.mult, op1=ALU.mult))
                                if j > 0:
                                    c(v.scalar_tensor_tensor(out=sd_w[:, j, 0:lo], in0=sd_e[:, 1, j, 0:lo], scalar=dt[1], in1=cb[:, 0:lo],
                                                             op0=ALU.mult, op1=ALU.mult))
                                c(v.tensor_scalar(sd_e[:, 0, j, lo:hi], sd_e[:, 0, j, lo:hi], dt[0], None, ALU.mult))
                                c(v.scalar_tensor_tensor(out=sd_e[:, 0, j, lo:hi], in0=sd_e[:, 1, j, lo:hi], scalar=dt[1], in1=sd_e[:, 0, j, lo:hi],
                                                         op0=ALU.mult, op1=ALU.add))
                                v.tensor_tensor(sd_w[:, j, lo:hi], sd_e[:, 0, j, lo:hi], cb[:, lo:hi], ALU.mult).then_inc(S("sd_w"), 1)
                        dve.wait_ge(S("sd_y"), i * 4 + (2 * pairs + 2))
                        c(v.scalar_tensor_tensor(out=sd_xs, in0=sd_xs, scalar=col("d_skip", i * 2 + pairs), in1=PS[:, 4, :], op0=ALU.mult, op1=ALU.add))
                        v.tensor_tensor(A[:, i * 2 + pairs, 0:T2], sd_xs, sd_sz, ALU.mult).then_inc(S("sd_out"), 1)
                c.end(2)
            for g in range(2):
                dve.wait_ge(S("sd_std"), g + 1)
                c(v.reciprocal(sd_rms[:, g, :], sd_rms[:, g, :]))
                for k in range(4 * g, 4 * g + 4):
                    v.scalar_tensor_tensor(out=A[:, k, 0:T2], in0=A[:, k, 0:T2], scalar=col("ssd_norm", k), in1=sd_rms[:, g, :],
                                           op0=ALU.mult, op1=ALU.mult).then_inc(S("sd_norm"), 1)

        def ssd_pool(pool, c):
            g_ = nc.gpsimd
            flat = lambda ap: ap.rearrange("p a b -> p (a b)")
            pool.wait_ge(S("mx_cols"), 4)
            for g in range(2):
                with pool.Fori(0, 2) as i:
                    for b in range(2):
                        for hh in range(2):
                            heads = 8 * g + 2 * b + hh
                            pool.wait_ge(S("sd_bcast"), i * 32 + 8 * heads)
                            g_.tensor_tensor(flat(sd_rm[0:48, :, :]), flat(sd_r[0:48, :, :]), sd_sel[0:48, ds(i * 4 + heads, 1)].to_broadcast([48, NC4 * T2]), ALU.mult).then_inc(S("sd_rm"), 1)
                            for q in range(8):
                                j, d = divmod(q, 2)
                                pool.wait_ge(S("sd_exp"), i * 32 + (8 * heads + q + 1))
                                own = sd_e[:, d, j, P * j:P * j + P]
                                g_.tensor_tensor(own, own, (LOWER, UPPER)[d][:, :], ALU.mult).then_inc(S("sd_mask"), 1)

        ml_q, ml_k = scratch(0, T2), scratch(512, T2)
        ml_v, ml_o = scratch(1024, NC4, 130), scratch(1544, NC4, P)
        ml_m, ml_d, ml_h = scratch(2056, T2), scratch(2568, 2, NC4, T2), scratch(6664, NC4, P)
        ml_nd, ml_ad, ml_ss, ml_sq = scratch(7176, 2), scratch(7178, 2), scratch(7180, 4), scratch(7184, P)

        def mlstm_pe(pe, unit, buffer_free, gemm, gemm_tokens, h):
            with pe.Fori(0, 8) as i:
                for j in range(4):
                    buffer_free("mlstm", i, 4, j, 2)
                    s = unit(UNITS["mlstm"], i, 4, j)
                    bank = (TILES["mlstm"] + j) % 2
                    if j < 2:
                        gemm(bank, [(s, 0, KD)], h, T2).then_inc(tile_full, 1)
                    else:
                        gemm_tokens(bank, s, h, [(0, P * q, P * q, P) for q in range(NC4)]).then_inc(tile_full, 1)
                pe.wait_ge(tile_free, i * 4 + (BUFS + TILES["mlstm"] + 4))
                pe.wait_ge(S("ml_rm"), i + 1)
                pe.wait_ge(S("ml_out"), i)
                apart(pe)
                for d in range(2):
                    mm = nc.tensor.matmul(PS[:, 2 + d, :], ONES[32 * d:32 * d + 8, :], ml_m[32 * d:32 * d + 8, :], start=True, stop=True)
                mm.then_inc(S("ml_bcast"), 1)
                for j in range(NC4):
                    if j >= 2:
                        pe.wait_ge(S("ml_w"), i * 8 + 2 * (j - 1))
                    nc.tensor.matmul(PS[:, 4 + j % 2, :], ml_k[:, P * j:P * j + P], ml_q, start=True, stop=True).then_inc(S("ml_s"), 1)
                pe.wait_ge(S("ml_w"), i * 8 + 8)
                for t in range(NC4):
                    if t >= 2:
                        pe.wait_ge(S("ml_h"), i * 4 + (t - 1))
                    for d in range(2):
                        js = range(0, t + 1) if d == 0 else range(t, NC4)
                        for j in js:
                            mm = nc.tensor.matmul(PS[:, 6 + t % 2, 256 * d:256 * d + 129], ml_d[:, d, j, P * t:P * t + P], ml_v[:, j, 0:129],
                                                  start=(j == js[0]), stop=(j == js[-1]))
                    mm.then_inc(S("ml_num"), 1)
                pe.wait_ge(S("ml_hn"), i + 1)
                for t in range(NC4):
                    mm = nc.tensor.transpose(PS[:, 2, P * t:P * t + P], ml_h[:, t, :], ID[:, :])
                mm.then_inc(S("ml_ot"), 1)
            pe.wait_ge(S("ml_out"), 8)
            pe.wait_ge(S("sd_norm"), 8)

        def mlstm_act(act, c, full):
            a = nc.scalar
            act.wait_ge(S("sd_norm"), 8)
            act.wait_ge(S("ml_ones"), 1)
            with act.Fori(0, 8) as i:
                bank = lambda j: (TILES["mlstm"] + j) % 2
                full("mlstm", i, 4, 0)
                a.activation(ml_q, PS[:, bank(0), :], ACT.Copy).then_inc(tile_free, 1)
                full("mlstm", i, 4, 1)
                a.activation(ml_k, PS[:, bank(1), :], ACT.Copy, scale=float(P) ** -0.5).then_inc(tile_free, 1)
                full("mlstm", i, 4, 2)
                a.activation(ml_v[:, :, 0:P], PS[:, bank(2), :].rearrange("p (j c) -> p j c", j=4), ACT.Copy).then_inc(tile_free, 1)
                full("mlstm", i, 4, 3)
                a.activation(ml_o, PS[:, bank(3), :].rearrange("p (j c) -> p j c", j=4), ACT.Sigmoid).then_inc(tile_free, 1)
                for q in range(8):
                    j, d = divmod(q, 2)
                    lo, hi = rng(d, j)
                    act.wait_ge(S("ml_arg"), i * 8 + (q + 1))
                    a.activation(ml_d[:, d, j, lo:hi], ml_d[:, d, j, lo:hi], ACT.Exp).then_inc(S("ml_exp"), 1)
                for t in range(NC4):
                    act.wait_ge(S("ml_h"), i * 4 + (t + 1))
                    a.activation(ml_sq, ml_h[:, t, :], ACT.Square, accum_out=ml_ss[:, t:t + 1]).then_inc(S("ml_sum"), 1)
                    act.wait_ge(S("ml_sum"), i * 4 + (t + 1))
                a.activation(ml_ss, ml_ss, ACT.Sqrt, bias=SMALL[:, 181:182], scale=1.0 / P).then_inc(S("ml_std"), 1)
                act.wait_ge(S("ml_ot"), i + 1)
                a.activation(A[:, i + 8, 0:T2], PS[:, 2, :], ACT.Copy, scale=col("mlstm_norm", i)).then_inc(S("ml_out"), 1)

        def mlstm_dve(dve, c):
            v = nc.vector
            v.memset(ml_v[:, :, P:P + 1], 1.0).then_inc(S("ml_ones"), 1)
            with dve.Fori(0, 8) as i:
                c.loop(i, 4 * (1 + 2 + 1 + 2) + 1 + 3)
                for q in range(8):
                    j, d = divmod(q, 2)
                    lo, hi = rng(d, j)
                    if q == 0:
                        dve.wait_ge(S("ml_bcast"), i + 1)
                    v.tensor_scalar(ml_d[:, d, j, lo:hi], PS[:, 2 + d, lo:hi], g_cols[:, j, ds(i + 32 * d, 1)], 0.0,
                                    ALU.add, ALU.min).then_inc(S("ml_arg"), 1)
                for q in range(8):
                    j, d = divmod(q, 2)
                    lo, hi = rng(d, j)
                    dve.wait_ge(S("ml_mask"), i * 8 + (q + 1))
                    dve.wait_ge(S("ml_s"), i * 4 + (j + 1))
                    v.tensor_tensor(ml_d[:, d, j, lo:hi], ml_d[:, d, j, lo:hi], PS[:, 4 + j % 2, lo:hi], ALU.mult).then_inc(S("ml_w"), 1)
                for t in range(NC4):
                    bank = 6 + t % 2
                    dve.wait_ge(S("ml_num"), i * 4 + (t + 1))
                    den = [PS[:, bank, 256 * d + P:256 * d + P + 1] for d in range(2)]
                    c(v.tensor_scalar(ml_nd, PS[:, bank, P:P + 257:256], -1.0, None, ALU.mult))
                    for d in range(2):
                        c(v.scalar_tensor_tensor(out=ml_ad[:, d:d + 1], in0=ml_nd[:, d:d + 1], scalar=fl_cols[:, t, ds(i + 32 * d, 1)],
                                                 in1=den[d], op0=ALU.max, op1=ALU.max))
                    c(v.reciprocal(ml_ad, ml_ad))
                    c(v.tensor_scalar(ml_h[:, t, :], PS[:, bank, 0:P], ml_ad[:, 0:1], None, ALU.mult))
                    c(v.scalar_tensor_tensor(out=ml_h[:, t, :], in0=PS[:, bank, 256:256 + P], scalar=ml_ad[:, 1:2], in1=ml_h[:, t, :],
                                             op0=ALU.mult, op1=ALU.add))
                    v.tensor_tensor(ml_h[:, t, :], ml_h[:, t, :], ml_o[:, t, :], ALU.mult).then_inc(S("ml_h"), 1)
                dve.wait_ge(S("ml_std"), i + 1)
                c(v.reciprocal(ml_ss, ml_ss))
                for t in range(NC4):
                    ins = v.tensor_scalar(ml_h[:, t, :], ml_h[:, t, :], ml_ss[:, t:t + 1], None, ALU.mult)
                    if t < NC4 - 1:
                        c(ins)
                ins.then_inc(S("ml_hn"), 1)
            c.end(8)

        def mlstm_pool(pool, c):
            pool.wait_ge(S("sd_norm"), 8)
            with pool.Fori(0, 8) as i:
                pool.wait_ge(S("ml_bcast"), i)
                nc.gpsimd.tensor_tensor(ml_m[0:40, :], ML_NEG_M[0:40, :], sd_sel[0:40, ds(i, 1)].to_broadcast([40, T2]), ALU.mult).then_inc(S("ml_rm"), 1)
                for q in range(8):
                    j, d = divmod(q, 2)
                    pool.wait_ge(S("ml_exp"), i * 8 + (q + 1))
                    own = ml_d[:, d, j, P * j:P * j + P]
                    nc.gpsimd.tensor_tensor(own, own, (LOWER, UPPER)[d][:, :], ALU.mult).then_inc(S("ml_mask"), 1)

        GC = 64
        NG = T2 // GC
        gl_q, gl_k, gl_v, gl_sr = scratch(0, T2), scratch(512, T2), scratch(1024, NC4, 256), scratch(2048, 2, T2)
        gl_x, gl_ab, gl_bc = scratch(3072, 2, T2), scratch(4096, 2, T2), scratch(5120, 2, T2)
        gl_qi, gl_ki, gl_ke = scratch(6144, 2, T2), scratch(7168, 2, T2), scratch(8192, 2, T2)
        gl_kt, gl_dec, gl_st = scratch(9216, 2, NC4, P), scratch(10240, 2, NG), scratch(10256, 2, NG, 256)
        gl_att, gl_o, gl_sq, gl_rn = scratch(14352, 2, NC4, GC), scratch(14864, 2, T2), scratch(15888, 2, T2), scratch(16912, T2)
        gl_reset, gl_lr, gl_ws = scratch(17424, 2, T2), scratch(18448, T2), scratch(19472, P)
        gl_w2 = sb("gate_w2_sb", [48, T2])
        gl_mask = scratch(19600, 2, GC)
        GSTEPS = [[(0, q, q + 1) for q in range(NG - 1)], [(1, q, q - 1) for q in range(NG - 1, 0, -1)]]
        GSTEPS = [s for pair in zip(*GSTEPS) for s in pair]
        NST = len(GSTEPS)

        def gl_rows(ch):
            return slice(GC * (ch % 2), GC * (ch % 2) + GC)

        def gla_pe(pe, unit, buffer_free, gemm, gemm_tokens, h):
            pe.wait_ge(tile_free, BUFS + TILES["gla_pre"])
            s = unit(UNITS["gla_pre"], 0, 0, 0)
            gemm(TILES["gla_pre"] % 2, [(s, 0, KD)], h, T2, 0, 48).then_inc(tile_full, 1)
            with pe.Fori(0, 2) as i:
                for b in range(2):
                    for j in range(6):
                        buffer_free("gla", i, 12, 6 * b + j, 2)
                        s = unit(UNITS["gla"], i, 12, 6 * b + j)
                        bank = (TILES["gla"] + j) % 2
                        if j in (2, 3):
                            gemm_tokens(bank, s, h, [(0, P * q, P * q, P) for q in range(NC4)]).then_inc(tile_full, 1)
                        else:
                            gemm(bank, [(s, 0, KD)], h, T2).then_inc(tile_full, 1)
                    pe.wait_ge(S("gl_out"), i * 4 + 2 * b)
                    pe.wait_ge(S("gl_ws"), i * 2 + (b + 1))
                    apart(pe)
                    for d in range(2):
                        mm = nc.tensor.matmul(PS[:, 2 + d, :], gl_ws[32 * d:32 * d + 16, :], gl_lr[32 * d:32 * d + 16, :], start=True, stop=True)
                    mm.then_inc(S("gl_lg"), 1)
                    pe.wait_ge(S("gl_in"), i * 4 + (2 * b + 2))
                    for d in range(2):
                        for j in range(NC4):
                            mm = nc.tensor.transpose(PS[:, 4 + d, P * j:P * j + P], gl_ke[:, d, P * j:P * j + P], ID[:, :])
                        mm.then_inc(S("gl_kp"), 1)
                    for d in range(2):
                        for ch in range(NG):
                            mm = nc.tensor.matmul(PS[gl_rows(ch), 6 + d, GC * (ch // 2):GC * (ch // 2) + GC], gl_ki[:, d, GC * ch:GC * ch + GC],
                                                  gl_qi[:, d, GC * ch:GC * ch + GC], start=True, stop=True)
                        mm.then_inc(S("gl_att"), 1)
                    pe.wait_ge(S("gl_kt"), i * 4 + (2 * b + 2))
                    pe.wait_ge(tile_free, i * 12 + (BUFS + TILES["gla"] + 6 * b + 6))
                    for q, (d, ch, to) in enumerate(GSTEPS):
                        if q >= 2:
                            pe.wait_ge(S("gl_st"), i * (2 * NST) + (NST * b + q - 1))
                        nc.tensor.matmul(PS[:, 2 + q % 2, 0:256], gl_kt[gl_rows(ch), d, ch // 2, :], gl_v[gl_rows(ch), ch // 2, :],
                                         start=True, stop=True).then_inc(S("gl_u"), 1)
                    pe.wait_ge(S("gl_am"), i * 4 + (2 * b + 2))
                    pe.wait_ge(S("gl_st"), i * (2 * NST) + NST * (b + 1))
                    for a in range(2):
                        for par in range(2):
                            for ch in range(par, NG, 2):
                                dst = PS[:, (4, 7)[par] + a * (1, -1)[par], GC * (ch // 2):GC * (ch // 2) + GC]
                                ds_ = [d for d in range(2) if (ch > 0 if d == 0 else ch < NG - 1)]
                                for d in range(2):
                                    nc.tensor.matmul(dst, gl_v[gl_rows(ch), ch // 2, P * a:P * a + P], gl_att[gl_rows(ch), d, ch // 2, :],
                                                     start=(d == 0), stop=False)
                                for d in ds_:
                                    mm = nc.tensor.matmul(dst, gl_st[:, d, ch, P * a:P * a + P], gl_qi[:, d, GC * ch:GC * ch + GC],
                                                          start=False, stop=(d == ds_[-1]))
                        mm.then_inc(S("gl_o"), 1)
                    for a in range(2):
                        pe.wait_ge(S("gl_sq"), i * 4 + (2 * b + a + 1))
                        mm = nc.tensor.matmul(PS[:, 2, :], MEANW[:, 2, :], gl_sq[:, a, :], start=(a == 0), stop=(a == 1))
                    mm.then_inc(S("gl_ms"), 1)
            pe.wait_ge(S("gl_out"), 8)

        def gla_act(act, c, full):
            a_ = nc.scalar
            full("gla_pre", 0, 0, 0)
            act.wait_ge(S("gl_zero"), 1)
            a_.activation(gl_lr[0:48, :], PS[0:48, TILES["gla_pre"] % 2, :], ACT.Copy).then_inc(tile_free, 1)
            with act.Fori(0, 2) as i:
                c.loop(i, 4)
                for b in range(2):
                    bank = lambda j: (TILES["gla"] + j) % 2
                    act.wait_ge(S("gl_out"), i * 4 + 2 * b)
                    full("gla", i, 12, 6 * b)
                    a_.activation(gl_q, PS[:, bank(0), :], ACT.Copy, scale=float(P) ** -0.5).then_inc(tile_free, 1)
                    full("gla", i, 12, 6 * b + 1)
                    a_.activation(gl_k, PS[:, bank(1), :], ACT.Copy).then_inc(tile_free, 1)
                    for a in range(2):
                        full("gla", i, 12, 6 * b + 2 + a)
                        a_.activation(gl_v[:, :, P * a:P * a + P], PS[:, bank(2 + a), :].rearrange("p (j c) -> p j c", j=4), ACT.Copy).then_inc(tile_free, 1)
                    for a in range(2):
                        full("gla", i, 12, 6 * b + 4 + a)
                        a_.activation(gl_sr[:, a, :], PS[:, bank(4 + a), :], ACT.Silu).then_inc(tile_free, 1)
                    act.wait_ge(S("gl_lg"), i * 2 + (b + 1))
                    for d in range(2):
                        a_.activation(gl_x[:, d, :], PS[:, 2 + d, :], ACT.Identity, bias=col("gate_b", i * 2 + (b + 4 * d))).then_inc(S("gl_lx"), 1)
                    for d in range(2):
                        act.wait_ge(S("gl_abs"), i * 4 + (2 * b + d + 1))
                        c(a_.activation(gl_ab[:, d, :], gl_ab[:, d, :], ACT.Exp, scale=-1.0))
                        a_.activation(gl_ab[:, d, :], gl_ab[:, d, :], ACT.Ln, bias=SMALL[:, 182:183]).then_inc(S("gl_ln"), 1)
                    for d in range(2):
                        act.wait_ge(S("gl_cum"), i * 4 + (2 * b + d + 1))
                        a_.activation(gl_qi[:, d, :], gl_bc[:, d, :], ACT.Exp, scale=1.0 / 16)
                        a_.activation(gl_ki[:, d, :], gl_bc[:, d, :], ACT.Exp, scale=-1.0 / 16).then_inc(S("gl_exp"), 1)
                    for d in range(2):
                        act.wait_ge(S("gl_kp"), i * 4 + (2 * b + d + 1))
                        a_.activation(gl_kt[:, d, :, :], PS[:, 4 + d, :].rearrange("p (j c) -> p j c", j=4), ACT.Copy).then_inc(S("gl_kt"), 1)
                    for a in range(2):
                        act.wait_ge(S("gl_o"), i * 4 + (2 * b + a + 1))
                        for par in range(2):
                            o = a_.activation(gl_o[:, a, :].rearrange("p (j r c) -> p r j c", j=4, r=2)[:, par],
                                              PS[:, (4, 7)[par] + a * (1, -1)[par], 0:256].rearrange("p (j c) -> p j c", j=4), ACT.Copy)
                        o.then_inc(S("gl_oc"), 1)
                        act.wait_ge(S("gl_oc"), i * 4 + (2 * b + a + 1))
                        a_.activation(gl_sq[:, a, :], gl_o[:, a, :], ACT.Square).then_inc(S("gl_sq"), 1)
                    act.wait_ge(S("gl_ms"), i * 2 + (b + 1))
                    a_.activation(gl_rn, PS[:, 2, :], ACT.Sqrt, bias=SMALL[:, 181:182]).then_inc(S("gl_std"), 1)
            c.end(2)

        def gla_dve(dve, c):
            v = nc.vector
            c(v.memset(gl_reset[:, :, :], 1.0))
            for d, at in ((0, 0), (1, GC - 1)):
                c(v.memset(gl_reset[:, d, :].rearrange("p (a b) -> p a b", b=GC)[:, :, at:at + 1], 0.0))
            for d, keep in ((0, LOWER), (1, UPPER)):
                for par in range(2):
                    r = slice(GC * par, GC * par + GC)
                    c(v.tensor_copy(gl_mask[r, d, :], keep[r, r]))
            v.memset(gl_rn, 0.0).then_inc(S("gl_zero"), 1)
            dve.wait_ge(w2_loaded, 16)
            with dve.Fori(0, 2) as i:
                c.loop(i, 2 * (2 * 1 + 2 * 3 + 1 + 2))
                for b in range(2):
                    v.tensor_copy(gl_ws[0:48, :], gl_w2[0:48, ds(i * 256 + P * b, P)]).then_inc(S("gl_ws"), 1)
                    for d in range(2):
                        dve.wait_ge(S("gl_lx"), i * 4 + (2 * b + d + 1))
                        v.scalar_tensor_tensor(out=gl_ab[:, d, :], in0=gl_x[:, d, :], scalar=-1.0, in1=gl_x[:, d, :], op0=ALU.mult,
                                               op1=ALU.max).then_inc(S("gl_abs"), 1)
                    for d in range(2):
                        dve.wait_ge(S("gl_ln"), i * 4 + (2 * b + d + 1))
                        c(v.scalar_tensor_tensor(out=gl_x[:, d, :], in0=gl_x[:, d, :], scalar=0.0, in1=gl_ab[:, d, :], op0=ALU.min, op1=ALU.subtract))
                        rev = (1, -1)[d]
                        v.tensor_tensor_scan(gl_bc[:, d, ::rev], gl_reset[:, d, ::rev], gl_x[:, d, ::rev], 0.0, ALU.mult, ALU.add).then_inc(S("gl_cum"), 1)
                    for d in range(2):
                        dve.wait_ge(S("gl_exp"), i * 4 + (2 * b + d + 1))
                        end = (GC - 1, 0)[d]
                        chunks = lambda ap: ap.rearrange("p (a b) -> p a b", b=GC)
                        c(v.tensor_copy(gl_dec[:, d, :], chunks(gl_qi[:, d, :])[:, :, end]))
                        c(v.tensor_tensor(gl_qi[:, d, :], gl_qi[:, d, :], gl_q, ALU.mult))
                        c(v.tensor_tensor(gl_ki[:, d, :], gl_ki[:, d, :], gl_k, ALU.mult))
                        v.tensor_tensor(chunks(gl_ke[:, d, :]), chunks(gl_ki[:, d, :]), gl_dec[:, d, :].rearrange("p (a b) -> p a b", b=1).to_broadcast([P, NG, GC]),
                                        ALU.mult).then_inc(S("gl_in"), 1)
                    for d in range(2):
                        dve.wait_ge(S("gl_att"), i * 4 + (2 * b + d + 1))
                        v.tensor_tensor(gl_att[:, d, :, :], PS[:, 6 + d, 0:256].rearrange("p (a b) -> p a b", b=GC),
                                        gl_mask[:, d, :].rearrange("p (a b) -> p a b", a=1).to_broadcast([P, NC4, GC]), ALU.mult).then_inc(S("gl_am"), 1)
                    for q, (d, ch, to) in enumerate(GSTEPS):
                        dve.wait_ge(S("gl_u"), i * (2 * NST) + (NST * b + q + 1))
                        u = PS[:, 2 + q % 2, 0:256]
                        if q < 2:
                            ins = v.tensor_copy(gl_st[:, d, to, :], u)
                        else:
                            dve.wait_ge(S("gl_st"), i * (2 * NST) + (NST * b + q - 1))
                            ins = v.scalar_tensor_tensor(out=gl_st[:, d, to, :], in0=gl_st[:, d, ch, :], scalar=gl_dec[:, d, ch:ch + 1], in1=u,
                                                         op0=ALU.mult, op1=ALU.add)
                        ins.then_inc(S("gl_st"), 1)
                    dve.wait_ge(S("gl_std"), i * 2 + (b + 1))
                    c(v.reciprocal(gl_rn, gl_rn))
                    for a in range(2):
                        k = i * 4 + (2 * b + a)
                        c(v.scalar_tensor_tensor(out=gl_o[:, a, :], in0=gl_o[:, a, :], scalar=col("gla_norm", k), in1=gl_rn, op0=ALU.mult, op1=ALU.mult))
                        v.tensor_tensor(A[:, k, 0:T2], gl_o[:, a, :], gl_sr[:, a, :], ALU.mult).then_inc(S("gl_out"), 1)
            c.end(2)

        @block.sync
        def _(sp):
            sp.dma_start(PAR[:, :], cols).then_inc(loaded, 16)
            sp.dma_start(X[:, :, :], x_t).then_inc(loaded, 16)
            sp.dma_start(gl_w2[:, :], gate_w2).then_inc(w2_loaded, 16)
            last = {"lru": "ffn0", "ffn0": "fox_f", "fox": "ffn1", "ffn1": "ssd_pre", "mix": "ffn2", "ffn2": "gla_pre", "gla": "ffn3"}
            if phases[-1] == "lru":
                n_units = UNITS["ffn0"]
            else:
                n_units = UNITS[last[phases[-1]]] if phases[-1] in last else N_UNITS
            full, rest = divmod(n_units, SLOTS)
            for b in range(SLOTS):
                sp.dma_start(W[:, b, :, :], units[b]).then_inc(w_full[b], 16)
            with sp.Fori(1, full) as i:
                for b in range(SLOTS):
                    sp.wait_ge(w_started, i * SLOTS + (b + 2 - SLOTS))
                    sp.dma_start(W[:, b, :, :], units[i * SLOTS + b]).then_inc(w_full[b], 16)
            for b in range(rest):
                sp.wait_ge(w_started, (full - 1) * SLOTS + b + 2)
                sp.dma_start(W[:, b, :, :], units[full * SLOTS + b]).then_inc(w_full[b], 16)
            sp.wait_ge(*when(phases[-1], "x", KD))
            sp.dma_start(out, X[:, :, META:T1]).then_inc(out_done, 16)
            sp.wait_ge(out_done, 16)

        @block.tensor
        def _(pe):
            def unit(base, i, per, j):
                u = base + j
                slot = u % SLOTS
                if isinstance(i, int):
                    pe.wait_ge(w_full[slot], 16 * ((u + i * per) // SLOTS + 1))
                else:
                    pe.wait_ge(w_full[slot], i * (16 * (per // SLOTS)) + 16 * (u // SLOTS + 1))
                return slot

            def buffer_free(name, i, per, j, bufs):
                pe.wait_ge(tile_free, i * per + (TILES[name] + j + 1 + BUFS - bufs))

            def gemm(bank, slots, rhs, T, m0=0, m1=P, last=True):
                ks = [(s, q, k) for s, first, count in slots for q, k in enumerate(range(first, first + count))]
                for b, t, n in parts(T):
                    for x, (s, q, k) in enumerate(ks):
                        mm = nc.tensor.matmul(PS[0:m1 - m0, bank + b, 0:n], W[:, s, q, m0:m1], rhs(k)[:, t:t + n],
                                              start=(x == 0), stop=(x == len(ks) - 1))
                        if last and q == 0 and (b, t, n) == parts(T)[-1]:
                            mm.then_inc(w_started, 1)
                return mm

            def gemm_tokens(bank, slot, h, chunks):
                for b, c, t, rows in chunks:
                    for k in range(KD):
                        mm = nc.tensor.matmul(PS[0:rows, bank + b, c:c + P], h(k)[:, t:t + rows], W[:, slot, k, :],
                                              start=(k == 0), stop=(k == KD - 1))
                        if k == 0 and (b, c, t, rows) == chunks[-1]:
                            mm.then_inc(w_started, 1)
                return mm

            def x1(k):
                return X[:, k, :]

            def h2(k):
                return Z[:, k, 0:T2]

            def bank4(n):
                return 2 * (n % 4)

            def projection(name, K, T, per, trips):
                us = [(k, min(KD, K - k)) for k in range(0, K, KD)]
                pe.wait_ge(tile_free, BUFS + TILES[name])
                with pe.Fori(0, trips) as i:
                    for j in range(per):
                        buffer_free(name, i, per, j, min(per, BUFS))
                        slots = [(unit(UNITS[name], i, per * len(us), j * len(us) + q), k, n) for q, (k, n) in enumerate(us)]
                        mm = gemm(bank4(TILES[name] + j), slots, lambda k: A[:, k, 0:T], T)
                        mm.then_inc(tile_full, 1)

            def norm(name, T, src, centred, group=None):
                if centred:
                    pe.wait_ge(tile_free, BUFS + {"lru": TILES["ffn0"], "ffn0": TILES["fox_f"], "fox": TILES["ffn1"], "ffn1": TILES["ssd_pre"]}[name])
                    for k in range(KD):
                        pe.wait_ge(*when(name, "z", k + 1))
                        for b, t, n in parts(T):
                            mm = nc.tensor.matmul(PS[:, b, 0:n], MEANW[:, 0, :], src(k)[:, t:t + n], start=(k == 0), stop=(k == KD - 1))
                    mm.then_inc(shared("mean", name), 1)
                for k in range(KD):
                    pe.wait_ge(*when(name, "sq", k + 1))
                    for b, t, n in parts(T):
                        mm = nc.tensor.matmul(PS[:, 2 + b, 0:n], MEANW[:, 0, :], A[:, k, t:t + n], start=(k == 0), stop=(k == KD - 1))
                mm.then_inc(shared("var", name), 1)

            def ffn(n, T, h):
                name = f"ffn{n}"
                pe.wait_ge(tile_free, BUFS + TILES[name])
                with pe.Fori(0, NF // 2) as i:
                    for j in range(4):
                        buffer_free(name, i, 4, j, 4)
                        s = unit(UNITS[name], i, 4, j)
                        gemm(bank4(TILES[name] + j), [(s, 0, KD)], h, T).then_inc(tile_full, 1)
                pe.wait_ge(*when(name, "act", NF))
                with pe.Fori(0, 2) as i:
                    for j in range(4):
                        pe.wait_ge(tile_free, i * 4 + (TILES[name] + 2 * NF + j + 1))
                        slots = [(unit(UNITS[name] + 2 * NF, i, 12, 3 * j + q), KD * q, min(KD, NF - KD * q)) for q in range(3)]
                        gemm(bank4(TILES[name] + 2 * NF + j), slots, lambda k: A[:, k, 0:T], T).then_inc(tile_full, 1)

            pe.wait_ge(consts_ready, 1)
            pe.wait_ge(loaded, 32)

            rc = scratch(1600, 3, T1)
            with pe.Fori(0, 4) as i:
                def lru_tile(j, slot, fn):
                    buffer_free("lru", i, 12, j, 4)
                    fn(bank4(j)).then_inc(tile_full, 1)
                for j in range(3):
                    s = unit(0, i, 8, j)
                    lru_tile(j, s, lambda bank: gemm(bank, [(s, 0, KD)], x1, T1))
                pe.wait_ge(S("lru_conv"), i * 3 + 3)
                for g in range(2):
                    s = unit(0, i, 8, 3 + g)
                    for o in range(3):
                        pieces = [(q, k) for q, (oo, k) in enumerate(LRU_PIECES) if oo == o]

                        def blocks(bank):
                            for b, t, n in parts(T1):
                                for x, (q, k) in enumerate(pieces):
                                    mm = nc.tensor.matmul(PS[:, bank + b, 0:n], W[:, s, q, :], rc[:, k, t:t + n],
                                                          start=(x == 0), stop=(x == len(pieces) - 1))
                                    if o == 2 and b == 1 and x == 0:
                                        mm.then_inc(w_started, 1)
                            return mm
                        lru_tile(3 + 3 * g + o, s, blocks)
                for j in range(3):
                    s = unit(0, i, 8, 5 + j)
                    lru_tile(9 + j, s, lambda bank: gemm(bank, [(s, 0, KD)], x1, T1))
            pe.wait_ge(S("lru_act"), 12)
            projection("lru_out", 12, T1, 2, 4)
            norm("lru", T1, x_src := (lambda k: Z[:, k, :]), True)
            if "ffn0" in phases:
                pe.wait_ge(*when("lru", "x", KD))
                ffn(0, T1, x1)
                norm("ffn0", T1, x_src, True)
            if "fox" in phases:
                pe.wait_ge(*when("ffn0", "x", KD))
                fox_pe(pe, unit, buffer_free, gemm, gemm_tokens, x1)
                projection("fox_out", 8, T1, 4, 2)
                norm("fox", T1, x_src, True)
            if "ffn1" in phases:
                pe.wait_ge(*when("fox", "x", KD))
                ffn(1, T1, x1)
                norm("ffn1", T1, x_src, True)
            h_src = lambda k: Z[:, k, 0:T2]
            if "mix" in phases:
                norm("mixin", T2, None, False)
                pe.wait_ge(*when("mixin", "x", KD))
                ssd_pe(pe, unit, buffer_free, gemm, h2)
                mlstm_pe(pe, unit, buffer_free, gemm, gemm_tokens, h2)
                projection("mix_out", 16, T2, 2, 4)
                norm("mix", T2, None, False)
            if "ffn2" in phases:
                norm("ffn2in", T2, None, False)
                pe.wait_ge(*when("ffn2in", "x", KD))
                ffn(2, T2, h2)
                norm("ffn2", T2, None, False)
            if "gla" in phases:
                norm("glain", T2, None, False)
                pe.wait_ge(*when("glain", "x", KD))
                gla_pe(pe, unit, buffer_free, gemm, gemm_tokens, h2)
                projection("gla_out", 8, T2, 4, 2)
                norm("gla", T2, None, False)
            if "ffn3" in phases:
                norm("ffn3in", T2, None, False)
                pe.wait_ge(*when("ffn3in", "x", KD))
                ffn(3, T2, h2)
                norm("ffn3", T2, None, False)

        @block.scalar
        def _(act):
            c = Chain(act, s_act)
            act.sem_inc(tile_free, BUFS)

            def full(name, i, per, j):
                act.wait_ge(tile_full, i * per + (TILES[name] + j + 1))

            def project(name, T, per, trips, into):
                with act.Fori(0, trips) as i:
                    for j in range(per):
                        full(name, i, per, j)
                        nc.scalar.activation(sv(into(i * per + j), T), ps_tile(2 * ((TILES[name] + j) % 4), T), ACT.Copy).then_inc(tile_free, 1)

            def z_of(T):
                return lambda m: Z[:, m, 0:T]

            def norm(name, T, src, centred, ready, ready_n, eps):
                if centred:
                    act.wait_ge(*when(name, "mean", 1))
                    nc.scalar.activation(sv(NORM_MU[:, 0:T], T), ps_tile(0, T), ACT.Copy).then_inc(shared("mu", name), 1)
                for k in range(KD):
                    act.wait_ge(ready, ready_n(k))
                    nc.scalar.activation(A[:, k, 0:T], src(k), ACT.Square).then_inc(shared("sq", name), 1)
                act.wait_ge(*when(name, "var", 1))
                nc.scalar.activation(sv(NORM_R[:, 0:T], T), ps_tile(2, T), ACT.Sqrt, bias=SMALL[:, eps:eps + 1]).then_inc(shared("std", name), 1)
                if centred:
                    for k in range(KD):
                        act.wait_ge(*when(name, "sc", k + 1))
                        nc.scalar.activation(X[:, k, :], Z[:, k, :], ACT.Identity, bias=bias_col(name, k)).then_inc(shared("x", name), 1)

            def bias_col(name, k):
                return {"lru": col("ln1_b", k), "ffn0": col("ln2_b", k), "fox": col("ln1_b", 8 + k), "ffn1": col("ln2_b", 8 + k)}[name]

            def ffn(n, T, into):
                name = f"ffn{n}"
                off = 2 if T == T1 else 1
                xp, y, g = scratch(0, 4, 532), scratch(2128, 4, T1), scratch(4240, 2, T1)
                par = COLS[name]
                act.wait_ge(*when(name, "pad", 1))
                with act.Fori(0, NF // 2) as i:
                    for j in range(4):
                        full(name, i, 4, j)
                        act.wait_ge(*when(name, "conv", i * 4))
                        act.wait_ge(*when(name, "act", i * 2))
                        nc.scalar.activation(sv(xp[:, j, off:off + T], T), ps_tile(2 * ((TILES[name] + j) % 4), T), ACT.Copy).then_inc(tile_free, 1)
                        act.wait_ge(tile_free, i * 4 + (BUFS + TILES[name] + j + 1))
                        w0 = 16 * i + (par + 8 * (j // 2) + 4 * (j % 2))
                        nc.scalar.activation(y[:, j, 0:T], xp[:, j, 0:T], ACT.Identity, bias=PAR[:, ds(w0 + 3, 1)],
                                             scale=PAR[:, ds(w0, 1)]).then_inc(shared("tap", name), 1)
                    for j in range(2):
                        act.wait_ge(*when(name, "conv", i * 4 + (2 * j + 1)))
                        nc.scalar.activation(g[:, j, 0:T], y[:, 2 * j, 0:T], ACT.Gelu_apprx_tanh).then_inc(shared("gelu", name), 1)
                with act.Fori(0, 2) as i:
                    for j in range(4):
                        act.wait_ge(tile_full, i * 4 + (TILES[name] + 2 * NF + j + 1))
                        nc.scalar.activation(sv(into(i * 4 + j), T), ps_tile(2 * ((TILES[name] + j) % 4), T), ACT.Copy).then_inc(tile_free, 1)

            act.wait_ge(setup_lam, 1)
            nc.scalar.activation(SMALL[:, 12:24], SMALL[:, 0:12], ACT.Exp, scale=-1.0).then_inc(setup_lam_act, 1)

            xp, rc, r, ig, aa, th, mm, gg = [scratch(at, 3, n) for at, n in
                                             [(0, 532)] + [(1600 + 3 * T1 * q, T1) for q in range(7)]]
            act.wait_ge(lam_ready, 1)
            act.wait_ge(S("lru_pad"), 1)
            with act.Fori(0, 4) as i:
                c.loop(i, 3)
                act.wait_ge(S("lru_act"), i * 3)
                for j in range(3):
                    full("lru", i, 12, j)
                    nc.scalar.activation(sv(xp[:, j, 3:3 + T1], T1), ps_tile(2 * j, T1), ACT.Copy).then_inc(tile_free, 1)
                    act.wait_ge(tile_free, i * 12 + (BUFS + j + 1))
                    w0 = 15 * i + (COLS["a_conv"] + 5 * j)
                    nc.scalar.activation(rc[:, j, :], xp[:, j, 0:T1], ACT.Identity, bias=PAR[:, ds(w0 + 4, 1)],
                                         scale=PAR[:, ds(w0, 1)]).then_inc(S("lru_tap"), 1)
                for g, dst, b in ((0, r, "a_br"), (1, ig, "a_bi")):
                    for j in range(3):
                        full("lru", i, 12, 3 + 3 * g + j)
                        nc.scalar.activation(sv(dst[:, j, :], T1), ps_tile(2 * ((3 + 3 * g + j) % 4), T1), ACT.Sigmoid,
                                             bias=col(b, i * 3 + j)).then_inc(tile_free, 1)
                act.wait_ge(tile_free, i * 12 + (BUFS + 9))
                for j in range(3):
                    c(nc.scalar.activation(aa[:, j, :], r[:, j, :], ACT.Exp, scale=SMALL[:, ds(i * 3 + (72 + j), 1)]))
                    nc.scalar.activation(th[:, j, :], r[:, j, :], ACT.Tanh, scale=SMALL[:, ds(i * 3 + (60 + j), 1)]).then_inc(S("lru_at"), 1)
                for j in range(3):
                    act.wait_ge(S("lru_m"), i * 3 + (j + 1))
                    nc.scalar.activation(mm[:, j, :], mm[:, j, :], ACT.Sqrt).then_inc(S("lru_sqrt"), 1)
                for j in range(3):
                    full("lru", i, 12, 9 + j)
                    nc.scalar.activation(sv(gg[:, j, :], T1), ps_tile(2 * ((9 + j) % 4), T1), ACT.Gelu_apprx_tanh).then_inc(tile_free, 1)
            c.end(4)
            project("lru_out", T1, 2, 4, z_of(T1))
            z_src = lambda k: Z[:, k, :]
            norm("lru", T1, z_src, True, *at_k("lru", "ctr"), 180)
            if "ffn0" in phases:
                ffn(0, T1, z_of(T1))
                norm("ffn0", T1, z_src, True, *at_k("ffn0", "ctr"), 180)
            if "fox" in phases:
                fox_act(act, c, full)
                project("fox_out", T1, 4, 2, z_of(T1))
                norm("fox", T1, z_src, True, *at_k("fox", "ctr"), 180)
            if "ffn1" in phases:
                ffn(1, T1, z_of(T1))
                norm("ffn1", T1, z_src, True, *at_k("ffn1", "ctr"), 180)
            x2 = lambda k: X[:, k, META:T1]
            z2 = lambda k: Z[:, k, 0:T2]
            if "mix" in phases:
                norm("mixin", T2, x2, False, *at_k("ffn1", "x"), 181)
                ssd_act(act, c, full)
                mlstm_act(act, c, full)
                project("mix_out", T2, 2, 4, z_of(T2))
                norm("mix", T2, z2, False, tile_free, lambda k: BUFS + TILES["mix_out"] + k + 1, 181)
            if "ffn2" in phases:
                norm("ffn2in", T2, x2, False, *at_k("mix", "x"), 181)
                ffn(2, T2, z_of(T2))
                norm("ffn2", T2, z2, False, tile_free, lambda k: BUFS + TILES["ffn2"] + 2 * NF + k + 1, 181)
            if "gla" in phases:
                norm("glain", T2, x2, False, *at_k("ffn2", "x"), 181)
                gla_act(act, c, full)
                project("gla_out", T2, 4, 2, z_of(T2))
                norm("gla", T2, z2, False, tile_free, lambda k: BUFS + TILES["gla_out"] + k + 1, 181)
            if "ffn3" in phases:
                norm("ffn3in", T2, x2, False, *at_k("gla", "x"), 181)
                ffn(3, T2, z_of(T2))
                norm("ffn3", T2, z2, False, tile_free, lambda k: BUFS + TILES["ffn3"] + 2 * NF + k + 1, 181)

        @block.vector
        def _(dve):
            c = Chain(dve, s_dve)
            v = nc.vector

            def log1p_of_exp(x, e, z, t, poly):
                c(v.tensor_scalar(t, e, 2.0, None, ALU.add))
                c(v.reciprocal(t, t))
                c(v.tensor_tensor(z, e, t, ALU.mult))
                c(v.tensor_tensor(t, z, z, ALU.mult))
                c(v.tensor_scalar(poly, t, 1.0 / 15, None, ALU.mult))
                for k in (13, 11, 9, 7, 5, 3):
                    c(v.scalar_tensor_tensor(out=poly, in0=poly, scalar=1.0 / k, in1=t, op0=ALU.add, op1=ALU.mult))
                c(v.scalar_tensor_tensor(out=poly, in0=poly, scalar=1.0, in1=z, op0=ALU.add, op1=ALU.mult))
                c(v.tensor_scalar(poly, poly, 2.0, None, ALU.mult))

            def residual(name, tiles, count):
                for k in range(KD):
                    dve.wait_ge(tile_free, BUFS + tiles + k + 1)
                    v.scalar_tensor_tensor(out=Z[:, k, :], in0=X[:, k, :], scalar=ALPHA, in1=Z[:, k, :], op0=ALU.mult,
                                           op1=ALU.add).then_inc(shared("z", name), 1)

            def ln(name, g, k0):
                dve.wait_ge(*when(name, "mu", 1))
                for k in range(KD):
                    dve.wait_ge(*when(name, "z", k + 1))
                    v.tensor_tensor(Z[:, k, :], Z[:, k, :], NORM_MU[:, :], ALU.subtract).then_inc(shared("ctr", name), 1)
                dve.wait_ge(*when(name, "std", 1))
                c(v.reciprocal(NORM_R[:, :], NORM_R[:, :]))
                for k in range(KD):
                    dve.wait_ge(*when(name, "ctr", k + 1))
                    v.scalar_tensor_tensor(out=Z[:, k, :], in0=Z[:, k, :], scalar=col(g, k0 + k), in1=NORM_R[:, :],
                                           op0=ALU.mult, op1=ALU.mult).then_inc(shared("sc", name), 1)

            def rms_in(name, g):
                dve.wait_ge(*when(name, "std", 1))
                c(v.reciprocal(NORM_R[:, 0:T2], NORM_R[:, 0:T2]))
                for k in range(KD):
                    v.scalar_tensor_tensor(out=Z[:, k, 0:T2], in0=X[:, k, META:T1], scalar=col("norm_g", g * 8 + k),
                                           in1=NORM_R[:, 0:T2], op0=ALU.mult, op1=ALU.mult).then_inc(shared("x", name), 1)

            def rms_out(name, g):
                dve.wait_ge(*when(name, "std", 1))
                c(v.reciprocal(NORM_R[:, 0:T2], NORM_R[:, 0:T2]))
                for k in range(KD):
                    c(v.scalar_tensor_tensor(out=Z[:, k, 0:T2], in0=Z[:, k, 0:T2], scalar=col("norm_g", g * 8 + k),
                                             in1=NORM_R[:, 0:T2], op0=ALU.mult, op1=ALU.mult))
                    v.tensor_tensor(X[:, k, META:T1], X[:, k, META:T1], Z[:, k, 0:T2], ALU.add).then_inc(shared("x", name), 1)
                dve.wait_ge(*when(name, "x", KD))

            def ffn(n, T):
                name = f"ffn{n}"
                off = 2 if T == T1 else 1
                xp, y, g = scratch(0, 4, 532), scratch(2128, 4, T1), scratch(4240, 2, T1)
                par = COLS[name]
                c(v.memset(xp[:, :, 0:2], 0.0))
                v.memset(xp[:, :, T + off:T + 2] if T == T2 else xp[:, :, 0:2], 0.0).then_inc(shared("pad", name), 1)
                with dve.Fori(0, NF // 2) as i:
                    c.loop(i, 4)
                    for j in range(4):
                        dve.wait_ge(*when(name, "tap", i * 4 + (j + 1)))
                        w0 = 16 * i + (par + 8 * (j // 2) + 4 * (j % 2))
                        c(v.scalar_tensor_tensor(out=y[:, j, 0:T], in0=xp[:, j, 1:1 + T], scalar=PAR[:, ds(w0 + 1, 1)],
                                                 in1=y[:, j, 0:T], op0=ALU.mult, op1=ALU.add))
                        v.scalar_tensor_tensor(out=y[:, j, 0:T], in0=xp[:, j, 2:2 + T], scalar=PAR[:, ds(w0 + 2, 1)],
                                               in1=y[:, j, 0:T], op0=ALU.mult, op1=ALU.add).then_inc(shared("conv", name), 1)
                    for j in range(2):
                        dve.wait_ge(*when(name, "gelu", i * 2 + (j + 1)))
                        dve.wait_ge(*when(name, "conv", i * 4 + (2 * j + 2)))
                        v.tensor_tensor(A[:, i * 2 + j, 0:T], g[:, j, 0:T], y[:, 2 * j + 1, 0:T], ALU.mult).then_inc(shared("act", name), 1)
                c.end(NF // 2)

            dve.wait_ge(loaded, 32)
            lam, e, z, t, poly = [SMALL[:, 12 * q:12 * q + 12] for q in range(5)]
            v.scalar_tensor_tensor(out=lam, in0=PAR[:, COLS["a_lam"]:COLS["a_lam"] + 12], scalar=-1.0,
                                   in1=PAR[:, COLS["a_lam"]:COLS["a_lam"] + 12], op0=ALU.mult, op1=ALU.max).then_inc(setup_lam, 1)
            c(v.memset(SMALL[:, 180:181], 1e-5))
            c(v.memset(SMALL[:, 181:182], 1e-6))
            c(v.memset(SMALL[:, 182:183], 1.0))
            dve.wait_ge(setup_lam_act, 1)
            log1p_of_exp(lam, e, z, t, poly)
            c(v.tensor_scalar(t, PAR[:, COLS["a_lam"]:COLS["a_lam"] + 12], -1.0, 0.0, ALU.mult, ALU.max))
            c(v.tensor_tensor(poly, poly, t, ALU.add))
            c(v.tensor_scalar(SMALL[:, 60:72], poly, 8.0, None, ALU.mult))
            v.tensor_scalar(SMALL[:, 72:84], poly, -8.0, None, ALU.mult).then_inc(lam_ready, 1)

            xp, rc, r, ig, aa, th, mm, gg = [scratch(at, 3, n) for at, n in
                                             [(0, 532)] + [(1600 + 3 * T1 * q, T1) for q in range(7)]]
            v.memset(xp[:, :, 0:3], 0.0).then_inc(S("lru_pad"), 1)
            with dve.Fori(0, 4) as i:
                c.loop(i, 3 * (2 + 1 + 3))
                for j in range(3):
                    dve.wait_ge(S("lru_tap"), i * 3 + (j + 1))
                    w0 = 15 * i + (COLS["a_conv"] + 5 * j)
                    for k in (1, 2):
                        c(v.scalar_tensor_tensor(out=rc[:, j, :], in0=xp[:, j, k:k + T1], scalar=PAR[:, ds(w0 + k, 1)],
                                                 in1=rc[:, j, :], op0=ALU.mult, op1=ALU.add))
                    v.scalar_tensor_tensor(out=rc[:, j, :], in0=xp[:, j, 3:3 + T1], scalar=PAR[:, ds(w0 + 3, 1)],
                                           in1=rc[:, j, :], op0=ALU.mult, op1=ALU.add).then_inc(S("lru_conv"), 1)
                for j in range(3):
                    dve.wait_ge(S("lru_at"), i * 3 + (j + 1))
                    c(v.tensor_tensor(mm[:, j, :], aa[:, j, :], aa[:, j, :], ALU.mult))
                    v.scalar_tensor_tensor(out=mm[:, j, :], in0=mm[:, j, :], scalar=1.0, in1=th[:, j, :], op0=ALU.add,
                                           op1=ALU.mult).then_inc(S("lru_m"), 1)
                for j in range(3):
                    dve.wait_ge(S("lru_sqrt"), i * 3 + (j + 1))
                    c(v.tensor_tensor(ig[:, j, :], ig[:, j, :], rc[:, j, :], ALU.mult))
                    c(v.tensor_tensor(ig[:, j, :], ig[:, j, :], mm[:, j, :], ALU.mult))
                    c(v.tensor_tensor_scan(r[:, j, :], aa[:, j, :], ig[:, j, :], 0.0, ALU.mult, ALU.add))
                for j in range(3):
                    dve.wait_ge(tile_free, i * 12 + (BUFS + 10 + j))
                    v.tensor_tensor(A[:, i * 3 + j, :], gg[:, j, :], r[:, j, :], ALU.mult).then_inc(S("lru_act"), 1)
            c.end(4)
            residual("lru", TILES["lru_out"], 8)
            ln("lru", "ln1_g", 0)
            if "ffn0" in phases:
                ffn(0, T1)
                dve.wait_ge(*when("lru", "x", KD))
                residual("ffn0", TILES["ffn0"] + 2 * NF, 8)
                ln("ffn0", "ln2_g", 0)
            if "fox" in phases:
                fox_dve(dve, c)
                dve.wait_ge(*when("ffn0", "x", KD))
                residual("fox", TILES["fox_out"], 8)
                ln("fox", "ln1_g", 8)
            if "ffn1" in phases:
                ffn(1, T1)
                dve.wait_ge(*when("fox", "x", KD))
                residual("ffn1", TILES["ffn1"] + 2 * NF, 8)
                ln("ffn1", "ln2_g", 8)
            if "mix" in phases:
                dve.wait_ge(*when("ffn1", "x", KD))
                rms_in("mixin", 0)
                ssd_dve(dve, c, log1p_of_exp)
                mlstm_dve(dve, c)
                rms_out("mix", 1)
            if "ffn2" in phases:
                rms_in("ffn2in", 2)
                ffn(2, T2)
                rms_out("ffn2", 3)
            if "gla" in phases:
                rms_in("glain", 4)
                gla_dve(dve, c)
                rms_out("gla", 5)
            if "ffn3" in phases:
                rms_in("ffn3in", 6)
                ffn(3, T2)
                rms_out("ffn3", 7)

        @block.gpsimd
        def _(pool):
            c = Chain(pool, s_pool)
            g = nc.gpsimd
            c(g.memset(ONES[:, :], 1.0))
            for q, n in enumerate((D, 512, 256)):
                c(g.memset(MEANW[:, q, :], 1.0 / n))
            c(g.affine_select(out=ID[:, :], in_=ONES[:, :], compare_op=ALU.is_equal, fill=0.0, base=0, pattern=[[-1, P]], channel_multiplier=1))
            c(g.memset(CAUSAL_ADD[:, :], 0.0))
            c(g.affine_select(out=CAUSAL_ADD[:, :], in_=CAUSAL_ADD[:, :], compare_op=ALU.is_ge, fill=-BIG, base=0, pattern=[[-1, P]], channel_multiplier=1))
            c(g.affine_select(out=LOWER[:, :], in_=ONES[:, :], compare_op=ALU.is_ge, fill=0.0, base=0, pattern=[[1, P]], channel_multiplier=-1))
            c(g.affine_select(out=UPPER[:, :], in_=ONES[:, :], compare_op=ALU.is_ge, fill=0.0, base=0, pattern=[[-1, P]], channel_multiplier=1))
            g.memset(NORM_MU[:, :], 0.0).then_inc(consts_ready, 1)
            if "mix" in phases:
                ssd_pool(pool, c)
                mlstm_pool(pool, c)


def _unit_cols(w, c0, n=P):
    k = w.shape[0] // P
    return w[:, c0:c0 + n].reshape(k, P, n).transpose(1, 0, 2)


def _layout(inputs):
    f = {k: np.asarray(v) for k, v in inputs.items()}
    units = np.zeros((N_UNITS, P, KD, P), np.float32)
    at = [0]

    def put(w, c0, n=P, into=0):
        t = _unit_cols(w, c0, n)
        for k in range(0, t.shape[1], KD):
            q = min(KD, t.shape[1] - k)
            units[at[0], :, 0:q, into:into + n] = t[:, k:k + q]
            at[0] += 1

    def at_phase(name):
        assert at[0] == UNITS[name], (name, at[0], UNITS[name])

    def put_ffn(name, w_in, w_out):
        at_phase(name)
        for t in range(NF):
            put(w_in, t * P)
            put(w_in, DFF + t * P)
        for m in range(KD):
            put(w_out, m * P)

    a_in = f["a_w_in"][0]
    for g in range(4):
        for j in range(3):
            put(a_in, RNN + (3 * g + j) * P)
        for w in (f["a_w_r"][0], f["a_w_i"][0]):
            dense = np.zeros((3 * P, 3 * P), np.float32)
            for b in range(4):
                dense[b * LRU:(b + 1) * LRU, b * LRU:(b + 1) * LRU] = w[4 * g + b]
            for q, (o, k) in enumerate(LRU_PIECES):
                units[at[0], :, q, :] = dense[k * P:(k + 1) * P, o * P:(o + 1) * P]
            at[0] += 1
        for j in range(3):
            put(a_in, (3 * g + j) * P)
    at_phase("lru_out")
    for m in range(KD):
        put(f["a_w_out"][0], m * P)
    put_ffn("ffn0", f["f_w_in"][0], f["f_w_out"][0])
    kv, bw = f["kv_w"], f["b_w_in"][0]
    put(kv, 2 * D, 16)
    at_phase("fox")
    for h in range(KD):
        put(bw, h * P)
        put(kv, h * P)
        put(kv, D + h * P)
        put(bw, D + h * P)
    at_phase("fox_out")
    for m in range(KD):
        put(f["b_w_out"][0], m * P)
    put_ffn("ffn1", f["f_w_in"][1], f["f_w_out"][1])
    ab = f["ab_w_in_2"][0]
    z0, xbc0, dt0, q0 = 0, D, D + 1536, D + 1536 + 32
    gates0 = q0 + 4 * D
    at_phase("ssd_pre")
    put(ab, dt0, 16)
    at[0] -= 1
    put(ab, dt0 + 16, 16, 32)
    for d in range(2):
        put(ab, gates0 + 8 * d, 8, 32 * d)
        at[0] -= 1
        put(ab, gates0 + 16 + 8 * d, 8, 64 + 32 * d)
        if d == 0:
            at[0] -= 1
    for b in range(4):
        put(ab, xbc0 + D + b * P)
    at_phase("ssd")
    for h in range(KD):
        put(ab, xbc0 + h * P)
        put(ab, z0 + h * P)
    at_phase("mlstm")
    for h in range(KD):
        for s in range(4):
            put(ab, q0 + s * D + h * P)
    at_phase("mix_out")
    for m in range(KD):
        put(f["ab_w_out_2"][0], m * P)
    put_ffn("ffn2", f["ffn_w_up_2"][0], f["ffn_w_down_2"][0])
    cw = f["c_w_in_2"][0]
    put(cw, 3072, 16)
    at[0] -= 1
    put(cw, 3072 + 16, 16, 32)
    at_phase("gla")
    for h in range(4):
        put(cw, h * P)
        put(cw, 512 + h * P)
        for s in range(2):
            for a in range(2):
                put(cw, D + s * D + (2 * h + a) * P)
    at_phase("gla_out")
    for m in range(KD):
        put(f["c_w_out_2"][0], m * P)
    put_ffn("ffn3", f["ffn_w_up_2"][1], f["ffn_w_down_2"][1])
    assert at[0] == N_UNITS

    cols = np.zeros((P, N_COLS), np.float32)

    def vec(name, v, k=0, step=1):
        v = np.asarray(v).reshape(-1, P)
        for t in range(v.shape[0]):
            cols[:, COLS[name] + k + t * step] = v[t]

    def conv(name, w, b, k, step):
        for q in range(w.shape[0]):
            vec(name, w[q], k + q, step)
        vec(name, b, k + w.shape[0], step)

    conv("a_conv", f["a_conv_w"][0], f["a_conv_b"][0], 0, 5)
    vec("a_br", f["a_b_r"][0])
    vec("a_bi", f["a_b_i"][0])
    vec("a_lam", f["a_lambda"][0])
    cols[0:16, COLS["fox_fb"]] = f["kv_f_b"]
    for name in ("ln1_g", "ln1_b", "ln2_g", "ln2_b"):
        vec(name, f[name])
    vec("norm_g", f["norm_g_2"])
    for n, (w, b) in enumerate(((f["f_conv_w"][0], f["f_conv_b"][0]), (f["f_conv_w"][1], f["f_conv_b"][1]),
                                (f["ffn_conv_w_2"][0], f["ffn_conv_b_2"][0]), (f["ffn_conv_w_2"][1], f["ffn_conv_b_2"][1]))):
        conv(f"ffn{n}", w[:, 0:DFF], b[0:DFF], 0, 8)
        conv(f"ffn{n}", w[:, DFF:], b[DFF:], 4, 8)
    conv("ab_conv", f["ab_conv_w_2"][0], f["ab_conv_b_2"][0], 0, 6)
    for d in range(2):
        cols[32 * d:32 * d + 16, COLS["dt_bias"]] = f["ab_dt_bias_2"][0, d]
        cols[32 * d:32 * d + 16, COLS["a_log"]] = f["ab_a_log_2"][0, d]
        cols[32 * d:32 * d + 8, COLS["ig_bias"]] = f["ab_ig_bias_2"][0, d]
        cols[32 * d:32 * d + 8, COLS["fg_bias"]] = f["ab_fg_bias_2"][0, d]
    vec("d_skip", np.repeat(f["ab_d_skip_2"][0], 64))
    vec("ssd_norm", f["ab_ssd_norm_2"][0])
    vec("mlstm_norm", f["ab_mlstm_norm_2"][0])
    vec("gate_b", f["c_gate_b_2"][0])
    vec("gla_norm", f["c_norm_2"][0])

    gate_w2 = np.zeros((48, 512), np.float32)
    gate_w2[0:16] = f["c_gate_w2_2"][0, 0]
    gate_w2[32:48] = f["c_gate_w2_2"][0, 1]

    x_t = np.concatenate([f["meta"], f["x"][0]], axis=0).reshape(T1, KD, P).transpose(2, 1, 0)
    return {"x_t": np.ascontiguousarray(x_t), "units": units, "cols": cols, "gate_w2": gate_w2}


def kernel(**inputs):
    import concourse.bacc as _bacc
    from concourse.bass_utils import run_bass_kernel_spmd as _run

    nc = _bacc.Bacc("TRN2", target_bir_lowering=False, num_devices=1)
    arrays = _layout(inputs)
    args = [nc.dram_tensor(name, a.shape, F32, kind="ExternalInput").ap() for name, a in arrays.items()]
    out = nc.dram_tensor("out_t", (P, KD, SEQ), F32, kind="ExternalOutput").ap()
    build(nc, *args, out)
    r = _run(nc, [arrays], core_ids=[0])
    got = r.results[0]["out_t"]
    return np.ascontiguousarray(got.transpose(2, 1, 0).reshape(1, SEQ, D))
```

```python
from contextlib import ExitStack

import concourse.bass as bass
from concourse import mybir
import numpy as np

F32 = mybir.dt.float32
ALU = mybir.AluOpType
ACT = mybir.ActivationFunctionType
AXX = mybir.AxisListType.X
ds = bass.ds

P = 128
D = 1024
KD = D // P
META = 16
SEQ = 512
T1 = META + SEQ
T2 = SEQ
HALF = T1 // 2
RNN = 3 * D // 2
LRU = 96
DFF = 2816
NF = DFF // P
SLOTS = 4
BUFS = 4
ALPHA = float((2 * 2) ** 0.25)
BIG = 1.0e30
LRU_PIECES = [(0, 0), (0, 1), (1, 0), (1, 1), (1, 2), (2, 1), (2, 2)]

UNITS = {}
_u = 0
for _name, _count in [("lru", 32), ("lru_out", 16), ("ffn0", 68), ("fox_f", 1), ("fox", 32), ("fox_out", 8), ("ffn1", 68),
                      ("ssd_pre", 6), ("ssd", 16), ("mlstm", 32), ("mix_out", 16), ("ffn2", 68),
                      ("gla_pre", 1), ("gla", 24), ("gla_out", 8), ("ffn3", 68)]:
    UNITS[_name] = _u
    _u += _count
N_UNITS = _u

COLS = {}
_c = 0
for _name, _count in [("a_conv", 12 * 5), ("a_br", 12), ("a_bi", 12), ("a_lam", 12), ("fox_fb", 1),
                      ("ln1_g", 16), ("ln1_b", 16), ("ln2_g", 16), ("ln2_b", 16), ("norm_g", 64),
                      ("ffn0", 8 * NF), ("ffn1", 8 * NF), ("ffn2", 8 * NF), ("ffn3", 8 * NF),
                      ("ab_conv", 12 * 6), ("dt_bias", 1), ("a_log", 1), ("ig_bias", 1), ("fg_bias", 1),
                      ("d_skip", 8), ("ssd_norm", 8), ("mlstm_norm", 8), ("gate_b", 8), ("gla_norm", 8)]:
    COLS[_name] = _c
    _c += _count
N_COLS = _c


class Chain:

    def __init__(self, eng, sem):
        self.eng, self.sem, self.n, self.at = eng, sem, 0, 0

    def __call__(self, ins):
        ins.then_inc(self.sem, 1)
        self.n += 1
        self.eng.wait_ge(self.sem, self.at + self.n)

    def loop(self, i, per, begin=0):
        self.n -= begin * per
        self.start, self.per, self.begin = self.n, per, begin
        self.at = i * per

    def end(self, trips):
        assert self.n - self.start == self.per, ("per", self.n - self.start)
        self.n += (trips - 1 + self.begin) * self.per
        self.at = 0


def build(nc, x_t, units, cols, gate_w2, out, stop_after=None):
    ctx = ExitStack()
    with ctx:
        def sb(name, shape):
            return ctx.enter_context(nc.sbuf_tensor(name, shape, F32))

        def sem(name):
            return ctx.enter_context(nc.semaphore(name))

        X = sb("residual", [P, KD, T1])
        Z = sb("stream", [P, KD, T1])
        A = sb("acts", [P, NF, T1])
        W = sb("w_ring", [P, SLOTS, KD, P])
        PAR = sb("params", [P, N_COLS])
        ID = sb("identity", [P, P])
        ONES = sb("ones", [P, P])
        MEANW = sb("mean_weights", [P, 3, P])
        CAUSAL_ADD = sb("causal_add", [P, P])
        LOWER = sb("keep_l_ge_s", [P, P])
        UPPER = sb("keep_l_le_s", [P, P])
        NORM_MU = sb("norm_mu", [P, T1])
        NORM_R = sb("norm_r", [P, T1])
        SMALL = sb("small", [P, 192])
        SCR = sb("scratch", [P, 20200])
        PS = ctx.enter_context(nc.psum_tensor("psum", [P, 8, 512], F32))
        PSF = PS[:, :, :].rearrange("p b c -> p (b c)")

        SQ_AT = 8000

        def scratch(at, *shape):
            n = int(np.prod(shape))
            v = SCR[:, at:at + n]
            if len(shape) == 2:
                v = v.rearrange("p (a b) -> p a b", a=shape[0])
            if len(shape) == 3:
                v = v.rearrange("p (a b c) -> p a b c", a=shape[0], b=shape[1])
            return v

        def ps_tile(bank, T, rows=P):
            return PS[0:rows, bank:bank + 2, 0:HALF] if T == T1 else PS[0:rows, bank, 0:T]

        def sv(ap, T):
            return ap.rearrange("p (h t) -> p h t", h=2) if T == T1 else ap

        def parts(T):
            return [(0, 0, HALF), (1, HALF, HALF)] if T == T1 else [(0, 0, T)]

        def col(name, k=0, rows=P):
            if isinstance(k, int):
                return PAR[0:rows, COLS[name] + k:COLS[name] + k + 1]
            return PAR[0:rows, ds(k + COLS[name], 1)]

        w_full = [sem(f"w_full{b}") for b in range(SLOTS)]
        w_started = sem("w_started")
        tile_full = sem("tile_full")
        tile_free = sem("tile_free")
        loaded = sem("loaded")
        x_loaded = [sem(f"x_loaded{q}") for q in range(4)]
        w2_loaded = sem("w2_loaded")
        consts_ready = sem("consts_ready")
        out_done = sem("out_done")
        s_dve = sem("dve_chain")
        s_act = sem("act_chain")
        s_pool = sem("pool_chain")
        setup_lam = sem("setup_lam")
        setup_lam_act = sem("setup_lam_act")
        lam_ready = sem("lam_ready")

        sems = {}

        def S(name):
            if name not in sems:
                sems[name] = sem(name)
            return sems[name]

        NORMS = ["lru", "ffn0", "fox", "ffn1", "mixin", "mix", "ffn2in", "ffn2", "glain", "gla", "ffn3in", "ffn3"]
        SUMMED = ["mix", "ffn2", "gla", "ffn3"]
        FFNS = ["ffn0", "ffn1", "ffn2", "ffn3"]
        PER = {"z": KD, "mean": 1, "mu": 1, "ctr": KD, "sc": KD, "sq": KD, "zsum": KD - 1, "sqsum": KD - 1, "var": 1, "std": 1, "x": KD,
               "pad": 1, "tap": 2 * NF, "conv": 2 * NF, "gelu": NF, "act": NF}

        def shared(what, name):
            return S(("ffn_" if what in ("pad", "tap", "conv", "gelu", "act") else "norm_") + what)

        def when(name, what, n):
            order = FFNS if what in ("pad", "tap", "conv", "gelu", "act") else SUMMED if what == "sqsum" else NORMS
            return shared(what, name), n + PER[what] * order.index(name) + (what in ("conv", "act"))

        def credit(eng, *names):
            for name in names:
                eng.sem_inc(S(name), 1)

        def at_k(name, what):
            return shared(what, name), lambda k: when(name, what, k + 1)[1]

        block = ctx.enter_context(nc.Block())

        TILES = {}
        n = 0
        for name, count in [("lru", 48), ("lru_out", 8), ("ffn0", 52), ("fox_f", 1), ("fox", 32), ("fox_out", 8), ("ffn1", 52),
                            ("ssd_pre", 7), ("ssd", 16), ("mlstm", 32), ("mix_out", 8), ("ffn2", 52),
                            ("gla_pre", 1), ("gla", 24), ("gla_out", 8), ("ffn3", 52)]:
            TILES[name] = n
            n += count
        TILES["end"] = n

        phases = ["lru", "ffn0", "fox", "ffn1", "mix", "ffn2", "gla", "ffn3"]
        if stop_after is not None:
            phases = phases[:phases.index(stop_after) + 1]

        CH = [(0, META)] + [(META + P * q, P) for q in range(SEQ // P)]
        STEPS = [(ch, hh) for ch in range(len(CH)) for hh in range(2)]
        NS = len(STEPS)
        fx_q, fx_sg = scratch(9452, 2, T1), scratch(1056, T1)
        fx_v = scratch(1584, 5, P)
        fx_p, fx_ptb, fx_o = scratch(2224, 2, T1), scratch(3280, 2, 5, P), scratch(4560, P)
        fx_nm, fx_sum, fx_rs = scratch(4688, 2), scratch(4690, 2), scratch(4692, 4)
        FX_BANK = (4, 6, 2, 0)
        fx_c, fx_nc = scratch(4700, T1), scratch(5228, T1)
        fx_k = scratch(6812, 2, T1)
        FX_GATES = (64, 0)
        fx_x, fx_ab, fx_e = scratch(7868, T1), scratch(8396, T1), scratch(8924, T1)

        def apart(pe):
            pe.sem_inc(S("pe_steps"), 1)

        def fox_pe(pe, unit, buffer_free, gemm, gemm_tokens, h):
            pe.wait_ge(tile_free, BUFS + TILES["fox_f"])
            s = unit(UNITS["fox_f"], 0, 0, 0)
            gemm(2 * (TILES["fox_f"] % 4), [(s, 0, KD)], h, T1, 0, 16, ready=lambda k: when("ffn0", "x", k + 1)).then_inc(tile_full, 1)
            bank = lambda j: FX_BANK[j]
            with pe.Fori(0, KD) as i:
                def tile(j):
                    buffer_free("fox", i, 4, j, 4)
                    s = unit(UNITS["fox"], i, 4, j)
                    if j == 2:
                        chunks = [(1, 0, 0, META)] + [(0, P * q, META + P * q, P) for q in range(4)]
                        gemm_tokens(bank(j), s, h, chunks).then_inc(tile_full, 1)
                    else:
                        gemm(bank(j), [(s, 0, KD)], h, T1).then_inc(tile_full, 1)

                def scores(n):
                    ch, hh = STEPS[n]
                    qs, qn = CH[ch]
                    ke = qs + qn
                    base = 512 * (4 + 2 * (n % 2))
                    if n >= 2:
                        pe.wait_ge(S("fx_exp"), i * NS + (n - 1))
                    apart(pe)
                    for a, b in [(0, min(ke, 512))] + ([(512, ke)] if ke > 512 else []):
                        nc.tensor.matmul(PSF[0:qn, base + a:base + b], fx_q[:, hh, qs:ke], fx_k[:, hh, a:b], start=True, stop=False)
                        da = max(a, qs)
                        mm = nc.tensor.matmul(PSF[0:qn, base + da:base + b], ID[0:qn, 0:qn], CAUSAL_ADD[0:qn, da - qs:b - qs],
                                              start=False, stop=True)
                    mm.then_inc(S("fx_s"), 1)

                def turn(ch):
                    qn = CH[ch][1]
                    pe.wait_ge(S("fx_on"), i * NS + (2 * ch + 2))
                    if ch > 0:
                        pe.wait_ge(S("fx_out"), i * 5 + ch + 1)
                    apart(pe)
                    nc.tensor.transpose(PS[:, 3, 0:qn], fx_o[0:qn, :], ID[0:qn, 0:qn]).then_inc(S("fx_ot"), 1)

                def weigh(n):
                    ch, hh = STEPS[n]
                    qn = CH[ch][1]
                    pe.wait_ge(S("fx_pt"), i * NS + (n + 1))
                    if n > 0:
                        pe.wait_ge(S("fx_on"), i * NS + n)
                    apart(pe)
                    for kb in range(ch + 1):
                        kn = CH[kb][1]
                        mm = nc.tensor.matmul(PS[0:qn, 2, 0:P], fx_ptb[0:kn, n % 2, kb, 0:qn], fx_v[0:kn, kb, :],
                                              start=(kb == 0), stop=(kb == ch))
                    mm.then_inc(S("fx_pv"), 1)

                tile(0)
                tile(1)
                pe.wait_ge(S("fx_out"), i * 5 + 1)
                tile(2)
                pe.wait_ge(tile_free, i * 4 + (BUFS + TILES["fox"] + 2))
                pe.wait_ge(S("fx_sel"), i * 2 + 2)
                scores(0)
                tile(3)
                scores(1)
                pe.wait_ge(tile_free, i * 4 + (BUFS + TILES["fox"] + 4))
                for n, (ch, hh) in enumerate(STEPS):
                    qs, qn = CH[ch]
                    pe.wait_ge(S("fx_exp"), i * NS + (n + 1))
                    if n > 0:
                        pe.wait_ge(S("fx_pt"), i * NS + n)
                    apart(pe)
                    for kb in range(ch + 1):
                        ks, kn = CH[kb]
                        dst = PS[0:kn, 1, 0:qn] if kb == 0 else PS[0:kn, 0, P * (kb - 1):P * (kb - 1) + qn]
                        mm = nc.tensor.transpose(dst, fx_p[0:qn, n % 2, ks:ks + kn], ID[0:qn, 0:qn])
                    mm.then_inc(S("fx_tr"), 1)
                    if n + 2 < NS:
                        scores(n + 2)
                    if hh == 1 and ch > 0:
                        turn(ch - 1)
                    if n > 0:
                        weigh(n - 1)
                weigh(NS - 1)
                turn(len(CH) - 1)
            pe.wait_ge(S("fx_out"), 5 * KD + 1)

        def fox_act(act, c, full):
            full("fox_f", 0, 0, 0)
            nc.scalar.activation(sv(fx_x[0:16, :], T1), ps_tile(2 * (TILES["fox_f"] % 4), T1, 16), ACT.Identity,
                                 bias=col("fox_fb", 0, 16)).then_inc(tile_free, 1)
            act.wait_ge(S("fx_abs"), 1)
            c(nc.scalar.activation(fx_e[0:16, :], fx_ab[0:16, :], ACT.Exp, scale=-1.0))
            nc.scalar.activation(fx_ab[0:16, :], fx_e[0:16, :], ACT.Ln, bias=SMALL[0:16, 182:183]).then_inc(S("fx_ln"), 1)
            bank = lambda j: FX_BANK[j]
            act.wait_ge(S("fx_zero"), 1)
            with act.Fori(0, KD) as i:
                act.wait_ge(S("fx_out"), i * 5 + 1)
                full("fox", i, 4, 0)
                for hh in range(2):
                    half = slice(64 * hh, 64 * hh + 64)
                    q = nc.scalar.activation(sv(fx_q[half, hh, :], T1), PS[half, bank(0):bank(0) + 2, 0:HALF], ACT.Copy, scale=0.125)
                q.then_inc(tile_free, 1)
                full("fox", i, 4, 1)
                for hh in range(2):
                    half = slice(64 * hh, 64 * hh + 64)
                    k = nc.scalar.activation(sv(fx_k[half, hh, :], T1), PS[half, bank(1):bank(1) + 2, 0:HALF], ACT.Copy)
                k.then_inc(tile_free, 1)
                full("fox", i, 4, 2)
                nc.scalar.activation(fx_v[0:META, 0, :], PS[0:META, bank(2) + 1, 0:P], ACT.Copy)
                nc.scalar.activation(fx_v[:, 1:5, :], PS[:, bank(2), :].rearrange("p (a b) -> p a b", a=4), ACT.Copy).then_inc(tile_free, 1)

                def scaled(n):
                    ch, hh = STEPS[n]
                    qn = CH[ch][1]
                    act.wait_ge(S("fx_pv"), i * NS + (n + 1))
                    if hh == 0 and ch > 0:
                        act.wait_ge(S("fx_ot"), i * 5 + ch)
                    nc.scalar.activation(fx_o[0:qn, 64 * hh:64 * hh + 64], PS[0:qn, 2, 64 * hh:64 * hh + 64], ACT.Copy,
                                         scale=fx_rs[0:qn, n % 4:n % 4 + 1]).then_inc(S("fx_on"), 1)

                for n, (ch, hh) in enumerate(STEPS):
                    qs, qn = CH[ch]
                    ke = qs + qn
                    base = 512 * (4 + 2 * (n % 2))
                    act.wait_ge(S("fx_mx"), i * NS + (n + 1))
                    if n >= 2:
                        act.wait_ge(S("fx_tr"), i * NS + (n - 1))
                    nc.scalar.activation(fx_p[0:qn, n % 2, 0:ke], PSF[0:qn, base:base + ke], ACT.Exp, bias=fx_nm[0:qn, n % 2:n % 2 + 1],
                                         accum_out=fx_sum[0:qn, n % 2:n % 2 + 1]).then_inc(S("fx_exp"), 1)
                    if n == 0:
                        full("fox", i, 4, 3)
                        nc.scalar.activation(sv(fx_sg, T1), ps_tile(bank(3), T1), ACT.Sigmoid).then_inc(tile_free, 1)
                    if n >= 2:
                        scaled(n - 2)
                scaled(NS - 2)
                scaled(NS - 1)

        def fox_dve(dve, c):
            v = nc.vector
            c(v.memset(NORM_MU[:, :], 1.0))
            for hh, r0 in enumerate(FX_GATES):
                c(v.memset(fx_k[r0:r0 + 64, hh, :], 1.0))
                c(v.memset(fx_q[r0:r0 + 64, hh, :], 0.0))
                ones = v.memset(fx_q[r0 + 32:r0 + 48, hh, :], 1.0)
                if hh == 0:
                    c(ones)
            ones.then_inc(S("fx_zero"), 1)
            dve.wait_ge(S("fx_zero"), 1)
            dve.wait_ge(tile_free, BUFS + TILES["fox_f"] + 1)
            x, ab = fx_x[0:16, :], fx_ab[0:16, :]
            v.scalar_tensor_tensor(out=ab, in0=x, scalar=-1.0, in1=x, op0=ALU.mult, op1=ALU.max).then_inc(S("fx_abs"), 1)
            dve.wait_ge(S("fx_ln"), 1)
            c(v.scalar_tensor_tensor(out=x, in0=x, scalar=0.0, in1=ab, op0=ALU.min, op1=ALU.subtract))
            c(v.tensor_tensor_scan(fx_c[0:16, :], NORM_MU[0:16, :], x, 0.0, ALU.mult, ALU.add))
            c(v.tensor_scalar(fx_nc[0:16, :], fx_c[0:16, :], -1.0, None, ALU.mult))
            with dve.Fori(0, KD) as i:
                c.loop(i, 2 + NS)
                for hh in range(2):
                    sel, r0 = ID[0:16, ds(i * 2 + hh, 1)], FX_GATES[hh]
                    c(v.tensor_scalar(fx_q[r0:r0 + 16, hh, :], fx_c[0:16, :], sel, None, ALU.mult))
                    v.tensor_scalar(fx_k[r0 + 32:r0 + 48, hh, :], fx_nc[0:16, :], sel, None, ALU.mult).then_inc(S("fx_sel"), 1)

                def output(ch):
                    qs, qn = CH[ch]
                    dve.wait_ge(S("fx_ot"), i * 5 + (ch + 1))
                    v.tensor_tensor(A[:, i, qs:qs + qn], PS[:, 3, 0:qn], fx_sg[:, qs:qs + qn], ALU.mult).then_inc(S("fx_out"), 1)

                def highest(n):
                    qs, qn = CH[STEPS[n][0]]
                    base = 512 * (4 + 2 * (n % 2))
                    dve.wait_ge(S("fx_s"), i * NS + (n + 1))
                    v.tensor_reduce(fx_nm[0:qn, n % 2:n % 2 + 1], PSF[0:qn, base:base + qs + qn], AXX, ALU.max,
                                    negate=True).then_inc(S("fx_mx"), 1)

                highest(0)
                highest(1)
                for n, (ch, hh) in enumerate(STEPS):
                    qn = CH[ch][1]
                    dve.wait_ge(S("fx_tr"), i * NS + (n + 1))
                    c(v.reciprocal(fx_rs[0:qn, n % 4:n % 4 + 1], fx_sum[0:qn, n % 2:n % 2 + 1]))
                    last = v.tensor_copy(fx_ptb[0:META, n % 2, 0, 0:qn], PS[0:META, 1, 0:qn])
                    if ch > 0:
                        last = v.tensor_copy(fx_ptb[:, n % 2, 1:ch + 1, :], PS[:, 0, 0:P * ch].rearrange("p (a b) -> p a b", a=ch))
                    last.then_inc(S("fx_pt"), 1)
                    if n + 2 < NS:
                        highest(n + 2)
                    if hh == 0 and ch > 1:
                        output(ch - 2)
                output(len(CH) - 2)
                output(len(CH) - 1)
            c.end(KD)

        NC4 = T2 // P
        sd_xp, sd_y, sd_xs, sd_sz = scratch(0, 2, 516), scratch(1040, 2, T2), scratch(2064, T2), scratch(2576, T2)
        sd_xt, sd_cb = scratch(3088, NC4, P), scratch(3600, 2, NC4, T2)
        sd_r, sd_rm = scratch(7696, NC4, T2), scratch(9744, NC4, T2)
        sd_e, sd_w = scratch(11792, 2, NC4, T2), scratch(15888, NC4, T2)
        sd_bc = scratch(11792, 4, T2)
        sd_ec = sd_e.rearrange("p a b c -> p (a b c)").rearrange("p (a c) -> p a c", a=8)
        sd_rms = scratch(17936, 2, T2)
        sd_sel, sd_a, sd_tot = scratch(18960, 16), scratch(18976, 1), scratch(18977, 4)
        row_x, row_a, row_e, row_t, row_z = (A[0:48, 16 + q, 0:T2] for q in range(5))
        row_dt = A[0:48, 21, 0:T2]
        MIXC = sb("mixer_columns", [P, 4, 4, 48])
        nr_cols, dt_cols, g_cols, fl_cols = (MIXC[:, q, :, :] for q in range(4))
        ML_NEG_M = sb("mlstm_rows", [48, T2])

        def rng(d, j):
            return (P * j, T2) if d == 0 else (0, P * (j + 1))

        def mix_pre_bank(j):
            return (TILES["ssd_pre"] + j) % 2

        def ssd_pe(pe, unit, buffer_free, gemm, gemm_tokens, h):
            pe.wait_ge(tile_free, BUFS + TILES["ssd_pre"])
            for j, (u, m0, m1) in enumerate([(0, 0, 48), (1, 0, 40), (1, 64, 104), (2, 0, P), (3, 0, P), (4, 0, P), (5, 0, P)]):
                buffer_free("ssd_pre", 0, 0, j, 2)
                s = unit(UNITS["ssd_pre"], 0, 0, u) if j != 2 else s
                ready = (lambda k: when("mixin", "x", k + 1)) if j == 0 else None
                gemm(mix_pre_bank(j), [(s, 0, KD)], h, T2, m0, m1, last=(j != 1), ready=ready).then_inc(tile_full, 1)

            def tile(i, t):
                buffer_free("ssd", i, 4, t, 2)
                s = unit(UNITS["ssd"], i, 4, t)
                gemm((TILES["ssd"] + t) % 2, [(s, 0, KD)], h, T2).then_inc(tile_full, 1)

            tile(0, 0)
            tile(0, 1)
            pe.wait_ge(S("mx_bc"), 4)
            for g in range(2):
                for j in range(NC4):
                    q = 4 * g + j
                    if q >= 2:
                        pe.wait_ge(S("mx_cb"), q - 1)
                    nc.tensor.matmul(PS[:, 4 + q % 2, :], sd_bc[:, g, P * j:P * j + P], sd_bc[:, 2 + g, :], start=True, stop=True).then_inc(S("mx_cbp"), 1)
            for q, (name, bank, rows) in enumerate([("mx_dt", 3, 48), ("mx_r", 2, 48), ("mx_g", 6, 40), ("mx_fl", 7, 40)]):
                pe.wait_ge(S(name), 1)
                src = {"mx_dt": lambda j: row_dt[0:48, P * j:P * j + P], "mx_r": lambda j: sd_r[0:48, j, P * j:P * j + P],
                       "mx_g": lambda j: row_a[0:40, P * j:P * j + P], "mx_fl": lambda j: row_e[0:40, P * j:P * j + P]}[name]
                for j in range(NC4):
                    mm = nc.tensor.transpose(PS[:, bank, 64 * j:64 * j + rows], src(j), ID[0:rows, 0:rows])
                mm.then_inc(S("mx_turned"), 1)
            pe.wait_ge(S("mx_cols"), 4)

            def pair(i, b, fill):
                for hh in range(2):
                    heads = 2 * b + hh
                    pe.wait_ge(S("sd_rm"), i * 4 + (heads + 1))
                    for q in range(8):
                        j, d = divmod(q, 2)
                        a, z = rng(d, j)
                        pe.wait_ge(S("sd_arg"), i * 32 + max(8 * heads + q - 1, 0) + 1)
                        apart(pe)
                        nc.tensor.matmul(PS[:, 2 + q % 2, 0:z - a], ONES[32 * d:32 * d + 16, :], sd_rm[32 * d:32 * d + 16, j, a:z],
                                         start=True, stop=True).then_inc(S("sd_bcast"), 1)
                    fill(hh)
                    if hh == 0:
                        pe.wait_ge(S("sd_xs"), i * 2 + (b + 1))
                        for j in range(NC4):
                            mm = nc.tensor.transpose(PS[:, 5, P * j:P * j + P], sd_xs[:, P * j:P * j + P], ID[:, :])
                        mm.then_inc(S("sd_xt"), 1)
                    pe.wait_ge(S("sd_w"), i * 16 + 4 * (heads + 1))
                    if hh == 0:
                        pe.wait_ge(S("sd_xtc"), i * 2 + (b + 1))
                        pe.wait_ge(S("sd_out"), i * 2 + b + 1)
                    for j in range(NC4):
                        mm = nc.tensor.matmul(PS[64 * hh:64 * hh + 64, 4, :], sd_xt[:, j, 64 * hh:64 * hh + 64], sd_w[:, j, :],
                                              start=(j == 0), stop=(j == NC4 - 1))
                    mm.then_inc(S("sd_y"), 1)

            with pe.Fori(0, 3) as i:
                for b in range(2):
                    pair(i, b, lambda hh: tile(i, 2 * b + 2 + hh))
            pair(3, 0, lambda hh: tile(3, 2 + hh))
            pair(3, 1, lambda hh: mlstm_tile(pe, unit, buffer_free, gemm, gemm_tokens, h, 0, hh))
            for g in range(2):
                for k in range(4):
                    pe.wait_ge(S("sd_sq"), 4 * g + k + 1)
                    mm = nc.tensor.matmul(PS[:, 6 + g, :], MEANW[:, 1, :], sd_ec[:, 4 * g + k, :], start=(k == 0), stop=(k == 3))
                mm.then_inc(S("sd_ms"), 1)
            pe.wait_ge(S("sd_std"), 2)

        def ssd_act(act, c, full):
            a = nc.scalar
            full("ssd_pre", 0, 0, 0)
            a.activation(row_x, PS[0:48, mix_pre_bank(0), :], ACT.Identity, bias=col("dt_bias", 0, 48)).then_inc(tile_free, 1)
            c(a.activation(sd_a[0:48, :], col("a_log", 0, 48), ACT.Exp))
            act.wait_ge(S("mx_dtabs"), 1)
            a.activation(row_e, row_a, ACT.Exp, scale=-1.0).then_inc(S("mx_dtexp"), 1)
            act.wait_ge(S("mx_dt"), 1)
            full("ssd_pre", 0, 0, 1)
            a.activation(row_t[0:40, :], PS[0:40, mix_pre_bank(1), :], ACT.Identity, bias=col("ig_bias", 0, 40)).then_inc(tile_free, 1)
            full("ssd_pre", 0, 0, 2)
            a.activation(row_x[0:40, :], PS[0:40, mix_pre_bank(2), :], ACT.Identity, bias=col("fg_bias", 0, 40)).then_inc(tile_free, 1)
            act.wait_ge(S("mx_lfabs"), 1)
            c(a.activation(row_e[0:40, :], row_a[0:40, :], ACT.Exp, scale=-1.0))
            a.activation(row_a[0:40, :], row_e[0:40, :], ACT.Ln, bias=SMALL[0:40, 182:183]).then_inc(S("mx_lfln"), 1)
            act.wait_ge(S("mx_fm"), 1)
            a.activation(row_e[0:40, :], row_z[0:40, :], ACT.Exp, scale=-1.0).then_inc(S("mx_fl"), 1)
            act.wait_ge(S("mx_pad"), 1)
            for q in range(4):
                full("ssd_pre", 0, 0, 3 + q)
                if q >= 2:
                    act.wait_ge(S("mx_conv"), q - 1)
                conv_first(act, c, q % 2, mix_pre_bank(3 + q), COLS["ab_conv"] + 6 * (8 + q), "mx_tap", BUFS + TILES["ssd_pre"] + 4 + q)
                if q >= 1:
                    act.wait_ge(S("mx_conv"), q)
                    a.activation(sd_bc[:, q - 1, :], sd_y[:, (q - 1) % 2, :], ACT.Silu).then_inc(S("mx_bc"), 1)
            act.wait_ge(S("mx_conv"), 4)
            a.activation(sd_bc[:, 3, :], sd_y[:, 1, :], ACT.Silu).then_inc(S("mx_bc"), 1)
            for q in range(8):
                act.wait_ge(S("mx_cbp"), q + 1)
                a.activation(sd_cb[:, q // 4, q % 4, :], PS[:, 4 + q % 2, :], ACT.Copy).then_inc(S("mx_cb"), 1)
            for q, (dst, bank, rows, scale) in enumerate([(dt_cols, 3, 48, 1.0), (nr_cols, 2, 48, -1.0), (g_cols, 6, 40, 1.0), (fl_cols, 7, 40, 1.0)]):
                act.wait_ge(S("mx_turned"), q + 1)
                a.activation(dst[:, :, 0:rows], PS[:, bank, 0:256].rearrange("p (j c) -> p j c", j=4)[:, :, 0:rows], ACT.Copy,
                             scale=scale).then_inc(S("mx_cols"), 1)
            for g in range(2):
                with act.Fori(0, 2) as i:
                    for b in range(2):
                        pairs = 4 * g + b
                        t = 8 * g + 2 * b
                        full("ssd", i, 4, t)
                        act.wait_ge(S("sd_out"), i * 2 + pairs + 1)
                        conv_first(act, c, 0, (TILES["ssd"] + t) % 2, i * 12 + (COLS["ab_conv"] + 6 * pairs), "sd_tap", i * 4 + (BUFS + TILES["ssd"] + t + 1))
                        full("ssd", i, 4, t + 1)
                        a.activation(sd_sz, PS[:, (TILES["ssd"] + t + 1) % 2, :], ACT.Silu).then_inc(tile_free, 1)
                        for hh in range(2):
                            heads = 2 * pairs + hh
                            for q in range(8):
                                j, d = divmod(q, 2)
                                lo, hi = rng(d, j)
                                act.wait_ge(S("sd_arg"), i * 32 + (8 * heads + q + 1) + 1)
                                a.activation(sd_e[:, d, j, lo:hi], sd_e[:, d, j, lo:hi], ACT.Exp).then_inc(S("sd_exp"), 1)
                            if hh == 0:
                                act.wait_ge(S("sd_conv"), i * 2 + (pairs + 1))
                                a.activation(sd_xs, sd_y[:, 0, :], ACT.Silu).then_inc(S("sd_xs"), 1)
                                act.wait_ge(S("sd_xt"), i * 2 + (pairs + 1))
                                a.activation(sd_xt, PS[:, 5, :].rearrange("p (j c) -> p j c", j=4), ACT.Copy).then_inc(S("sd_xtc"), 1)
            act.wait_ge(S("sd_out"), 8 + 1)
            for k in range(8):
                a.activation(sd_ec[:, k, :], A[:, k, 0:T2], ACT.Square).then_inc(S("sd_sq"), 1)
            for g in range(2):
                act.wait_ge(S("sd_ms"), g + 1)
                a.activation(sd_rms[:, g, :], PS[:, 6 + g, :], ACT.Sqrt, bias=SMALL[:, 181:182]).then_inc(S("sd_std"), 1)

        def conv_first(act, c, b, bank, w0, signal, freed):
            nc.scalar.activation(sd_xp[:, b, 2:2 + T2], PS[:, bank, :], ACT.Copy).then_inc(tile_free, 1)
            act.wait_ge(tile_free, freed)
            w = lambda k: PAR[:, w0 + k:w0 + k + 1] if isinstance(w0, int) else PAR[:, ds(w0 + k, 1)]
            nc.scalar.activation(sd_y[:, b, :], sd_xp[:, b, 0:T2], ACT.Identity, bias=w(5), scale=w(0)).then_inc(S(signal), 1)

        def conv_rest(dve, c, b, w0, signal):
            w = lambda k: PAR[:, w0 + k:w0 + k + 1] if isinstance(w0, int) else PAR[:, ds(w0 + k, 1)]
            for k in range(1, 5):
                ins = nc.vector.scalar_tensor_tensor(out=sd_y[:, b, :], in0=sd_xp[:, b, k:k + T2], scalar=w(k), in1=sd_y[:, b, :],
                                                     op0=ALU.mult, op1=ALU.add)
                if k < 4:
                    c(ins)
            ins.then_inc(S(signal), 1)

        def ssd_dve(dve, c, log1p_of_exp):
            v = nc.vector
            c(v.memset(NORM_MU[:, :], 1.0))
            c(v.memset(sd_r[0:48, :, :], 0.0))
            c(v.memset(sd_xp[:, :, 0:2], 0.0))
            v.memset(sd_xp[:, :, 2 + T2:4 + T2], 0.0).then_inc(S("mx_pad"), 1)
            dve.wait_ge(consts_ready, 1)
            c(v.tensor_tensor(sd_sel[0:48, :], ID[0:48, 0:16], ID[0:48, 32:48], ALU.add))
            dve.wait_ge(tile_free, BUFS + TILES["ssd_pre"] + 1)
            v.scalar_tensor_tensor(out=row_a, in0=row_x, scalar=-1.0, in1=row_x, op0=ALU.mult, op1=ALU.max).then_inc(S("mx_dtabs"), 1)
            dve.wait_ge(S("mx_dtexp"), 1)
            log1p_of_exp(row_a, row_e, row_z, row_t, row_dt)
            v.scalar_tensor_tensor(out=row_dt, in0=row_x, scalar=0.0, in1=row_dt, op0=ALU.max, op1=ALU.add).then_inc(S("mx_dt"), 1)
            dve.wait_ge(S("mx_dt"), 1)
            row_la = sd_w[0:48, 0, :]
            c(v.tensor_scalar(row_la, row_dt, sd_a[0:48, :], -1.0, ALU.mult, ALU.mult))
            one = lambda r0, n: NORM_MU[r0:r0 + 16, 0:n]
            for j in range(NC4):
                lo, hi = P * j, P * j + P
                for r0, rev in ((0, 1), (32, -1)):
                    r = slice(r0, r0 + 16)
                    own, la = sd_r[r, j, lo:hi][:, ::rev], row_la[r, lo:hi][:, ::rev]
                    c(v.tensor_tensor_scan(own, one(r0, P), la, 0.0, ALU.mult, ALU.add))
                    last = hi - 1 if rev == 1 else lo
                    c(v.tensor_copy(sd_tot[r, j:j + 1], sd_r[r, j, last:last + 1]))
                    c(v.tensor_scalar(sd_r[r, j, lo:hi], sd_r[r, j, lo:hi], sd_tot[r, j:j + 1], None, ALU.subtract))
                    a, z = (hi, T2) if rev == 1 else (0, lo)
                    if z > a:
                        c(v.tensor_tensor_scan(sd_r[r, j, a:z][:, ::rev], one(r0, z - a), row_la[r, a:z][:, ::rev], 0.0, ALU.mult, ALU.add))
            v.memset(sd_tot[0:48, 0:1], 0.0).then_inc(S("mx_r"), 1)
            dve.wait_ge(tile_free, BUFS + TILES["ssd_pre"] + 3)
            x, ab, f, ig, m = row_x[0:40, :], row_a[0:40, :], row_e, row_t[0:40, :], row_z[0:40, :]
            v.scalar_tensor_tensor(out=ab, in0=x, scalar=-1.0, in1=x, op0=ALU.mult, op1=ALU.max).then_inc(S("mx_lfabs"), 1)
            dve.wait_ge(S("mx_lfln"), 1)
            c(v.scalar_tensor_tensor(out=x, in0=x, scalar=0.0, in1=ab, op0=ALU.min, op1=ALU.subtract))
            c(v.memset(row_e[0:40, :], 0.0))
            c(v.memset(row_z[0:40, :], 0.0))
            for r0, rev in ((0, 1), (32, -1)):
                r = slice(r0, r0 + 8)
                c(v.tensor_tensor_scan(row_e[r, ::rev], NORM_MU[r, 0:T2], row_x[r, ::rev], 0.0, ALU.mult, ALU.add))
            v.tensor_tensor(ab, ig, row_e[0:40, :], ALU.subtract).then_inc(S("mx_g"), 1)
            dve.wait_ge(S("mx_g"), 1)
            for r0, rev in ((0, 1), (32, -1)):
                r = slice(r0, r0 + 8)
                c(v.tensor_tensor_scan(row_z[r, ::rev], row_a[r, ::rev], row_a[r, ::rev], 0.0, ALU.max, ALU.max))
            c(v.tensor_scalar(ML_NEG_M[0:40, :], m, -1.0, None, ALU.mult))
            v.tensor_tensor(m, m, row_e[0:40, :], ALU.add).then_inc(S("mx_fm"), 1)
            for q in range(4):
                dve.wait_ge(S("mx_tap"), q + 1)
                conv_rest(dve, c, q % 2, COLS["ab_conv"] + 6 * (8 + q), "mx_conv")
            dve.wait_ge(S("mx_cols"), 4)
            for g in range(2):
                with dve.Fori(0, 2) as i:
                    c.loop(i, 2 * (3 + 2 * (3 + 3 + 2 * 4) + 1))
                    for b in range(2):
                        pairs = 4 * g + b
                        for hh in range(2):
                            heads = 2 * pairs + hh
                            for q in range(8):
                                j, d = divmod(q, 2)
                                lo, hi = rng(d, j)
                                dve.wait_ge(S("sd_bcast"), i * 32 + (8 * heads + q + 1) + 1)
                                v.tensor_scalar(sd_e[:, d, j, lo:hi], PS[:, 2 + q % 2, 0:hi - lo], nr_cols[:, j, ds(i * 4 + (heads + 32 * d), 1)], 0.0,
                                                ALU.add, ALU.min).then_inc(S("sd_arg"), 1)
                            if hh == 0:
                                dve.wait_ge(S("sd_tap"), i * 2 + (pairs + 1))
                                conv_rest(dve, c, 0, i * 12 + (COLS["ab_conv"] + 6 * pairs), "sd_conv")
                            dve.wait_ge(S("sd_y"), i * 4 + heads + 1)
                            for j in range(NC4):
                                lo, hi = P * j, P * j + P
                                dve.wait_ge(S("sd_mask"), i * 32 + (8 * heads + 2 * j + 2))
                                dt = [dt_cols[:, j, ds(i * 4 + (heads + 32 * d), 1)] for d in range(2)]
                                cb = sd_cb[:, g, j, :]
                                if j < NC4 - 1:
                                    c(v.scalar_tensor_tensor(out=sd_w[:, j, hi:T2], in0=sd_e[:, 0, j, hi:T2], scalar=dt[0], in1=cb[:, hi:T2],
                                                             op0=ALU.mult, op1=ALU.mult))
                                if j > 0:
                                    c(v.scalar_tensor_tensor(out=sd_w[:, j, 0:lo], in0=sd_e[:, 1, j, 0:lo], scalar=dt[1], in1=cb[:, 0:lo],
                                                             op0=ALU.mult, op1=ALU.mult))
                                c(v.tensor_scalar(sd_e[:, 0, j, lo:hi], sd_e[:, 0, j, lo:hi], dt[0], None, ALU.mult))
                                c(v.scalar_tensor_tensor(out=sd_e[:, 0, j, lo:hi], in0=sd_e[:, 1, j, lo:hi], scalar=dt[1], in1=sd_e[:, 0, j, lo:hi],
                                                         op0=ALU.mult, op1=ALU.add))
                                v.tensor_tensor(sd_w[:, j, lo:hi], sd_e[:, 0, j, lo:hi], cb[:, lo:hi], ALU.mult).then_inc(S("sd_w"), 1)
                        dve.wait_ge(S("sd_y"), i * 4 + (2 * pairs + 2) + 1)
                        c(v.scalar_tensor_tensor(out=sd_xs, in0=sd_xs, scalar=col("d_skip", i * 2 + pairs), in1=PS[:, 4, :], op0=ALU.mult, op1=ALU.add))
                        v.tensor_tensor(A[:, i * 2 + pairs, 0:T2], sd_xs, sd_sz, ALU.mult).then_inc(S("sd_out"), 1)
                c.end(2)

        def ssd_norm(dve, c):
            v = nc.vector
            for g in range(2):
                dve.wait_ge(S("sd_std"), g + 1)
                c(v.reciprocal(sd_rms[:, g, :], sd_rms[:, g, :]))
                for k in range(4 * g, 4 * g + 4):
                    v.scalar_tensor_tensor(out=A[:, k, 0:T2], in0=A[:, k, 0:T2], scalar=col("ssd_norm", k), in1=sd_rms[:, g, :],
                                           op0=ALU.mult, op1=ALU.mult).then_inc(S("sd_norm"), 1)

        def ssd_pool(pool, c):
            g_ = nc.gpsimd
            flat = lambda ap: ap.rearrange("p a b -> p (a b)")
            pool.wait_ge(S("mx_cols"), 4)
            for g in range(2):
                with pool.Fori(0, 2) as i:
                    for b in range(2):
                        for hh in range(2):
                            heads = 8 * g + 2 * b + hh
                            pool.wait_ge(S("sd_bcast"), i * 32 + 8 * heads + 1)
                            g_.tensor_tensor(flat(sd_rm[0:48, :, :]), flat(sd_r[0:48, :, :]), sd_sel[0:48, ds(i * 4 + heads, 1)].to_broadcast([48, NC4 * T2]), ALU.mult).then_inc(S("sd_rm"), 1)
                            for q in range(8):
                                j, d = divmod(q, 2)
                                pool.wait_ge(S("sd_exp"), i * 32 + (8 * heads + q + 1))
                                own = sd_e[:, d, j, P * j:P * j + P]
                                g_.tensor_tensor(own, own, (LOWER, UPPER)[d][:, :], ALU.mult).then_inc(S("sd_mask"), 1)

        ml_q, ml_k = scratch(0, T2), scratch(512, T2)
        ml_v, ml_o = scratch(1024, NC4, 130), scratch(1544, NC4, P)
        ml_m, ml_d, ml_h = scratch(2056, T2), scratch(2568, 2, NC4, T2), scratch(6664, NC4, P)
        ml_nd, ml_ad, ml_ss, ml_sq = scratch(7176, 2), scratch(7178, 2), scratch(7180, 4), scratch(7184, P)

        def mlstm_tile(pe, unit, buffer_free, gemm, gemm_tokens, h, i, j):
            buffer_free("mlstm", i, 4, j, 2)
            s = unit(UNITS["mlstm"], i, 4, j)
            bank = (TILES["mlstm"] + j) % 2
            if j % 4 < 2:
                gemm(bank, [(s, 0, KD)], h, T2).then_inc(tile_full, 1)
            else:
                gemm_tokens(bank, s, h, [(0, P * q, P * q, P) for q in range(NC4)]).then_inc(tile_full, 1)

        def mlstm_pe(pe, unit, buffer_free, gemm, gemm_tokens, h):
            tile = lambda i, j: mlstm_tile(pe, unit, buffer_free, gemm, gemm_tokens, h, i, j)

            def head(i, more):
                pe.wait_ge(S("ml_rm"), i + 1)
                pe.wait_ge(S("ml_out"), i + 1)
                apart(pe)
                for d in range(2):
                    mm = nc.tensor.matmul(PS[:, 2 + d, :], ONES[32 * d:32 * d + 8, :], ml_m[32 * d:32 * d + 8, :], start=True, stop=True)
                mm.then_inc(S("ml_bcast"), 1)
                tile(i, 2)
                pe.wait_ge(tile_free, i * 4 + (BUFS + TILES["mlstm"] + 2))

                def scores(j):
                    if j >= 2:
                        pe.wait_ge(S("ml_w"), i * 8 + 2 * (j - 1))
                    nc.tensor.matmul(PS[:, 4 + j % 2, :], ml_k[:, P * j:P * j + P], ml_q, start=True, stop=True).then_inc(S("ml_s"), 1)

                scores(0)
                scores(1)
                tile(i, 3)
                scores(2)
                scores(3)
                if more:
                    tile(i, 4)
                pe.wait_ge(S("ml_w"), i * 8 + 8)
                pe.wait_ge(tile_free, i * 4 + (BUFS + TILES["mlstm"] + 4))
                for t in range(NC4):
                    if t >= 2:
                        pe.wait_ge(S("ml_h"), i * 4 + (t - 1))
                    for d in range(2):
                        js = range(0, t + 1) if d == 0 else range(t, NC4)
                        for j in js:
                            mm = nc.tensor.matmul(PS[:, 6 + t % 2, 256 * d:256 * d + 129], ml_d[:, d, j, P * t:P * t + P], ml_v[:, j, 0:129],
                                                  start=(j == js[0]), stop=(j == js[-1]))
                    mm.then_inc(S("ml_num"), 1)
                if more:
                    tile(i, 5)
                pe.wait_ge(S("ml_hn"), i + 1)
                for t in range(NC4):
                    mm = nc.tensor.transpose(PS[:, 2, P * t:P * t + P], ml_h[:, t, :], ID[:, :])
                mm.then_inc(S("ml_ot"), 1)

            with pe.Fori(0, 7) as i:
                head(i, True)
            head(7, False)
            pe.wait_ge(S("ml_out"), 8 + 1)
            pe.wait_ge(S("sd_norm"), 8)

        def mlstm_act(act, c, full):
            a = nc.scalar
            act.wait_ge(S("ml_ones"), 1)
            with act.Fori(0, 8) as i:
                bank = lambda j: (TILES["mlstm"] + j) % 2
                full("mlstm", i, 4, 0)
                a.activation(ml_q, PS[:, bank(0), :], ACT.Copy).then_inc(tile_free, 1)
                full("mlstm", i, 4, 1)
                a.activation(ml_k, PS[:, bank(1), :], ACT.Copy, scale=float(P) ** -0.5).then_inc(tile_free, 1)
                for q in range(8):
                    j, d = divmod(q, 2)
                    lo, hi = rng(d, j)
                    act.wait_ge(S("ml_arg"), i * 8 + (q + 1))
                    a.activation(ml_d[:, d, j, lo:hi], ml_d[:, d, j, lo:hi], ACT.Exp).then_inc(S("ml_exp"), 1)
                full("mlstm", i, 4, 2)
                a.activation(ml_v[:, :, 0:P], PS[:, bank(2), :].rearrange("p (j c) -> p j c", j=4), ACT.Copy).then_inc(tile_free, 1)
                full("mlstm", i, 4, 3)
                a.activation(ml_o, PS[:, bank(3), :].rearrange("p (j c) -> p j c", j=4), ACT.Sigmoid).then_inc(tile_free, 1)
                for t in range(NC4):
                    act.wait_ge(S("ml_h"), i * 4 + (t + 1))
                    a.activation(ml_sq, ml_h[:, t, :], ACT.Square, accum_out=ml_ss[:, t:t + 1]).then_inc(S("ml_sum"), 1)
                    act.wait_ge(S("ml_sum"), i * 4 + (t + 1))
                a.activation(ml_ss, ml_ss, ACT.Sqrt, bias=SMALL[:, 181:182], scale=1.0 / P).then_inc(S("ml_std"), 1)
                act.wait_ge(S("ml_ot"), i + 1)
                a.activation(A[:, i + 8, 0:T2], PS[:, 2, :], ACT.Copy, scale=col("mlstm_norm", i)).then_inc(S("ml_out"), 1)

        def mlstm_dve(dve, c):
            v = nc.vector
            v.memset(ml_v[:, :, P:P + 1], 1.0).then_inc(S("ml_ones"), 1)

            def head(i, first):
                for q in range(8):
                    j, d = divmod(q, 2)
                    lo, hi = rng(d, j)
                    if q == 0:
                        dve.wait_ge(S("ml_bcast"), i + 1 + 1)
                    v.tensor_scalar(ml_d[:, d, j, lo:hi], PS[:, 2 + d, lo:hi], g_cols[:, j, ds(i + 32 * d, 1)], 0.0,
                                    ALU.add, ALU.min).then_inc(S("ml_arg"), 1)
                if first:
                    ssd_norm(dve, c)
                for q in range(8):
                    j, d = divmod(q, 2)
                    lo, hi = rng(d, j)
                    dve.wait_ge(S("ml_mask"), i * 8 + (q + 1))
                    dve.wait_ge(S("ml_s"), i * 4 + (j + 1))
                    v.tensor_tensor(ml_d[:, d, j, lo:hi], ml_d[:, d, j, lo:hi], PS[:, 4 + j % 2, lo:hi], ALU.mult).then_inc(S("ml_w"), 1)
                for t in range(NC4):
                    bank = 6 + t % 2
                    dve.wait_ge(S("ml_num"), i * 4 + (t + 1))
                    den = [PS[:, bank, 256 * d + P:256 * d + P + 1] for d in range(2)]
                    c(v.tensor_scalar(ml_nd, PS[:, bank, P:P + 257:256], -1.0, None, ALU.mult))
                    for d in range(2):
                        c(v.scalar_tensor_tensor(out=ml_ad[:, d:d + 1], in0=ml_nd[:, d:d + 1], scalar=fl_cols[:, t, ds(i + 32 * d, 1)],
                                                 in1=den[d], op0=ALU.max, op1=ALU.max))
                    c(v.reciprocal(ml_ad, ml_ad))
                    c(v.tensor_scalar(ml_h[:, t, :], PS[:, bank, 0:P], ml_ad[:, 0:1], None, ALU.mult))
                    c(v.scalar_tensor_tensor(out=ml_h[:, t, :], in0=PS[:, bank, 256:256 + P], scalar=ml_ad[:, 1:2], in1=ml_h[:, t, :],
                                             op0=ALU.mult, op1=ALU.add))
                    v.tensor_tensor(ml_h[:, t, :], ml_h[:, t, :], ml_o[:, t, :], ALU.mult).then_inc(S("ml_h"), 1)
                dve.wait_ge(S("ml_std"), i + 1)
                c(v.reciprocal(ml_ss, ml_ss))
                for t in range(NC4):
                    ins = v.tensor_scalar(ml_h[:, t, :], ml_h[:, t, :], ml_ss[:, t:t + 1], None, ALU.mult)
                    if t < NC4 - 1:
                        c(ins)
                ins.then_inc(S("ml_hn"), 1)

            head(0, True)
            with dve.Fori(1, 8) as i:
                c.loop(i, 4 * (1 + 2 + 1 + 2) + 1 + 3, begin=1)
                head(i, False)
            c.end(7)

        def mlstm_pool(pool, c):
            pool.wait_ge(S("sd_out"), 8 + 1)
            with pool.Fori(0, 8) as i:
                pool.wait_ge(S("ml_bcast"), i + 1)
                nc.gpsimd.tensor_tensor(ml_m[0:40, :], ML_NEG_M[0:40, :], sd_sel[0:40, ds(i, 1)].to_broadcast([40, T2]), ALU.mult).then_inc(S("ml_rm"), 1)
                for q in range(8):
                    j, d = divmod(q, 2)
                    pool.wait_ge(S("ml_exp"), i * 8 + (q + 1))
                    own = ml_d[:, d, j, P * j:P * j + P]
                    nc.gpsimd.tensor_tensor(own, own, (LOWER, UPPER)[d][:, :], ALU.mult).then_inc(S("ml_mask"), 1)

        GC = 64
        NG = T2 // GC
        GLA_HEADS = 4
        gl_q, gl_k, gl_v, gl_sr = scratch(0, T2), scratch(512, T2), scratch(1024, NC4, 256), scratch(2048, 2, T2)
        gl_x, gl_ab, gl_bc = scratch(3072, 2, T2), scratch(4096, 2, T2), scratch(5120, 2, T2)
        gl_qi, gl_ki, gl_ke = scratch(6144, 2, T2), scratch(7168, 2, T2), scratch(8192, 2, T2)
        gl_kt, gl_dec, gl_st = scratch(9216, 2, NC4, P), scratch(10240, 2, NG), scratch(10256, 2, NG, 256)
        gl_att, gl_o, gl_sq, gl_rn = scratch(14352, 2, NC4, GC), scratch(14864, 2, T2), scratch(15888, 2, T2), scratch(16912, T2)
        gl_reset, gl_lr, gl_ws = scratch(17424, 2, T2), scratch(18448, T2), scratch(19472, P)
        gl_w2 = sb("gate_w2_sb", [48, T2])
        gl_mask = scratch(19600, 2, GC)
        GSTEPS = [[(0, q, q + 1) for q in range(NG - 1)], [(1, q, q - 1) for q in range(NG - 1, 0, -1)]]
        GSTEPS = [s for pair in zip(*GSTEPS) for s in pair]
        NST = len(GSTEPS)

        def gl_rows(ch):
            return slice(GC * (ch % 2), GC * (ch % 2) + GC)

        def gla_pe(pe, unit, buffer_free, gemm, gemm_tokens, h):
            pe.wait_ge(tile_free, BUFS + TILES["gla_pre"])
            s = unit(UNITS["gla_pre"], 0, 0, 0)
            gemm(TILES["gla_pre"] % 2, [(s, 0, KD)], h, T2, 0, 48, ready=lambda k: when("glain", "x", k + 1)).then_inc(tile_full, 1)

            def tile(t):
                buffer_free("gla", 0, 0, t, 2)
                s = unit(UNITS["gla"], 0, 0, t)
                bank = (TILES["gla"] + t) % 2
                if t % 6 in (2, 3):
                    gemm_tokens(bank, s, h, [(0, P * q, P * q, P) for q in range(NC4)]).then_inc(tile_full, 1)
                else:
                    gemm(bank, [(s, 0, KD)], h, T2).then_inc(tile_full, 1)

            tile(0)
            tile(1)
            for n in range(GLA_HEADS):
                pe.wait_ge(S("gl_out"), 2 * n + 1)
                pe.wait_ge(S("gl_ws"), n + 1)
                apart(pe)
                for d in range(2):
                    mm = nc.tensor.matmul(PS[:, 2 + d, :], gl_ws[32 * d:32 * d + 16, :], gl_lr[32 * d:32 * d + 16, :], start=True, stop=True)
                mm.then_inc(S("gl_lg"), 1)
                for j in range(2, 6):
                    tile(6 * n + j)
                pe.wait_ge(S("gl_in"), 2 * n + 2)
                for d in range(2):
                    for j in range(NC4):
                        mm = nc.tensor.transpose(PS[:, 4 + d, P * j:P * j + P], gl_ke[:, d, P * j:P * j + P], ID[:, :])
                    mm.then_inc(S("gl_kp"), 1)
                for d in range(2):
                    for ch in range(NG):
                        mm = nc.tensor.matmul(PS[gl_rows(ch), 6 + d, GC * (ch // 2):GC * (ch // 2) + GC], gl_ki[:, d, GC * ch:GC * ch + GC],
                                              gl_qi[:, d, GC * ch:GC * ch + GC], start=True, stop=True)
                    mm.then_inc(S("gl_att"), 1)
                pe.wait_ge(S("gl_kt"), 2 * n + 2)
                pe.wait_ge(tile_free, BUFS + TILES["gla"] + 6 * n + 6)
                for q, (d, ch, to) in enumerate(GSTEPS):
                    if q >= 2:
                        pe.wait_ge(S("gl_st"), NST * n + q - 1)
                    nc.tensor.matmul(PS[:, 2 + q % 2, 0:256], gl_kt[gl_rows(ch), d, ch // 2, :], gl_v[gl_rows(ch), ch // 2, :],
                                     start=True, stop=True).then_inc(S("gl_u"), 1)
                if n + 1 < GLA_HEADS:
                    tile(6 * n + 6)
                pe.wait_ge(S("gl_am"), 2 * n + 2)
                pe.wait_ge(S("gl_st"), NST * (n + 1))
                for a in range(2):
                    for par in range(2):
                        for ch in range(par, NG, 2):
                            dst = PS[:, (4, 7)[par] + a * (1, -1)[par], GC * (ch // 2):GC * (ch // 2) + GC]
                            ds_ = [d for d in range(2) if (ch > 0 if d == 0 else ch < NG - 1)]
                            for d in range(2):
                                nc.tensor.matmul(dst, gl_v[gl_rows(ch), ch // 2, P * a:P * a + P], gl_att[gl_rows(ch), d, ch // 2, :],
                                                 start=(d == 0), stop=False)
                            for d in ds_:
                                mm = nc.tensor.matmul(dst, gl_st[:, d, ch, P * a:P * a + P], gl_qi[:, d, GC * ch:GC * ch + GC],
                                                      start=False, stop=(d == ds_[-1]))
                    mm.then_inc(S("gl_o"), 1)
                for a in range(2):
                    pe.wait_ge(S("gl_sq"), 2 * n + a + 1)
                    mm = nc.tensor.matmul(PS[:, 2, :], MEANW[:, 2, :], gl_sq[:, a, :], start=(a == 0), stop=(a == 1))
                mm.then_inc(S("gl_ms"), 1)
                if n + 1 < GLA_HEADS:
                    tile(6 * n + 7)
            pe.wait_ge(S("gl_out"), 8 + 1)

        def gla_act(act, c, full):
            a_ = nc.scalar
            full("gla_pre", 0, 0, 0)
            act.wait_ge(S("gl_zero"), 1)
            a_.activation(gl_lr[0:48, :], PS[0:48, TILES["gla_pre"] % 2, :], ACT.Copy).then_inc(tile_free, 1)
            with act.Fori(0, 2) as i:
                c.loop(i, 4)
                for b in range(2):
                    bank = lambda j: (TILES["gla"] + j) % 2
                    act.wait_ge(S("gl_out"), i * 4 + 2 * b + 1)
                    full("gla", i, 12, 6 * b)
                    a_.activation(gl_q, PS[:, bank(0), :], ACT.Copy, scale=float(P) ** -0.5).then_inc(tile_free, 1)
                    full("gla", i, 12, 6 * b + 1)
                    a_.activation(gl_k, PS[:, bank(1), :], ACT.Copy).then_inc(tile_free, 1)
                    act.wait_ge(S("gl_lg"), i * 2 + (b + 1))
                    for d in range(2):
                        a_.activation(gl_x[:, d, :], PS[:, 2 + d, :], ACT.Identity, bias=col("gate_b", i * 2 + (b + 4 * d))).then_inc(S("gl_lx"), 1)
                    for d in range(2):
                        act.wait_ge(S("gl_abs"), i * 4 + (2 * b + d + 1))
                        c(a_.activation(gl_ab[:, d, :], gl_ab[:, d, :], ACT.Exp, scale=-1.0))
                        a_.activation(gl_ab[:, d, :], gl_ab[:, d, :], ACT.Ln, bias=SMALL[:, 182:183]).then_inc(S("gl_ln"), 1)
                    for a in range(2):
                        full("gla", i, 12, 6 * b + 2 + a)
                        a_.activation(gl_v[:, :, P * a:P * a + P], PS[:, bank(2 + a), :].rearrange("p (j c) -> p j c", j=4), ACT.Copy).then_inc(tile_free, 1)
                    for d in range(2):
                        act.wait_ge(S("gl_cum"), i * 4 + (2 * b + d + 1))
                        a_.activation(gl_qi[:, d, :], gl_bc[:, d, :], ACT.Exp, scale=1.0 / 16)
                        a_.activation(gl_ki[:, d, :], gl_bc[:, d, :], ACT.Exp, scale=-1.0 / 16).then_inc(S("gl_exp"), 1)
                    for a in range(2):
                        full("gla", i, 12, 6 * b + 4 + a)
                        a_.activation(gl_sr[:, a, :], PS[:, bank(4 + a), :], ACT.Silu).then_inc(tile_free, 1)
                    for d in range(2):
                        act.wait_ge(S("gl_kp"), i * 4 + (2 * b + d + 1))
                        a_.activation(gl_kt[:, d, :, :], PS[:, 4 + d, :].rearrange("p (j c) -> p j c", j=4), ACT.Copy).then_inc(S("gl_kt"), 1)
                    for a in range(2):
                        act.wait_ge(S("gl_o"), i * 4 + (2 * b + a + 1))
                        for par in range(2):
                            o = a_.activation(gl_o[:, a, :].rearrange("p (j r c) -> p r j c", j=4, r=2)[:, par],
                                              PS[:, (4, 7)[par] + a * (1, -1)[par], 0:256].rearrange("p (j c) -> p j c", j=4), ACT.Copy)
                        o.then_inc(S("gl_oc"), 1)
                        act.wait_ge(S("gl_oc"), i * 4 + (2 * b + a + 1))
                        a_.activation(gl_sq[:, a, :], gl_o[:, a, :], ACT.Square).then_inc(S("gl_sq"), 1)
                    act.wait_ge(S("gl_ms"), i * 2 + (b + 1))
                    a_.activation(gl_rn, PS[:, 2, :], ACT.Sqrt, bias=SMALL[:, 181:182]).then_inc(S("gl_std"), 1)
            c.end(2)

        def gla_dve(dve, c):
            v = nc.vector
            c(v.memset(gl_reset[:, :, :], 1.0))
            for d, at in ((0, 0), (1, GC - 1)):
                c(v.memset(gl_reset[:, d, :].rearrange("p (a b) -> p a b", b=GC)[:, :, at:at + 1], 0.0))
            for d, keep in ((0, LOWER), (1, UPPER)):
                for par in range(2):
                    r = slice(GC * par, GC * par + GC)
                    c(v.tensor_copy(gl_mask[r, d, :], keep[r, r]))
            v.memset(gl_rn, 0.0).then_inc(S("gl_zero"), 1)
            dve.wait_ge(w2_loaded, 16)
            with dve.Fori(0, 2) as i:
                c.loop(i, 2 * (2 * 1 + 2 * 3 + 1 + 2))
                for b in range(2):
                    v.tensor_copy(gl_ws[0:48, :], gl_w2[0:48, ds(i * 256 + P * b, P)]).then_inc(S("gl_ws"), 1)
                    for d in range(2):
                        dve.wait_ge(S("gl_lx"), i * 4 + (2 * b + d + 1))
                        v.scalar_tensor_tensor(out=gl_ab[:, d, :], in0=gl_x[:, d, :], scalar=-1.0, in1=gl_x[:, d, :], op0=ALU.mult,
                                               op1=ALU.max).then_inc(S("gl_abs"), 1)
                    for d in range(2):
                        dve.wait_ge(S("gl_ln"), i * 4 + (2 * b + d + 1))
                        c(v.scalar_tensor_tensor(out=gl_x[:, d, :], in0=gl_x[:, d, :], scalar=0.0, in1=gl_ab[:, d, :], op0=ALU.min, op1=ALU.subtract))
                        rev = (1, -1)[d]
                        v.tensor_tensor_scan(gl_bc[:, d, ::rev], gl_reset[:, d, ::rev], gl_x[:, d, ::rev], 0.0, ALU.mult, ALU.add).then_inc(S("gl_cum"), 1)
                    for d in range(2):
                        dve.wait_ge(S("gl_exp"), i * 4 + (2 * b + d + 1))
                        end = (GC - 1, 0)[d]
                        chunks = lambda ap: ap.rearrange("p (a b) -> p a b", b=GC)
                        c(v.tensor_copy(gl_dec[:, d, :], chunks(gl_qi[:, d, :])[:, :, end]))
                        c(v.tensor_tensor(gl_qi[:, d, :], gl_qi[:, d, :], gl_q, ALU.mult))
                        c(v.tensor_tensor(gl_ki[:, d, :], gl_ki[:, d, :], gl_k, ALU.mult))
                        v.tensor_tensor(chunks(gl_ke[:, d, :]), chunks(gl_ki[:, d, :]), gl_dec[:, d, :].rearrange("p (a b) -> p a b", b=1).to_broadcast([P, NG, GC]),
                                        ALU.mult).then_inc(S("gl_in"), 1)
                    for d in range(2):
                        dve.wait_ge(S("gl_att"), i * 4 + (2 * b + d + 1))
                        v.tensor_tensor(gl_att[:, d, :, :], PS[:, 6 + d, 0:256].rearrange("p (a b) -> p a b", b=GC),
                                        gl_mask[:, d, :].rearrange("p (a b) -> p a b", a=1).to_broadcast([P, NC4, GC]), ALU.mult).then_inc(S("gl_am"), 1)
                    for q, (d, ch, to) in enumerate(GSTEPS):
                        dve.wait_ge(S("gl_u"), i * (2 * NST) + (NST * b + q + 1))
                        u = PS[:, 2 + q % 2, 0:256]
                        if q < 2:
                            ins = v.tensor_copy(gl_st[:, d, to, :], u)
                        else:
                            dve.wait_ge(S("gl_st"), i * (2 * NST) + (NST * b + q - 1))
                            ins = v.scalar_tensor_tensor(out=gl_st[:, d, to, :], in0=gl_st[:, d, ch, :], scalar=gl_dec[:, d, ch:ch + 1], in1=u,
                                                         op0=ALU.mult, op1=ALU.add)
                        ins.then_inc(S("gl_st"), 1)
                    dve.wait_ge(S("gl_std"), i * 2 + (b + 1))
                    c(v.reciprocal(gl_rn, gl_rn))
                    for a in range(2):
                        k = i * 4 + (2 * b + a)
                        c(v.scalar_tensor_tensor(out=gl_o[:, a, :], in0=gl_o[:, a, :], scalar=col("gla_norm", k), in1=gl_rn, op0=ALU.mult, op1=ALU.mult))
                        v.tensor_tensor(A[:, k, 0:T2], gl_o[:, a, :], gl_sr[:, a, :], ALU.mult).then_inc(S("gl_out"), 1)
            c.end(2)

        @block.sync
        def _(sp):
            sp.dma_start(W[:, 0, :, :], units[0]).then_inc(w_full[0], 16)
            for q in range(4):
                sp.dma_start(X[:, 2 * q:2 * q + 2, :], x_t[:, 2 * q:2 * q + 2, :]).then_inc(x_loaded[q], 16)
            sp.dma_start(PAR[:, :], cols).then_inc(loaded, 16)
            last = {"lru": "ffn0", "ffn0": "fox_f", "fox": "ffn1", "ffn1": "ssd_pre", "mix": "ffn2", "ffn2": "gla_pre", "gla": "ffn3"}
            if phases[-1] == "lru":
                n_units = UNITS["ffn0"]
            else:
                n_units = UNITS[last[phases[-1]]] if phases[-1] in last else N_UNITS
            full, rest = divmod(n_units, SLOTS)
            for b in range(1, SLOTS):
                sp.dma_start(W[:, b, :, :], units[b]).then_inc(w_full[b], 16)
            sp.dma_start(gl_w2[:, :], gate_w2).then_inc(w2_loaded, 16)
            with sp.Fori(1, full) as i:
                for b in range(SLOTS):
                    sp.wait_ge(w_started, i * SLOTS + (b + 2 - SLOTS))
                    sp.dma_start(W[:, b, :, :], units[i * SLOTS + b]).then_inc(w_full[b], 16)
            for b in range(rest):
                sp.wait_ge(w_started, (full - 1) * SLOTS + b + 2)
                sp.dma_start(W[:, b, :, :], units[full * SLOTS + b]).then_inc(w_full[b], 16)
            sp.wait_ge(*when(phases[-1], "x", KD))
            sp.dma_start(out, X[:, :, META:T1]).then_inc(out_done, 16)
            sp.wait_ge(out_done, 16)

        @block.tensor
        def _(pe):
            def unit(base, i, per, j):
                u = base + j
                slot = u % SLOTS
                if isinstance(i, int):
                    pe.wait_ge(w_full[slot], 16 * ((u + i * per) // SLOTS + 1))
                else:
                    pe.wait_ge(w_full[slot], i * (16 * (per // SLOTS)) + 16 * (u // SLOTS + 1))
                return slot

            def buffer_free(name, i, per, j, bufs):
                pe.wait_ge(tile_free, i * per + (TILES[name] + j + 1 + BUFS - bufs))

            def gemm(bank, slots, rhs, T, m0=0, m1=P, last=True, ready=None):
                for slot, first, count in slots:
                    s = slot if isinstance(slot, int) else slot()
                    for b, t, n in parts(T):
                        for q in range(count):
                            k = first + q
                            if ready and b == 0:
                                pe.wait_ge(*ready(k))
                            mm = nc.tensor.matmul(PS[0:m1 - m0, bank + b, 0:n], W[:, s, q, m0:m1], rhs(k)[:, t:t + n],
                                                  start=(k == 0), stop=(k == slots[-1][1] + slots[-1][2] - 1))
                            if last and q == 0 and (b, t, n) == parts(T)[-1]:
                                mm.then_inc(w_started, 1)
                return mm

            def gemm_tokens(bank, slot, h, chunks):
                for b, c, t, rows in chunks:
                    for k in range(KD):
                        mm = nc.tensor.matmul(PS[0:rows, bank + b, c:c + P], h(k)[:, t:t + rows], W[:, slot, k, :],
                                              start=(k == 0), stop=(k == KD - 1))
                        if k == 0 and (b, c, t, rows) == chunks[-1]:
                            mm.then_inc(w_started, 1)
                return mm

            def x1(k):
                return X[:, k, :]

            def h2(k):
                return Z[:, k, 0:T2]

            def bank4(n):
                return 2 * (n % 4)

            def projection(name, K, T, per, trips):
                us = [(k, min(KD, K - k)) for k in range(0, K, KD)]
                pe.wait_ge(tile_free, BUFS + TILES[name])
                with pe.Fori(0, trips) as i:
                    for j in range(per):
                        buffer_free(name, i, per, j, min(per, BUFS))
                        slots = [(lambda q=q: unit(UNITS[name], i, per * len(us), j * len(us) + q), k, n) for q, (k, n) in enumerate(us)]
                        mm = gemm(bank4(TILES[name] + j), slots, lambda k: A[:, k, 0:T], T)
                        mm.then_inc(tile_full, 1)

            def norm(name, T, centred, summed=False):
                if centred:
                    pe.wait_ge(tile_free, BUFS + {"lru": TILES["ffn0"], "ffn0": TILES["fox_f"], "fox": TILES["ffn1"], "ffn1": TILES["ssd_pre"]}[name])
                    pe.wait_ge(*when(name, "zsum", KD - 1))
                    for b, t, n in parts(T):
                        mm = nc.tensor.matmul(PS[:, b, 0:n], MEANW[:, 0, :], NORM_MU[:, t:t + n], start=True, stop=True)
                    mm.then_inc(shared("mean", name), 1)
                if summed:
                    pe.wait_ge(tile_free, BUFS + {"mix": TILES["ffn2"], "ffn2": TILES["gla_pre"], "gla": TILES["ffn3"], "ffn3": TILES["end"]}[name])
                    pe.wait_ge(*when(name, "sqsum", KD - 1))
                    nc.tensor.matmul(PS[:, 2, 0:T], MEANW[:, 0, :], NORM_MU[:, 0:T], start=True, stop=True).then_inc(shared("var", name), 1)
                    return
                for k in range(KD):
                    pe.wait_ge(*when(name, "sq", k + 1))
                    for b, t, n in parts(T):
                        mm = nc.tensor.matmul(PS[:, 2 + b, 0:n], MEANW[:, 0, :], A[:, k, t:t + n], start=(k == 0), stop=(k == KD - 1))
                mm.then_inc(shared("var", name), 1)

            def ffn(n, T, h, before):
                name = f"ffn{n}"
                normed = lambda k: when(before, "x", k + 1)
                pe.wait_ge(tile_free, BUFS + TILES[name])
                with pe.Fori(0, NF // 2) as i:
                    for j in range(4):
                        buffer_free(name, i, 4, j, 4)
                        s = unit(UNITS[name], i, 4, j)
                        gemm(bank4(TILES[name] + j), [(s, 0, KD)], h, T, ready=normed if j == 0 else None).then_inc(tile_full, 1)
                pe.wait_ge(*when(name, "act", NF))
                with pe.Fori(0, 2) as i:
                    for j in range(4):
                        pe.wait_ge(tile_free, i * 4 + (TILES[name] + 2 * NF + j + 1))
                        slots = [(lambda q=q: unit(UNITS[name] + 2 * NF, i, 12, 3 * j + q), KD * q, min(KD, NF - KD * q)) for q in range(3)]
                        gemm(bank4(TILES[name] + 2 * NF + j), slots, lambda k: A[:, k, 0:T], T).then_inc(tile_full, 1)

            credit(pe, "sd_bcast", "sd_y", "ml_bcast")
            pe.wait_ge(consts_ready, 1)

            rc = scratch(1600, 3, T1)
            with pe.Fori(0, 4) as i:
                def lru_tile(j, slot, fn):
                    buffer_free("lru", i, 12, j, 4)
                    fn(bank4(j)).then_inc(tile_full, 1)
                def dense_tile(j, u):
                    s = unit(0, i, 8, u)
                    here = (lambda k: (x_loaded[k // 2], 16)) if j == 0 else None
                    lru_tile(j, s, lambda bank: gemm(bank, [(s, 0, KD)], x1, T1, ready=here))
                for j in range(3):
                    dense_tile(j, j)
                dense_tile(3, 3)
                pe.wait_ge(S("lru_conv"), i * 3 + 3)
                for g in range(2):
                    s = unit(0, i, 8, 4 + g)
                    for o in range(3):
                        pieces = [(q, k) for q, (oo, k) in enumerate(LRU_PIECES) if oo == o]

                        def blocks(bank):
                            for b, t, n in parts(T1):
                                for x, (q, k) in enumerate(pieces):
                                    mm = nc.tensor.matmul(PS[:, bank + b, 0:n], W[:, s, q, :], rc[:, k, t:t + n],
                                                          start=(x == 0), stop=(x == len(pieces) - 1))
                                    if o == 2 and b == 1 and x == 0:
                                        mm.then_inc(w_started, 1)
                            return mm
                        lru_tile(4 + 3 * g + o, s, blocks)
                for j in (1, 2):
                    dense_tile(9 + j, 5 + j)
            pe.wait_ge(S("lru_act"), 12 + 1)
            projection("lru_out", 12, T1, 2, 4)
            norm("lru", T1, True)
            if "ffn0" in phases:
                ffn(0, T1, x1, "lru")
                norm("ffn0", T1, True)
            if "fox" in phases:
                fox_pe(pe, unit, buffer_free, gemm, gemm_tokens, x1)
                projection("fox_out", 8, T1, 4, 2)
                norm("fox", T1, True)
            if "ffn1" in phases:
                ffn(1, T1, x1, "fox")
                norm("ffn1", T1, True)
            if "mix" in phases:
                norm("mixin", T2, False)
                ssd_pe(pe, unit, buffer_free, gemm, gemm_tokens, h2)
                mlstm_pe(pe, unit, buffer_free, gemm, gemm_tokens, h2)
                projection("mix_out", 16, T2, 2, 4)
                norm("mix", T2, False, summed=True)
            if "ffn2" in phases:
                norm("ffn2in", T2, False)
                ffn(2, T2, h2, "ffn2in")
                norm("ffn2", T2, False, summed=True)
            if "gla" in phases:
                norm("glain", T2, False)
                gla_pe(pe, unit, buffer_free, gemm, gemm_tokens, h2)
                projection("gla_out", 8, T2, 4, 2)
                norm("gla", T2, False, summed=True)
            if "ffn3" in phases:
                norm("ffn3in", T2, False)
                ffn(3, T2, h2, "ffn3in")
                norm("ffn3", T2, False, summed=True)

        @block.scalar
        def _(act):
            c = Chain(act, s_act)
            credit(act, "ml_out")
            act.sem_inc(tile_free, BUFS)

            def full(name, i, per, j):
                act.wait_ge(tile_full, i * per + (TILES[name] + j + 1))

            def leave(name, m, bank, T, into):
                if T == T2:
                    norm_of = {"mix_out": "mix", "gla_out": "gla"}.get(name, name)
                    nc.scalar.activation(scratch(SQ_AT, KD, T2)[:, m, :], ps_tile(bank, T), ACT.Square).then_inc(shared("sq", norm_of), 1)
                nc.scalar.activation(sv(into(m), T), ps_tile(bank, T), ACT.Copy).then_inc(tile_free, 1)

            def project(name, T, per, trips, into):
                with act.Fori(0, trips) as i:
                    for j in range(per):
                        full(name, i, per, j)
                        leave(name, i * per + j, 2 * ((TILES[name] + j) % 4), T, into)

            def z_of(T):
                return lambda m: Z[:, m, 0:T]

            def norm(name, T, src, centred, ready, ready_n, eps):
                if centred:
                    act.wait_ge(*when(name, "mean", 1))
                    nc.scalar.activation(sv(NORM_MU[:, 0:T], T), ps_tile(0, T), ACT.Copy).then_inc(shared("mu", name), 1)
                spare = 96 + NORMS.index(name)
                nc.scalar.activation(SMALL[:, spare:spare + 1], SMALL[:, eps:eps + 1], ACT.Sqrt)
                for k in range(KD if ready else 0):
                    act.wait_ge(ready, ready_n(k))
                    nc.scalar.activation(A[:, k, 0:T], src(k), ACT.Square).then_inc(shared("sq", name), 1)
                act.wait_ge(*when(name, "var", 1))
                nc.scalar.activation(sv(NORM_R[:, 0:T], T), ps_tile(2, T), ACT.Sqrt, bias=SMALL[:, eps:eps + 1]).then_inc(shared("std", name), 1)
                if centred:
                    for k in range(KD):
                        act.wait_ge(*when(name, "sc", k + 1))
                        nc.scalar.activation(X[:, k, :], Z[:, k, :], ACT.Identity, bias=bias_col(name, k)).then_inc(shared("x", name), 1)

            def bias_col(name, k):
                return {"lru": col("ln1_b", k), "ffn0": col("ln2_b", k), "fox": col("ln1_b", 8 + k), "ffn1": col("ln2_b", 8 + k)}[name]

            def ffn(n, T, into):
                name = f"ffn{n}"
                off = 2 if T == T1 else 1
                xp, y, g = scratch(0, 4, 532), scratch(2128, 4, T1), scratch(4240, 2, T1)
                par = COLS[name]
                act.wait_ge(*when(name, "pad", 1))
                with act.Fori(0, NF // 2) as i:
                    for j in range(4):
                        full(name, i, 4, j)
                        act.wait_ge(*when(name, "conv", i * 4))
                        act.wait_ge(*when(name, "act", i * 2))
                        nc.scalar.activation(sv(xp[:, j, off:off + T], T), ps_tile(2 * ((TILES[name] + j) % 4), T), ACT.Copy).then_inc(tile_free, 1)
                        act.wait_ge(tile_free, i * 4 + (BUFS + TILES[name] + j + 1))
                        w0 = 16 * i + (par + 8 * (j // 2) + 4 * (j % 2))
                        nc.scalar.activation(y[:, j, 0:T], xp[:, j, 0:T], ACT.Identity, bias=PAR[:, ds(w0 + 3, 1)],
                                             scale=PAR[:, ds(w0, 1)]).then_inc(shared("tap", name), 1)
                    for j in range(2):
                        act.wait_ge(*when(name, "conv", i * 4 + (2 * j + 1)))
                        nc.scalar.activation(g[:, j, 0:T], y[:, 2 * j, 0:T], ACT.Gelu_apprx_tanh).then_inc(shared("gelu", name), 1)
                with act.Fori(0, 2) as i:
                    for j in range(4):
                        act.wait_ge(tile_full, i * 4 + (TILES[name] + 2 * NF + j + 1))
                        leave(name, i * 4 + j, 2 * ((TILES[name] + j) % 4), T, into)

            act.wait_ge(setup_lam, 1)
            nc.scalar.activation(SMALL[:, 12:24], SMALL[:, 0:12], ACT.Exp, scale=-1.0).then_inc(setup_lam_act, 1)

            xp, rc, r, ig, aa, th, mm, gg = [scratch(at, 3, n) for at, n in
                                             [(0, 532)] + [(1600 + 3 * T1 * q, T1) for q in range(7)]]
            act.wait_ge(lam_ready, 1)
            act.wait_ge(S("lru_pad"), 1)
            with act.Fori(0, 4) as i:
                c.loop(i, 3)
                act.wait_ge(S("lru_act"), i * 3 + 1)
                for j in range(3):
                    full("lru", i, 12, j)
                    nc.scalar.activation(sv(xp[:, j, 3:3 + T1], T1), ps_tile(2 * j, T1), ACT.Copy).then_inc(tile_free, 1)
                    act.wait_ge(tile_free, i * 12 + (BUFS + j + 1))
                    w0 = 15 * i + (COLS["a_conv"] + 5 * j)
                    nc.scalar.activation(rc[:, j, :], xp[:, j, 0:T1], ACT.Identity, bias=PAR[:, ds(w0 + 4, 1)],
                                         scale=PAR[:, ds(w0, 1)]).then_inc(S("lru_tap"), 1)
                def gate(j, t):
                    full("lru", i, 12, t)
                    nc.scalar.activation(sv(gg[:, j, :], T1), ps_tile(2 * (t % 4), T1), ACT.Gelu_apprx_tanh).then_inc(tile_free, 1)
                gate(0, 3)
                for g, dst, b in ((0, r, "a_br"), (1, ig, "a_bi")):
                    for j in range(3):
                        full("lru", i, 12, 4 + 3 * g + j)
                        nc.scalar.activation(sv(dst[:, j, :], T1), ps_tile(2 * ((4 + 3 * g + j) % 4), T1), ACT.Sigmoid,
                                             bias=col(b, i * 3 + j)).then_inc(tile_free, 1)
                act.wait_ge(tile_free, i * 12 + (BUFS + 10))
                for j in range(3):
                    c(nc.scalar.activation(aa[:, j, :], r[:, j, :], ACT.Exp, scale=SMALL[:, ds(i * 3 + (72 + j), 1)]))
                    nc.scalar.activation(th[:, j, :], r[:, j, :], ACT.Tanh, scale=SMALL[:, ds(i * 3 + (60 + j), 1)]).then_inc(S("lru_at"), 1)
                for j in range(3):
                    act.wait_ge(S("lru_m"), i * 3 + (j + 1))
                    nc.scalar.activation(mm[:, j, :], mm[:, j, :], ACT.Sqrt).then_inc(S("lru_sqrt"), 1)
                for j in (1, 2):
                    gate(j, 9 + j)
            c.end(4)
            project("lru_out", T1, 2, 4, z_of(T1))
            z_src = lambda k: Z[:, k, :]
            norm("lru", T1, z_src, True, *at_k("lru", "ctr"), 180)
            if "ffn0" in phases:
                ffn(0, T1, z_of(T1))
                norm("ffn0", T1, z_src, True, *at_k("ffn0", "ctr"), 180)
            if "fox" in phases:
                fox_act(act, c, full)
                project("fox_out", T1, 4, 2, z_of(T1))
                norm("fox", T1, z_src, True, *at_k("fox", "ctr"), 180)
            if "ffn1" in phases:
                ffn(1, T1, z_of(T1))
                norm("ffn1", T1, z_src, True, *at_k("ffn1", "ctr"), 180)
            x2 = lambda k: X[:, k, META:T1]
            if "mix" in phases:
                norm("mixin", T2, x2, False, *at_k("ffn1", "x"), 181)
                ssd_act(act, c, full)
                mlstm_act(act, c, full)
                project("mix_out", T2, 2, 4, z_of(T2))
                norm("mix", T2, None, False, None, None, 181)
            if "ffn2" in phases:
                norm("ffn2in", T2, x2, False, *at_k("mix", "x"), 181)
                ffn(2, T2, z_of(T2))
                norm("ffn2", T2, None, False, None, None, 181)
            if "gla" in phases:
                norm("glain", T2, x2, False, *at_k("ffn2", "x"), 181)
                gla_act(act, c, full)
                project("gla_out", T2, 4, 2, z_of(T2))
                norm("gla", T2, None, False, None, None, 181)
            if "ffn3" in phases:
                norm("ffn3in", T2, x2, False, *at_k("gla", "x"), 181)
                ffn(3, T2, z_of(T2))
                norm("ffn3", T2, None, False, None, None, 181)

        @block.vector
        def _(dve):
            c = Chain(dve, s_dve)
            v = nc.vector
            credit(dve, "lru_act", "fx_out", "sd_arg", "sd_out", "gl_out", "ffn_conv", "ffn_act")

            def log1p_of_exp(x, e, z, t, poly):
                c(v.tensor_scalar(t, e, 2.0, None, ALU.add))
                c(v.reciprocal(t, t))
                c(v.tensor_tensor(z, e, t, ALU.mult))
                c(v.tensor_tensor(t, z, z, ALU.mult))
                c(v.tensor_scalar(poly, t, 1.0 / 15, None, ALU.mult))
                for k in (13, 11, 9, 7, 5, 3):
                    c(v.scalar_tensor_tensor(out=poly, in0=poly, scalar=1.0 / k, in1=t, op0=ALU.add, op1=ALU.mult))
                c(v.scalar_tensor_tensor(out=poly, in0=poly, scalar=1.0, in1=z, op0=ALU.add, op1=ALU.mult))
                c(v.tensor_scalar(poly, poly, 2.0, None, ALU.mult))

            def residual(name, tiles):
                for k in range(KD):
                    dve.wait_ge(tile_free, BUFS + tiles + k + 1)
                    v.scalar_tensor_tensor(out=Z[:, k, :], in0=X[:, k, :], scalar=ALPHA, in1=Z[:, k, :], op0=ALU.mult,
                                           op1=ALU.add).then_inc(shared("z", name), 1)

            def ln(name, g, k0):
                dve.wait_ge(*when(name, "mu", 1))
                for k in range(KD):
                    dve.wait_ge(*when(name, "z", k + 1))
                    v.tensor_tensor(Z[:, k, :], Z[:, k, :], NORM_MU[:, :], ALU.subtract).then_inc(shared("ctr", name), 1)
                dve.wait_ge(*when(name, "std", 1))
                c(v.reciprocal(NORM_R[:, :], NORM_R[:, :]))
                for k in range(KD):
                    dve.wait_ge(*when(name, "ctr", k + 1))
                    v.scalar_tensor_tensor(out=Z[:, k, :], in0=Z[:, k, :], scalar=col(g, k0 + k), in1=NORM_R[:, :],
                                           op0=ALU.mult, op1=ALU.mult).then_inc(shared("sc", name), 1)

            def rms_in(name, g):
                dve.wait_ge(*when(name, "std", 1))
                c(v.reciprocal(NORM_R[:, 0:T2], NORM_R[:, 0:T2]))
                for k in range(KD):
                    v.scalar_tensor_tensor(out=Z[:, k, 0:T2], in0=X[:, k, META:T1], scalar=col("norm_g", g * 8 + k),
                                           in1=NORM_R[:, 0:T2], op0=ALU.mult, op1=ALU.mult).then_inc(shared("x", name), 1)

            def rms_out(name, g):
                dve.wait_ge(*when(name, "std", 1))
                c(v.reciprocal(NORM_R[:, 0:T2], NORM_R[:, 0:T2]))
                for k in range(KD):
                    c(v.scalar_tensor_tensor(out=Z[:, k, 0:T2], in0=Z[:, k, 0:T2], scalar=col("norm_g", g * 8 + k),
                                             in1=NORM_R[:, 0:T2], op0=ALU.mult, op1=ALU.mult))
                    v.tensor_tensor(X[:, k, META:T1], X[:, k, META:T1], Z[:, k, 0:T2], ALU.add).then_inc(shared("x", name), 1)
                dve.wait_ge(*when(name, "x", KD))

            def ffn(n, T):
                name = f"ffn{n}"
                off = 2 if T == T1 else 1
                xp, y, g = scratch(0, 4, 532), scratch(2128, 4, T1), scratch(4240, 2, T1)
                par = COLS[name]
                c(v.memset(xp[:, :, 0:2], 0.0))
                v.memset(xp[:, :, T + off:T + 2] if T == T2 else xp[:, :, 0:2], 0.0).then_inc(shared("pad", name), 1)
                with dve.Fori(0, NF // 2) as i:
                    c.loop(i, 4)
                    for j in range(4):
                        dve.wait_ge(*when(name, "tap", i * 4 + (j + 1)))
                        w0 = 16 * i + (par + 8 * (j // 2) + 4 * (j % 2))
                        c(v.scalar_tensor_tensor(out=y[:, j, 0:T], in0=xp[:, j, 1:1 + T], scalar=PAR[:, ds(w0 + 1, 1)],
                                                 in1=y[:, j, 0:T], op0=ALU.mult, op1=ALU.add))
                        v.scalar_tensor_tensor(out=y[:, j, 0:T], in0=xp[:, j, 2:2 + T], scalar=PAR[:, ds(w0 + 2, 1)],
                                               in1=y[:, j, 0:T], op0=ALU.mult, op1=ALU.add).then_inc(shared("conv", name), 1)
                    for j in range(2):
                        dve.wait_ge(*when(name, "gelu", i * 2 + (j + 1)))
                        dve.wait_ge(*when(name, "conv", i * 4 + (2 * j + 2)))
                        v.tensor_tensor(A[:, i * 2 + j, 0:T], g[:, j, 0:T], y[:, 2 * j + 1, 0:T], ALU.mult).then_inc(shared("act", name), 1)
                c.end(NF // 2)

            dve.wait_ge(loaded, 16)
            lam, e, z, t, poly = [SMALL[:, 12 * q:12 * q + 12] for q in range(5)]
            v.scalar_tensor_tensor(out=lam, in0=PAR[:, COLS["a_lam"]:COLS["a_lam"] + 12], scalar=-1.0,
                                   in1=PAR[:, COLS["a_lam"]:COLS["a_lam"] + 12], op0=ALU.mult, op1=ALU.max).then_inc(setup_lam, 1)
            c(v.memset(SMALL[:, 180:181], 1e-5))
            c(v.memset(SMALL[:, 181:182], 1e-6))
            c(v.memset(SMALL[:, 182:183], 1.0))
            dve.wait_ge(setup_lam_act, 1)
            log1p_of_exp(lam, e, z, t, poly)
            c(v.tensor_scalar(t, PAR[:, COLS["a_lam"]:COLS["a_lam"] + 12], -1.0, 0.0, ALU.mult, ALU.max))
            c(v.tensor_tensor(poly, poly, t, ALU.add))
            c(v.tensor_scalar(SMALL[:, 60:72], poly, 8.0, None, ALU.mult))
            v.tensor_scalar(SMALL[:, 72:84], poly, -8.0, None, ALU.mult).then_inc(lam_ready, 1)

            xp, rc, r, ig, aa, th, mm, gg = [scratch(at, 3, n) for at, n in
                                             [(0, 532)] + [(1600 + 3 * T1 * q, T1) for q in range(7)]]
            v.memset(xp[:, :, 0:3], 0.0).then_inc(S("lru_pad"), 1)
            with dve.Fori(0, 4) as i:
                c.loop(i, 3 * (2 + 1 + 3))
                for j in range(3):
                    dve.wait_ge(S("lru_tap"), i * 3 + (j + 1))
                    w0 = 15 * i + (COLS["a_conv"] + 5 * j)
                    for k in (1, 2):
                        c(v.scalar_tensor_tensor(out=rc[:, j, :], in0=xp[:, j, k:k + T1], scalar=PAR[:, ds(w0 + k, 1)],
                                                 in1=rc[:, j, :], op0=ALU.mult, op1=ALU.add))
                    v.scalar_tensor_tensor(out=rc[:, j, :], in0=xp[:, j, 3:3 + T1], scalar=PAR[:, ds(w0 + 3, 1)],
                                           in1=rc[:, j, :], op0=ALU.mult, op1=ALU.add).then_inc(S("lru_conv"), 1)
                for j in range(3):
                    dve.wait_ge(S("lru_at"), i * 3 + (j + 1))
                    c(v.tensor_tensor(mm[:, j, :], aa[:, j, :], aa[:, j, :], ALU.mult))
                    v.scalar_tensor_tensor(out=mm[:, j, :], in0=mm[:, j, :], scalar=1.0, in1=th[:, j, :], op0=ALU.add,
                                           op1=ALU.mult).then_inc(S("lru_m"), 1)
                for j in range(3):
                    dve.wait_ge(S("lru_sqrt"), i * 3 + (j + 1))
                    c(v.tensor_tensor(ig[:, j, :], ig[:, j, :], rc[:, j, :], ALU.mult))
                    c(v.tensor_tensor(ig[:, j, :], ig[:, j, :], mm[:, j, :], ALU.mult))
                    c(v.tensor_tensor_scan(r[:, j, :], aa[:, j, :], ig[:, j, :], 0.0, ALU.mult, ALU.add))
                for j in range(3):
                    dve.wait_ge(tile_free, i * 12 + (BUFS + 10 + j))
                    v.tensor_tensor(A[:, i * 3 + j, :], gg[:, j, :], r[:, j, :], ALU.mult).then_inc(S("lru_act"), 1)
            c.end(4)
            residual("lru", TILES["lru_out"])
            ln("lru", "ln1_g", 0)
            if "ffn0" in phases:
                ffn(0, T1)
                dve.wait_ge(*when("lru", "x", KD))
                residual("ffn0", TILES["ffn0"] + 2 * NF)
                ln("ffn0", "ln2_g", 0)
            if "fox" in phases:
                fox_dve(dve, c)
                dve.wait_ge(*when("ffn0", "x", KD))
                residual("fox", TILES["fox_out"])
                ln("fox", "ln1_g", 8)
            if "ffn1" in phases:
                ffn(1, T1)
                dve.wait_ge(*when("fox", "x", KD))
                residual("ffn1", TILES["ffn1"] + 2 * NF)
                ln("ffn1", "ln2_g", 8)
            if "mix" in phases:
                dve.wait_ge(*when("ffn1", "x", KD))
                rms_in("mixin", 0)
                ssd_dve(dve, c, log1p_of_exp)
                mlstm_dve(dve, c)
                rms_out("mix", 1)
            if "ffn2" in phases:
                rms_in("ffn2in", 2)
                ffn(2, T2)
                rms_out("ffn2", 3)
            if "gla" in phases:
                rms_in("glain", 4)
                gla_dve(dve, c)
                rms_out("gla", 5)
            if "ffn3" in phases:
                rms_in("ffn3in", 6)
                ffn(3, T2)
                rms_out("ffn3", 7)

        @block.gpsimd
        def _(pool):
            c = Chain(pool, s_pool)
            g = nc.gpsimd
            c(g.memset(ONES[:, :], 1.0))
            for q, n in enumerate((D, 512, 256)):
                c(g.memset(MEANW[:, q, :], 1.0 / n))
            c(g.affine_select(out=ID[:, :], in_=ONES[:, :], compare_op=ALU.is_equal, fill=0.0, base=0, pattern=[[-1, P]], channel_multiplier=1))
            c(g.memset(CAUSAL_ADD[:, :], 0.0))
            c(g.affine_select(out=CAUSAL_ADD[:, :], in_=CAUSAL_ADD[:, :], compare_op=ALU.is_ge, fill=-BIG, base=0, pattern=[[-1, P]], channel_multiplier=1))
            c(g.affine_select(out=LOWER[:, :], in_=ONES[:, :], compare_op=ALU.is_ge, fill=0.0, base=0, pattern=[[1, P]], channel_multiplier=-1))
            c(g.affine_select(out=UPPER[:, :], in_=ONES[:, :], compare_op=ALU.is_ge, fill=0.0, base=0, pattern=[[-1, P]], channel_multiplier=1))
            g.memset(NORM_MU[:, :], 0.0).then_inc(consts_ready, 1)

            def sums(name, what, src):
                pool.wait_ge(*when(name, what, 1))
                for k in range(1, KD):
                    pool.wait_ge(*when(name, what, k + 1))
                    if k > 1:
                        pool.wait_ge(*when(name, what + "sum", k - 1))
                    T = src(0).shape[-1]
                    g.tensor_tensor(NORM_MU[:, 0:T], src(0) if k == 1 else NORM_MU[:, 0:T], src(k), ALU.add).then_inc(shared(what + "sum", name), 1)

            z = lambda k: Z[:, k, :]
            sq = lambda k: scratch(SQ_AT, KD, T2)[:, k, :]
            for name in ("lru", "ffn0", "fox", "ffn1"):
                if name in phases:
                    sums(name, "z", z)
            if "mix" in phases:
                ssd_pool(pool, c)
                mlstm_pool(pool, c)
            for name in ("mix", "ffn2", "gla", "ffn3"):
                if name in phases:
                    sums(name, "sq", sq)


def _unit_cols(w, c0, n=P):
    k = w.shape[0] // P
    return w[:, c0:c0 + n].reshape(k, P, n).transpose(1, 0, 2)


def _layout(inputs):
    f = {k: np.asarray(v) for k, v in inputs.items()}
    units = np.zeros((N_UNITS, P, KD, P), np.float32)
    at = [0]

    def put(w, c0, n=P, into=0):
        t = _unit_cols(w, c0, n)
        for k in range(0, t.shape[1], KD):
            q = min(KD, t.shape[1] - k)
            units[at[0], :, 0:q, into:into + n] = t[:, k:k + q]
            at[0] += 1

    def at_phase(name):
        assert at[0] == UNITS[name], (name, at[0], UNITS[name])

    def put_ffn(name, w_in, w_out):
        at_phase(name)
        for t in range(NF):
            put(w_in, t * P)
            put(w_in, DFF + t * P)
        for m in range(KD):
            put(w_out, m * P)

    a_in = f["a_w_in"][0]
    for g in range(4):
        for j in range(3):
            put(a_in, RNN + (3 * g + j) * P)
        put(a_in, 3 * g * P)
        for w in (f["a_w_r"][0], f["a_w_i"][0]):
            dense = np.zeros((3 * P, 3 * P), np.float32)
            for b in range(4):
                dense[b * LRU:(b + 1) * LRU, b * LRU:(b + 1) * LRU] = w[4 * g + b]
            for q, (o, k) in enumerate(LRU_PIECES):
                units[at[0], :, q, :] = dense[k * P:(k + 1) * P, o * P:(o + 1) * P]
            at[0] += 1
        for j in (1, 2):
            put(a_in, (3 * g + j) * P)
    at_phase("lru_out")
    for m in range(KD):
        put(f["a_w_out"][0], m * P)
    put_ffn("ffn0", f["f_w_in"][0], f["f_w_out"][0])
    kv, bw = f["kv_w"], f["b_w_in"][0]
    put(kv, 2 * D, 16)
    at_phase("fox")
    for h in range(KD):
        put(bw, h * P)
        put(kv, h * P)
        put(kv, D + h * P)
        put(bw, D + h * P)
    at_phase("fox_out")
    for m in range(KD):
        put(f["b_w_out"][0], m * P)
    put_ffn("ffn1", f["f_w_in"][1], f["f_w_out"][1])
    ab = f["ab_w_in_2"][0]
    z0, xbc0, dt0, q0 = 0, D, D + 1536, D + 1536 + 32
    gates0 = q0 + 4 * D
    at_phase("ssd_pre")
    put(ab, dt0, 16)
    at[0] -= 1
    put(ab, dt0 + 16, 16, 32)
    for d in range(2):
        put(ab, gates0 + 8 * d, 8, 32 * d)
        at[0] -= 1
        put(ab, gates0 + 16 + 8 * d, 8, 64 + 32 * d)
        if d == 0:
            at[0] -= 1
    for b in range(4):
        put(ab, xbc0 + D + b * P)
    at_phase("ssd")
    for h in range(KD):
        put(ab, xbc0 + h * P)
        put(ab, z0 + h * P)
    at_phase("mlstm")
    for h in range(KD):
        for s in range(4):
            put(ab, q0 + s * D + h * P)
    at_phase("mix_out")
    for m in range(KD):
        put(f["ab_w_out_2"][0], m * P)
    put_ffn("ffn2", f["ffn_w_up_2"][0], f["ffn_w_down_2"][0])
    cw = f["c_w_in_2"][0]
    put(cw, 3072, 16)
    at[0] -= 1
    put(cw, 3072 + 16, 16, 32)
    at_phase("gla")
    for h in range(4):
        put(cw, h * P)
        put(cw, 512 + h * P)
        for s in range(2):
            for a in range(2):
                put(cw, D + s * D + (2 * h + a) * P)
    at_phase("gla_out")
    for m in range(KD):
        put(f["c_w_out_2"][0], m * P)
    put_ffn("ffn3", f["ffn_w_up_2"][1], f["ffn_w_down_2"][1])
    assert at[0] == N_UNITS

    cols = np.zeros((P, N_COLS), np.float32)

    def vec(name, v, k=0, step=1):
        v = np.asarray(v).reshape(-1, P)
        for t in range(v.shape[0]):
            cols[:, COLS[name] + k + t * step] = v[t]

    def conv(name, w, b, k, step):
        for q in range(w.shape[0]):
            vec(name, w[q], k + q, step)
        vec(name, b, k + w.shape[0], step)

    conv("a_conv", f["a_conv_w"][0], f["a_conv_b"][0], 0, 5)
    vec("a_br", f["a_b_r"][0])
    vec("a_bi", f["a_b_i"][0])
    vec("a_lam", f["a_lambda"][0])
    cols[0:16, COLS["fox_fb"]] = f["kv_f_b"]
    for name in ("ln1_g", "ln1_b", "ln2_g", "ln2_b"):
        vec(name, f[name])
    vec("norm_g", f["norm_g_2"])
    for n, (w, b) in enumerate(((f["f_conv_w"][0], f["f_conv_b"][0]), (f["f_conv_w"][1], f["f_conv_b"][1]),
                                (f["ffn_conv_w_2"][0], f["ffn_conv_b_2"][0]), (f["ffn_conv_w_2"][1], f["ffn_conv_b_2"][1]))):
        conv(f"ffn{n}", w[:, 0:DFF], b[0:DFF], 0, 8)
        conv(f"ffn{n}", w[:, DFF:], b[DFF:], 4, 8)
    conv("ab_conv", f["ab_conv_w_2"][0], f["ab_conv_b_2"][0], 0, 6)
    for d in range(2):
        cols[32 * d:32 * d + 16, COLS["dt_bias"]] = f["ab_dt_bias_2"][0, d]
        cols[32 * d:32 * d + 16, COLS["a_log"]] = f["ab_a_log_2"][0, d]
        cols[32 * d:32 * d + 8, COLS["ig_bias"]] = f["ab_ig_bias_2"][0, d]
        cols[32 * d:32 * d + 8, COLS["fg_bias"]] = f["ab_fg_bias_2"][0, d]
    vec("d_skip", np.repeat(f["ab_d_skip_2"][0], 64))
    vec("ssd_norm", f["ab_ssd_norm_2"][0])
    vec("mlstm_norm", f["ab_mlstm_norm_2"][0])
    vec("gate_b", f["c_gate_b_2"][0])
    vec("gla_norm", f["c_norm_2"][0])

    gate_w2 = np.zeros((48, 512), np.float32)
    gate_w2[0:16] = f["c_gate_w2_2"][0, 0]
    gate_w2[32:48] = f["c_gate_w2_2"][0, 1]

    x_t = np.concatenate([f["meta"], f["x"][0]], axis=0).reshape(T1, KD, P).transpose(2, 1, 0)
    return {"x_t": np.ascontiguousarray(x_t), "units": units, "cols": cols, "gate_w2": gate_w2}


def kernel(**inputs):
    import concourse.bacc as _bacc
    from concourse.bass_utils import run_bass_kernel_spmd as _run

    nc = _bacc.Bacc("TRN2", target_bir_lowering=False, num_devices=1)
    arrays = _layout(inputs)
    args = [nc.dram_tensor(name, a.shape, F32, kind="ExternalInput").ap() for name, a in arrays.items()]
    out = nc.dram_tensor("out_t", (P, KD, SEQ), F32, kind="ExternalOutput").ap()
    build(nc, *args, out)
    r = _run(nc, [arrays], core_ids=[0])
    got = r.results[0]["out_t"]
    return np.ascontiguousarray(got.transpose(2, 1, 0).reshape(1, SEQ, D))
```
